# Optimizing a Trainium2 kernel written in Bass

```python
import math
import jax, jax.numpy as jnp
from jax import lax
import numpy as np

D_MODEL = 1024
BATCH = 1
SEQ = 128
DEPTH = 2
DEC_BATCH = 1
DEC_SEQ = 512
PAST_LEN = 128

GRID_W = 64
N_SSD = (DEPTH + 1) // 2
N_GDN = DEPTH // 2
CHUNK = 64
CONV_K = 3
EPS = 1e-6
SSD_INNER = 2 * D_MODEL
SSD_HEAD_DIM = 64
SSD_HEADS = SSD_INNER // SSD_HEAD_DIM
SSD_GROUPS = 4
SSD_HPG = SSD_HEADS // SSD_GROUPS
SSD_STATE = 128
SSD_GN = SSD_GROUPS * SSD_STATE
SSD_CONV_DIM = SSD_INNER + 2 * SSD_GN
SSD_PROJ = SSD_INNER + SSD_CONV_DIM + 2 * SSD_HEADS
GDN_HEADS = 8
GDN_DK = 128
GDN_DV = 256
GDN_QK = GDN_HEADS * GDN_DK
GDN_VW = GDN_HEADS * GDN_DV
GDN_CONV_DIM = 2 * GDN_QK + GDN_VW
GDN_PROJ = GDN_CONV_DIM + GDN_VW + 4 * GDN_HEADS
PEER_HEADS = 8
N_KEYS = 128
N_EXPERTS = N_KEYS * N_KEYS
PEER_TOPK = 16
PEER_DKEY = 256
PEER_HALF = PEER_DKEY // 2
PEER_BLOCK = 128

kernel_name = "bidir_ssd_deltanet_peer_diffusion_step"

def rmsnorm(x, g):
    xf = x.astype(jnp.float32)
    xf = xf * lax.rsqrt(jnp.mean(xf * xf, axis=-1, keepdims=True) + EPS)
    return (xf * g.astype(jnp.float32)).astype(x.dtype)

def adaln(x, g, shift, scale):
    return rmsnorm(x, g) * (1 + scale) + shift

def l2norm(x):
    return x * lax.rsqrt(jnp.sum(x * x, axis=-1, keepdims=True) + EPS)

def short_conv(x, w):
    pad = CONV_K // 2
    n = x.shape[1]
    xp = jnp.pad(x, ((0, 0), (pad, pad), (0, 0)))
    return sum(xp[:, t:t + n] * w[t] for t in range(CONV_K))

def grid_pos_embed(n, dtype):
    rows = n // GRID_W
    r = jnp.repeat(jnp.arange(rows, dtype=jnp.float32), GRID_W)
    col = jnp.tile(jnp.arange(GRID_W, dtype=jnp.float32), rows)
    quarter = D_MODEL // 4
    omega = 1.0 / (10000.0 ** (jnp.arange(quarter, dtype=jnp.float32) / quarter))
    def enc(p):
        ang = p[:, None] * omega[None, :]
        return jnp.concatenate([jnp.sin(ang), jnp.cos(ang)], axis=-1)
    return jnp.concatenate([enc(r), enc(col)], axis=-1).astype(dtype)

def ssd_scan(x, dt, a, bm, cm, s0):
    b, n, G, R, P = x.shape
    N = bm.shape[-1]
    nc = n // CHUNK
    x = x.reshape(b, nc, CHUNK, G, R, P)
    dt = dt.reshape(b, nc, CHUNK, G, R)
    bm = bm.reshape(b, nc, CHUNK, G, N)
    cm = cm.reshape(b, nc, CHUNK, G, N)
    acs = jnp.cumsum(dt * a, axis=2)
    xdt = x * dt[..., None]
    idx = jnp.arange(CHUNK)
    tril = (idx[:, None] >= idx[None, :])[:, :, None, None]
    lmat = jnp.exp(jnp.where(tril, acs[:, :, :, None] - acs[:, :, None], -jnp.inf))
    cb = jnp.einsum('bcign,bcjgn->bcijg', cm, bm)
    y_in = jnp.einsum('bcijgr,bcjgrp->bcigrp', cb[..., None] * lmat, xdt)
    xw = xdt * jnp.exp(acs[:, :, -1:] - acs)[..., None]
    e_acs = jnp.exp(acs)
    dec = jnp.exp(acs[:, :, -1])
    def step(s, inp):
        xw_c, b_c, c_c, e_c, d_c = inp
        y_c = jnp.einsum('bign,bgrpn->bigrp', c_c, s) * e_c[..., None]
        s = s * d_c[..., None, None] + jnp.einsum('bjgn,bjgrp->bgrpn', b_c, xw_c)
        return s, y_c
    seqs = tuple(jnp.moveaxis(t, 1, 0) for t in (xw, bm, cm, e_acs, dec))
    s_fin, y_x = lax.scan(step, s0, seqs)
    y = y_in + jnp.moveaxis(y_x, 0, 1)
    return y.reshape(b, n, G, R, P), s_fin

def gdn_scan(q, k, v, beta, g, s0):
    b, n, H, DK = q.shape
    DV = v.shape[-1]
    nc = n // CHUNK
    def to_chunks(t):
        t = t.reshape((b, nc, CHUNK) + t.shape[2:])
        return jnp.moveaxis(t, 2, 3)
    q, k, v, beta, g = (to_chunks(t) for t in (q, k, v, beta, g))
    gc = jnp.cumsum(g, axis=-1)
    idx = jnp.arange(CHUNK)
    incl = idx[:, None] >= idx[None, :]
    strict = idx[:, None] > idx[None, :]
    decay = jnp.exp(jnp.where(incl, gc[..., :, None] - gc[..., None, :], -jnp.inf))
    kb = k * beta[..., None]
    vb = v * beta[..., None]
    m = jnp.where(strict, jnp.einsum('bnhid,bnhjd->bnhij', kb, k) * decay, 0.0)
    eye = jnp.eye(CHUNK, dtype=m.dtype)
    tmat = lax.linalg.triangular_solve(m + eye, jnp.broadcast_to(eye, m.shape), left_side=True, lower=True)
    u = tmat @ vb
    w = tmat @ (kb * jnp.exp(gc)[..., None])
    a_qk = jnp.where(incl, jnp.einsum('bnhid,bnhjd->bnhij', q, k) * decay, 0.0)
    qg = q * jnp.exp(gc)[..., None]
    kg = k * jnp.exp(gc[..., -1:] - gc)[..., None]
    glast = jnp.exp(gc[..., -1])
    def step(s, inp):
        u_c, w_c, a_c, qg_c, kg_c, gl_c = inp
        v_new = u_c - w_c @ s
        o_c = qg_c @ s + a_c @ v_new
        s = s * gl_c[..., None, None] + jnp.swapaxes(kg_c, -1, -2) @ v_new
        return s, o_c
    seqs = tuple(jnp.moveaxis(t, 1, 0) for t in (u, w, a_qk, qg, kg, glast))
    s_fin, o = lax.scan(step, s0, seqs)
    o = jnp.moveaxis(jnp.moveaxis(o, 0, 1), 3, 2).reshape(b, n, H, DV)
    return o, s_fin

def ssd_mixer(h, w_in, conv_w, conv_b, dt_bias, a_log, d_skip, norm_g, w_out, s0_f, s0_b):
    f32 = jnp.float32
    b, n, _ = h.shape
    proj = h @ w_in
    z = proj[..., :SSD_INNER]
    xbc = proj[..., SSD_INNER:SSD_INNER + SSD_CONV_DIM]
    dt_raw = proj[..., SSD_INNER + SSD_CONV_DIM:]
    xbc = jax.nn.silu(short_conv(xbc, conv_w) + conv_b).astype(f32)
    xs = xbc[..., :SSD_INNER].reshape(b, n, SSD_GROUPS, SSD_HPG, SSD_HEAD_DIM)
    bm = xbc[..., SSD_INNER:SSD_INNER + SSD_GN].reshape(b, n, SSD_GROUPS, SSD_STATE)
    cm = xbc[..., SSD_INNER + SSD_GN:].reshape(b, n, SSD_GROUPS, SSD_STATE)
    dt = jax.nn.softplus(dt_raw.astype(f32).reshape(b, n, 2, SSD_GROUPS, SSD_HPG)
                         + dt_bias.astype(f32).reshape(2, SSD_GROUPS, SSD_HPG))
    a = -jnp.exp(a_log.astype(f32)).reshape(2, SSD_GROUPS, SSD_HPG)
    st = (b, SSD_GROUPS, SSD_HPG, SSD_HEAD_DIM, SSD_STATE)
    y_f, s_f = ssd_scan(xs, dt[:, :, 0], a[0], bm, cm, s0_f.astype(f32).reshape(st))
    y_b, s_b = ssd_scan(xs[:, ::-1], dt[:, ::-1, 1], a[1], bm[:, ::-1], cm[:, ::-1], s0_b.astype(f32).reshape(st))
    y = y_f + y_b[:, ::-1] + xs * d_skip.astype(f32).reshape(SSD_GROUPS, SSD_HPG, 1)
    y = rmsnorm(y.reshape(b, n, SSD_INNER) * jax.nn.silu(z.astype(f32)), norm_g)
    out = y.astype(h.dtype) @ w_out
    hs = (b, SSD_HEADS, SSD_HEAD_DIM, SSD_STATE)
    return out, s_f.reshape(hs).astype(h.dtype), s_b.reshape(hs).astype(h.dtype)

def gdn_mixer(h, w_in, conv_w, dt_bias, a_log, norm_g, w_out, s0_f, s0_b):
    f32 = jnp.float32
    b, n, _ = h.shape
    proj = h @ w_in
    qkv = jax.nn.silu(short_conv(proj[..., :GDN_CONV_DIM], conv_w)).astype(f32)
    z = proj[..., GDN_CONV_DIM:GDN_CONV_DIM + GDN_VW].astype(f32).reshape(b, n, GDN_HEADS, GDN_DV)
    ab = proj[..., GDN_CONV_DIM + GDN_VW:].astype(f32).reshape(b, n, 2, 2, GDN_HEADS)
    q = l2norm(qkv[..., :GDN_QK].reshape(b, n, GDN_HEADS, GDN_DK)) * (GDN_DK ** -0.5)
    k = l2norm(qkv[..., GDN_QK:2 * GDN_QK].reshape(b, n, GDN_HEADS, GDN_DK))
    v = qkv[..., 2 * GDN_QK:].reshape(b, n, GDN_HEADS, GDN_DV)
    beta = jax.nn.sigmoid(ab[:, :, 0])
    g = -jnp.exp(a_log.astype(f32)) * jax.nn.softplus(ab[:, :, 1] + dt_bias.astype(f32))
    o_f, s_f = gdn_scan(q, k, v, beta[:, :, 0], g[:, :, 0], s0_f.astype(f32))
    o_b, s_b = gdn_scan(q[:, ::-1], k[:, ::-1], v[:, ::-1], beta[:, ::-1, 1], g[:, ::-1, 1], s0_b.astype(f32))
    o = rmsnorm(o_f + o_b[:, ::-1], norm_g) * jax.nn.silu(z)
    out = o.reshape(b, n, GDN_VW).astype(h.dtype) @ w_out
    return out, s_f.astype(h.dtype), s_b.astype(h.dtype)

def peer(h, w_q, keys, u_tab, v_tab):
    b, n, D = h.shape
    xt = h.reshape(-1, PEER_BLOCK, D)
    def block(xb):
        t = xb.shape[0]
        q = (xb @ w_q).reshape(t, PEER_HEADS, 2, PEER_HALF)
        s = jnp.einsum('thsk,shnk->thsn', q, keys).astype(jnp.float32)
        sv, si = lax.top_k(s, PEER_TOPK)
        comb = (sv[:, :, 0, :, None] + sv[:, :, 1, None, :]).reshape(t, PEER_HEADS, PEER_TOPK * PEER_TOPK)
        cv, ci = lax.top_k(comb, PEER_TOPK)
        i1 = jnp.take_along_axis(si[:, :, 0], ci // PEER_TOPK, axis=-1)
        i2 = jnp.take_along_axis(si[:, :, 1], ci % PEER_TOPK, axis=-1)
        eid = (i1 * N_KEYS + i2).reshape(t, PEER_HEADS * PEER_TOPK)
        gate = jax.nn.softmax(cv, axis=-1).reshape(t, PEER_HEADS * PEER_TOPK)
        u = jnp.take(u_tab, eid, axis=0)
        act = jax.nn.gelu(jnp.einsum('td,ted->te', xb, u).astype(jnp.float32), approximate=False) * gate
        vv = jnp.take(v_tab, eid, axis=0)
        return jnp.einsum('te,ted->td', act.astype(xb.dtype), vv)
    return lax.map(block, xt).reshape(b, n, D)

def setup_inputs(seed: int = 0) -> dict:
    key = jax.random.key(seed)
    ks = jax.random.split(key, 32)
    D = D_MODEL
    def nrm(i, shape, s):
        return jax.random.normal(ks[i], shape, jnp.float32) * s
    def uni(i, shape, lo, hi):
        return jax.random.uniform(ks[i], shape, jnp.float32, lo, hi)
    def dt_bias(i, shape):
        dt = jnp.exp(uni(i, shape, math.log(1e-3), math.log(1e-1)))
        return dt + jnp.log(-jnp.expm1(-dt))
    ssd_st = (DEC_BATCH, N_SSD, SSD_HEADS, SSD_HEAD_DIM, SSD_STATE)
    gdn_st = (DEC_BATCH, N_GDN, GDN_HEADS, GDN_DK, GDN_DV)
    return {
        "x_prompt": nrm(0, (BATCH, SEQ, D), 1.0),
        "x_sample": nrm(1, (DEC_BATCH, DEC_SEQ, D), 1.0),
        "c": nrm(2, (DEC_BATCH, D), 1.0),
        "state_ssd_fwd": nrm(3, ssd_st, 0.02),
        "state_ssd_bwd": nrm(4, ssd_st, 0.02),
        "state_gdn_fwd": nrm(5, gdn_st, 0.1),
        "state_gdn_bwd": nrm(6, gdn_st, 0.1),
        "c_ctx": nrm(7, (D,), 1.0),
        "w_mod": nrm(8, (DEPTH, D, 6 * D), 0.5 * D ** -0.5),
        "b_mod": nrm(9, (DEPTH, 6 * D), 0.02),
        "norm_mix_g": 1.0 + nrm(10, (DEPTH, D), 0.02),
        "norm_ffn_g": 1.0 + nrm(11, (DEPTH, D), 0.02),
        "ssd_w_in": nrm(12, (N_SSD, D, SSD_PROJ), D ** -0.5),
        "ssd_conv_w": nrm(13, (N_SSD, CONV_K, SSD_CONV_DIM), CONV_K ** -0.5),
        "ssd_conv_b": nrm(14, (N_SSD, SSD_CONV_DIM), 0.02),
        "ssd_dt_bias": dt_bias(15, (N_SSD, 2, SSD_HEADS)),
        "ssd_a_log": jnp.log(uni(16, (N_SSD, 2, SSD_HEADS), 1.0, 16.0)),
        "ssd_d": 1.0 + nrm(17, (N_SSD, SSD_HEADS), 0.02),
        "ssd_norm_g": 1.0 + nrm(18, (N_SSD, SSD_INNER), 0.02),
        "ssd_w_out": nrm(19, (N_SSD, SSD_INNER, D), SSD_INNER ** -0.5),
        "gdn_w_in": nrm(20, (N_GDN, D, GDN_PROJ), D ** -0.5),
        "gdn_conv_w": nrm(21, (N_GDN, CONV_K, GDN_CONV_DIM), CONV_K ** -0.5),
        "gdn_dt_bias": dt_bias(22, (N_GDN, 2, GDN_HEADS)),
        "gdn_a_log": jnp.log(uni(23, (N_GDN, 2, GDN_HEADS), 1.0, 16.0)),
        "gdn_norm_g": 1.0 + nrm(24, (N_GDN, GDN_DV), 0.02),
        "gdn_w_out": nrm(25, (N_GDN, GDN_VW, D), GDN_VW ** -0.5),
        "peer_w_q": nrm(26, (DEPTH, D, PEER_HEADS * PEER_DKEY), D ** -0.5),
        "peer_keys": nrm(27, (DEPTH, 2, PEER_HEADS, N_KEYS, PEER_HALF), PEER_HALF ** -0.5),
        "peer_u": nrm(28, (DEPTH, N_EXPERTS, D), D ** -0.5),
        "peer_v": nrm(29, (DEPTH, N_EXPERTS, D), 0.5),
        "final_norm_g": 1.0 + nrm(30, (D,), 0.02),
    }

def reference(x_prompt, x_sample, c, state_ssd_fwd, state_ssd_bwd, state_gdn_fwd, state_gdn_bwd, c_ctx,
              w_mod, b_mod, norm_mix_g, norm_ffn_g,
              ssd_w_in, ssd_conv_w, ssd_conv_b, ssd_dt_bias, ssd_a_log, ssd_d, ssd_norm_g, ssd_w_out,
              gdn_w_in, gdn_conv_w, gdn_dt_bias, gdn_a_log, gdn_norm_g, gdn_w_out,
              peer_w_q, peer_keys, peer_u, peer_v, final_norm_g):
    xp = x_prompt
    xs = x_sample + grid_pos_embed(x_sample.shape[1], x_sample.dtype)[None]
    bp = xp.shape[0]
    ssd_f, ssd_b, gdn_f, gdn_b = [], [], [], []
    for i in range(DEPTH):
        mod_p = jnp.split((jax.nn.silu(c_ctx) @ w_mod[i] + b_mod[i])[None, None, :], 6, axis=-1)
        mod_s = jnp.split((jax.nn.silu(c) @ w_mod[i] + b_mod[i])[:, None, :], 6, axis=-1)
        hp = adaln(xp, norm_mix_g[i], mod_p[0], mod_p[1])
        hs = adaln(xs, norm_mix_g[i], mod_s[0], mod_s[1])
        j = i // 2
        if i % 2 == 0:
            prm = (ssd_w_in[j], ssd_conv_w[j], ssd_conv_b[j], ssd_dt_bias[j], ssd_a_log[j], ssd_d[j], ssd_norm_g[j], ssd_w_out[j])
            z0 = jnp.zeros((bp, SSD_HEADS, SSD_HEAD_DIM, SSD_STATE), xp.dtype)
            mp, sf, sb = ssd_mixer(hp, *prm, z0, z0)
            ms, _, _ = ssd_mixer(hs, *prm, state_ssd_fwd[:, j], state_ssd_bwd[:, j])
            ssd_f.append(sf)
            ssd_b.append(sb)
        else:
            prm = (gdn_w_in[j], gdn_conv_w[j], gdn_dt_bias[j], gdn_a_log[j], gdn_norm_g[j], gdn_w_out[j])
            z0 = jnp.zeros((bp, GDN_HEADS, GDN_DK, GDN_DV), xp.dtype)
            mp, sf, sb = gdn_mixer(hp, *prm, z0, z0)
            ms, _, _ = gdn_mixer(hs, *prm, state_gdn_fwd[:, j], state_gdn_bwd[:, j])
            gdn_f.append(sf)
            gdn_b.append(sb)
        xp = xp + mod_p[2] * mp
        xs = xs + mod_s[2] * ms
        hp = adaln(xp, norm_ffn_g[i], mod_p[3], mod_p[4])
        hs = adaln(xs, norm_ffn_g[i], mod_s[3], mod_s[4])
        xp = xp + mod_p[5] * peer(hp, peer_w_q[i], peer_keys[i], peer_u[i], peer_v[i])
        xs = xs + mod_s[5] * peer(hs, peer_w_q[i], peer_keys[i], peer_u[i], peer_v[i])
    y_prompt = rmsnorm(xp, final_norm_g)
    y_sample = rmsnorm(xs, final_norm_g)
    new_state_ssd_fwd = jnp.stack(ssd_f, axis=1)
    new_state_ssd_bwd = jnp.stack(ssd_b, axis=1)
    new_state_gdn_fwd = jnp.stack(gdn_f, axis=1)
    new_state_gdn_bwd = jnp.stack(gdn_b, axis=1)
    return (y_prompt, y_sample, new_state_ssd_fwd, new_state_ssd_bwd, new_state_gdn_fwd, new_state_gdn_bwd)


_drawn_inputs = setup_inputs


def setup_inputs(seed=0):
    import zlib

    import numpy as np

    out = dict(_drawn_inputs(seed))
    spreads = {}
    factors = {'state_ssd_fwd': 8.0,
     'state_ssd_bwd': 7.258,
     'state_gdn_fwd': 4.361,
     'state_gdn_bwd': 3.677,
     'norm_ffn_g': 3.251,
     'ssd_d': 8.0,
     'ssd_norm_g': 3.955,
     'gdn_norm_g': 70.432,
     'final_norm_g': 2.753}
    for name, (base, spread) in spreads.items():
        noise = np.random.default_rng([zlib.crc32(name.encode()), seed]).standard_normal(out[name].shape)
        drawn = base * np.exp(spread * noise) if base else spread * noise
        out[name] = __import__('jax').numpy.asarray(drawn.astype(out[name].dtype))
    for name, factor in factors.items():
        out[name] = (out[name] * factor).astype(out[name].dtype)
    return out
```

```python
from contextlib import ExitStack

import concourse.bass as bass
import numpy as np
from concourse import mybir

ALU = mybir.AluOpType
ACT = mybir.ActivationFunctionType
AX = mybir.AxisListType
F32 = mybir.dt.float32
U32 = mybir.dt.uint32

P = 128
D = 1024
KT = D // P
CTX, LAT = 128, 512
T = CTX + LAT
NC = T // P
SEG = ((0, LAT), (LAT, T))
CTXC = NC - 1
DEPTH = 2
EPS = 1e-6
NEG = -1.0e30
SLOT = 1024
NSLOT = 4

SG, SR, SP_, SN = 4, 8, 64, 128
SH = SG * SR
SXT = SR * SP_ // P
SCONV = SXT + 2
STILES = SCONV + SXT
SINNER = SH * SP_
GH, GDK, GDV = 8, 128, 256
GVT = GDV // P
GCONV = 2 + GVT
GTILES = GCONV + GVT
LEVELS = 7
PH, NK, TOPK, PHALF = 8, 128, 16, 128
NE = NK * NK
EB = 4
NB = NK // EB

CONSTS = ("ident", "ones", "tri_f", "tri_b", "neg_f", "neg_b", "sneg_f", "sneg_b", "iota")


def constants():
    r, c = np.arange(P)[:, None], np.arange(P)[None, :]
    out = {
        "ident": r == c,
        "ones": np.ones((P, P)),
        "tri_f": r <= c,
        "tri_b": r >= c,
        "neg_f": np.where(c >= r, 0.0, NEG),
        "neg_b": np.where(c <= r, 0.0, NEG),
        "sneg_f": np.where(c < r, 0.0, NEG),
        "sneg_b": np.where(c > r, 0.0, NEG),
        "iota": c + 0 * r,
    }
    return np.ascontiguousarray(np.stack([out[n] for n in CONSTS], 1).astype(np.float32))


def level_masks():
    r, c = np.arange(P)[:, None], np.arange(P)[None, :]
    low = [(r // s % 2 == 1) & (c // s == r // s - 1) for s in (1 << n for n in range(LEVELS))]
    return np.stack([np.stack(low, 1), np.stack([m.T for m in low], 1)], 1).astype(np.float32)


class Slots:

    def __init__(self, sem, order):
        self.ready = [sem(f"psum{s}_ready") for s in range(NSLOT)]
        self.free = [sem(f"psum{s}_free") for s in range(NSLOT)]
        self.per = [0] * NSLOT
        self.at = {}
        for key, slot in order:
            self.at[key] = (slot, self.per[slot])
            self.per[slot] += 1

    def slot(self, key):
        return self.at[key][0]

    def credit(self, engine):
        for s in range(NSLOT):
            if self.per[s]:
                engine.sem_inc(self.free[s], 1)

    def claim(self, pe, key, i=0):
        s, n = self.at[key]
        pe.wait_ge(self.free[s], i * self.per[s] + n + 1)

    def wait(self, engine, key, i=0):
        s, n = self.at[key]
        engine.wait_ge(self.ready[s], i * self.per[s] + n + 1)


class Core:

    def __init__(self, nc, ctx, dram):
        self.nc, self.dram = nc, dram

        def sb(name, shape, dtype=F32):
            return ctx.enter_context(nc.sbuf_tensor(name, shape, dtype))

        self.x = sb("residual", [P, KT, T])
        self.h = sb("hidden", [P, KT, T])
        self.const = sb("consts", [P, len(CONSTS), P])
        self.mod = sb("modulation", [P, DEPTH, 6, KT, 2])
        self.gains = sb("norm_gains", [P, 2 * DEPTH + 1, KT, 2])
        self.ps = ctx.enter_context(nc.psum_tensor("psum", [P, NSLOT, SLOT], F32))

    def c(self, name):
        return self.const[:, CONSTS.index(name), :]

    def stage(self, ctx, name):
        nc = self.nc
        sems = []

        def clear():
            nc.clear_and_free_semaphores(sems)
            nc.all_engine_barrier()

        ctx.callback(clear)

        def sb(label, shape, dtype=F32):
            return ctx.enter_context(nc.sbuf_tensor(f"{name}_{label}", shape, dtype))

        def sem(label):
            sems.append(nc.alloc_semaphore(f"{name}_{label}"))
            return sems[-1]

        return sb, sem


def one(ap, i):
    return ap[:, bass.ds(i, 1)]


def both(nc, out, lhsT, rhs, start, stop):
    nc.tensor.matmul(out[:, 0:LAT], lhsT, rhs[:, 0:LAT], start=start, stop=stop)
    return nc.tensor.matmul(out[:, LAT:T], lhsT, rhs[:, LAT:T], start=start, stop=stop)


def bcast(ap, axis, shape):
    return ap.unsqueeze(axis).to_broadcast(shape)



def load_phase(k):
    nc, d = k.nc, k.dram
    with ExitStack() as ctx:
        sb, sem = k.stage(ctx, "load")
        pos = sb("pos", [P, KT, LAT])
        loaded, added = sem("loaded"), sem("added")
        block = ctx.enter_context(nc.Block())

        @block.sync
        def _(sp):
            sp.dma_start(k.x[:], d["x"]).then_inc(loaded, 16)
            sp.dma_start(pos[:], d["pos"]).then_inc(loaded, 16)
            sp.dma_start(k.const[:], d["consts"]).then_inc(loaded, 16)
            sp.dma_start(k.gains[:], d["gains"]).then_inc(loaded, 16)

        @block.vector
        def _(dve):
            dve.wait_ge(loaded, 64)
            nc.vector.tensor_tensor(k.x[:, :, 0:LAT], k.x[:, :, 0:LAT], pos[:], ALU.add).then_inc(added, 1)
            dve.wait_ge(added, 1)


def modulation_phase(k):
    nc, d = k.nc, k.dram
    W = 4
    N = DEPTH * 6 * KT // W
    with ExitStack() as ctx:
        sb, sem = k.stage(ctx, "mod")
        cond, silu = sb("cond", [P, KT, 2]), sb("silu", [P, KT, 2])
        bias = sb("bias", [P, DEPTH * 6 * KT, 2])
        w = sb("w", [P, 2, KT, W * P])
        out = k.mod[:].rearrange("p l s k g -> p (l s k) g")
        small, activated = sem("small_loaded"), sem("silu_ready")
        w_loaded = [sem(f"w{b}_loaded") for b in range(2)]
        w_free, made, taken = sem("w_free"), sem("product_ready"), sem("product_taken")
        block = ctx.enter_context(nc.Block())

        @block.sync
        def _(sp):
            sp.dma_start(cond[:], d["cond"]).then_inc(small, 16)
            sp.dma_start(bias[:], d["b_mod"]).then_inc(small, 16)
            with sp.Fori(0, N // 2) as i:
                for b in range(2):
                    sp.wait_ge(w_free, 2 * i + b + 1)
                    sp.dma_start(w[:, b], d["w_mod"][bass.ds(2 * i + b, 1)].rearrange("o p k n -> p (o k) n")
                                 ).then_inc(w_loaded[b], 16)

        @block.scalar
        def _(act):
            act.wait_ge(small, 32)
            nc.scalar.activation(silu[:], cond[:], ACT.Silu).then_inc(activated, 1)

        @block.tensor
        def _(pe):
            pe.sem_inc(w_free, 2)
            pe.wait_ge(activated, 1)
            with pe.Fori(0, N // 2) as i:
                for b in range(2):
                    pe.wait_ge(w_loaded[b], 16 * (i + 1))
                    pe.wait_ge(taken, 2 * i + b + 1)
                    for q in range(W):
                        for kt in range(KT):
                            last = nc.tensor.matmul(k.ps[:, b, 2 * q:2 * q + 2], w[:, b, kt, q * P:(q + 1) * P],
                                                    silu[:, kt, :], start=(kt == 0), stop=(kt == KT - 1))
                    last.then_inc(made, 1)
                    pe.wait_ge(made, 2 * i + b + 1)
                    pe.sem_inc(w_free, 1)

        @block.vector
        def _(dve):
            dve.sem_inc(taken, 2)
            dve.wait_ge(small, 32)
            with dve.Fori(0, N // 2) as i:
                for b in range(2):
                    dve.wait_ge(made, 2 * i + b + 1)
                    at = bass.ds(W * (2 * i + b), W)
                    nc.vector.tensor_tensor(out[:, at, :], k.ps[:, b, 0:2 * W].rearrange("p (q g) -> p q g", g=2),
                                            bias[:, at, :], ALU.add).then_inc(taken, 1)



def norm_phase(k, name, src, tiles, finish, out_dram=None):
    nc = k.nc
    with ExitStack() as ctx:
        sb, sem = k.stage(ctx, name)
        sq, rms, rstd = sb("squares", [P, 2, T]), sb("rms", [P, T]), sb("rstd", [P, T])
        epsc = sb("eps", [P, 1])
        squared, summed, rooted, normed, stored = (sem(s) for s in ("squared", "summed", "rooted", "normed", "stored"))
        eps_set = sem("eps_set")
        block = ctx.enter_context(nc.Block())
        out = k.ps[:, 0, 0:T]

        @block.scalar
        def _(act):
            for t in range(tiles):
                if t >= 2:
                    act.wait_ge(summed, t - 1)
                nc.scalar.activation(sq[:, t % 2], src[:, t], ACT.Square).then_inc(squared, 1)
            act.wait_ge(summed, tiles)
            act.wait_ge(eps_set, 1)
            nc.scalar.activation(rms[:], out, ACT.Sqrt, scale=1.0 / (tiles * P), bias=epsc[:]).then_inc(rooted, 1)

        @block.tensor
        def _(pe):
            for t in range(tiles):
                pe.wait_ge(squared, t + 1)
                both(nc, out, k.c("ones"), sq[:, t % 2], t == 0, t == tiles - 1).then_inc(summed, 1)

        @block.vector
        def _(dve):
            nc.vector.memset(epsc[:], EPS).then_inc(eps_set, 1)
            dve.wait_ge(rooted, 1)
            nc.vector.reciprocal(rstd[:], rms[:])
            dve.drain()
            finish(dve, rstd)
            dve.drain()
            dve.sem_inc(normed, 1)

        @block.sync
        def _(sp):
            sp.wait_ge(normed, 1)
            if out_dram is not None:
                sp.dma_start(out_dram, k.h[:]).then_inc(stored, 16)
                sp.wait_ge(stored, 16)


def adaln_phase(k, layer, half):
    nc = k.nc
    with ExitStack() as ctx:
        gain = ctx.enter_context(nc.sbuf_tensor(f"adaln_gain{layer}{half}", [P, KT, 2], F32))

        def finish(dve, rstd):
            nc.vector.scalar_tensor_tensor(gain[:], k.mod[:, layer, 3 * half + 1], 1.0, k.gains[:, 2 * half + layer],
                                           ALU.add, ALU.mult)
            for t in range(KT):
                nc.vector.tensor_tensor(k.h[:, t], k.x[:, t], rstd[:], ALU.mult)
            dve.drain()
            for t in range(KT):
                for g, (a, b) in enumerate(SEG):
                    nc.vector.tensor_scalar(k.h[:, t, a:b], k.h[:, t, a:b], gain[:, t, g:g + 1],
                                            k.mod[:, layer, 3 * half, t, g:g + 1], ALU.mult, ALU.add)

        norm_phase(k, f"adaln{layer}{half}", k.x, KT, finish)


def final_phase(k):
    nc = k.nc

    def finish(dve, rstd):
        for t in range(KT):
            nc.vector.scalar_tensor_tensor(k.h[:, t], k.x[:, t], k.gains[:, 2 * DEPTH, t, 0:1], rstd[:],
                                           ALU.mult, ALU.mult)

    norm_phase(k, "final", k.x, KT, finish, out_dram=k.dram["y"])



def softplus_steps(nc, engine, which, v, e, u, l, done):
    if which == "act":
        nc.scalar.activation(e, v, ACT.Abs)
        engine.drain()
        nc.scalar.activation(e, e, ACT.Exp, scale=-1.0).then_inc(done, 1)
        engine.wait_ge(done, 2)
        nc.scalar.activation(l, u, ACT.Ln).then_inc(done, 1)
        return
    engine.wait_ge(done, 1)
    nc.vector.tensor_scalar(u, e, 1.0, None, ALU.add).then_inc(done, 1)
    engine.wait_ge(done, 3)
    nc.vector.tensor_scalar(u, u, 1.0, None, ALU.subtract)
    engine.drain()
    nc.vector.scalar_tensor_tensor(l, u, 0.0, l, ALU.is_equal, ALU.add)
    engine.drain()
    nc.vector.scalar_tensor_tensor(u, u, 0.0, u, ALU.is_equal, ALU.add)
    engine.drain()
    nc.vector.reciprocal(u, u)
    engine.drain()
    nc.vector.tensor_tensor(l, l, u, ALU.mult)
    engine.drain()
    nc.vector.tensor_tensor(l, l, e, ALU.mult)
    engine.drain()
    nc.vector.scalar_tensor_tensor(v, v, 0.0, l, ALU.max, ALU.add)
    engine.drain()


def conv_taps(nc, out, src, w0, w2):
    for a, b in SEG:
        nc.vector.scalar_tensor_tensor(out[:, a + 1:b], src[:, a:b - 1], w0, out[:, a + 1:b], ALU.mult, ALU.add)
    nc.vector.drain()
    for a, b in SEG:
        last = nc.vector.scalar_tensor_tensor(out[:, a:b - 1], src[:, a + 1:b], w2, out[:, a:b - 1],
                                              ALU.mult, ALU.add)
    return last


def out_projection_phase(k, name, w_dram, src, tiles, layer):
    nc = k.nc
    with ExitStack() as ctx:
        sb, sem = k.stage(ctx, name)
        w = sb("w", [P, 2, tiles, P])
        w_loaded = [sem(f"w{b}_loaded") for b in range(2)]
        w_free, made, taken = sem("w_free"), sem("product_ready"), sem("product_taken")
        block = ctx.enter_context(nc.Block())

        @block.sync
        def _(sp):
            with sp.Fori(0, KT // 2) as i:
                for b in range(2):
                    sp.wait_ge(w_free, 2 * i + b + 1)
                    sp.dma_start(w[:, b], w_dram[bass.ds(2 * i + b, 1)].rearrange("o p k n -> p (o k) n")
                                 ).then_inc(w_loaded[b], 16)

        @block.tensor
        def _(pe):
            pe.sem_inc(w_free, 2)
            with pe.Fori(0, KT // 2) as i:
                for b in range(2):
                    pe.wait_ge(w_loaded[b], 16 * (i + 1))
                    pe.wait_ge(taken, 2 * i + b + 1)
                    for t in range(tiles):
                        last = both(nc, k.ps[:, b], w[:, b, t], src[:, t], t == 0, t == tiles - 1)
                    last.then_inc(made, 1)
                    pe.wait_ge(made, 2 * i + b + 1)
                    pe.sem_inc(w_free, 1)

        @block.vector
        def _(dve):
            dve.sem_inc(taken, 2)
            with dve.Fori(0, KT // 2) as i:
                for b in range(2):
                    dve.wait_ge(made, 2 * i + b + 1)
                    for g, (lo, hi) in enumerate(SEG):
                        x = k.x[:, bass.ds(2 * i + b, 1), lo:hi].rearrange("p o t -> p (o t)")
                        gate = k.mod[:, layer, 2, bass.ds(2 * i + b, 1), g]
                        last = nc.vector.scalar_tensor_tensor(x, k.ps[:, b, lo:hi], gate, x, ALU.mult, ALU.add)
                    last.then_inc(taken, 1)



SDT, SDTA, SACS, SW, SDEC = range(5)


def ssd_steps_phase(k, stats):
    nc, d = k.nc, k.dram
    H2 = 2 * SH
    with ExitStack() as ctx:
        sb, sem = k.stage(ctx, "ssd_dt")
        w, bias, alog = sb("w", [P, KT, H2]), sb("bias", [P, H2]), sb("alog", [P, H2])
        e, u, l = (sb(n, [P, NC * H2]) for n in ("e", "u", "l"))
        loaded, made, raw, steps, neg_a = (sem(s) for s in ("loaded", "product_ready", "raw", "softplus", "minus_a"))
        dta_ready, sums, weighed = sem("dta_ready"), sem("sums_ready"), sem("exponents")
        dt = stats[:, SDT].rearrange("p c h -> p (c h)")
        block = ctx.enter_context(nc.Block())
        sum_ps = k.ps[:, 1, 0:NC * H2].rearrange("p (c h) -> p c h", h=H2)
        tot_ps = k.ps[:, 2, 0:NC * H2].rearrange("p (c h) -> p c h", h=H2)

        @block.sync
        def _(sp):
            sp.dma_start(w[:], d["ssd_w_dt"]).then_inc(loaded, 16)
            sp.dma_start(bias[:], d["ssd_dt_bias"]).then_inc(loaded, 16)
            sp.dma_start(alog[:], d["ssd_a_log"]).then_inc(loaded, 16)

        @block.tensor
        def _(pe):
            pe.wait_ge(loaded, 48)
            for c in range(NC):
                for t in range(KT):
                    last = nc.tensor.matmul(k.ps[:, 0, c * H2:(c + 1) * H2], k.h[:, t, c * P:(c + 1) * P], w[:, t],
                                            start=(t == 0), stop=(t == KT - 1))
            last.then_inc(made, 1)
            pe.wait_ge(dta_ready, 1)
            for i, tri in enumerate(("tri_f", "tri_b")):
                for c in range(NC):
                    nc.tensor.matmul(sum_ps[:, c, i * SH:(i + 1) * SH], k.c(tri),
                                     stats[:, SDTA, c, i * SH:(i + 1) * SH], start=True, stop=True)
            nc.tensor.matmul(k.ps[:, 2, 0:NC * H2], k.c("ones"), stats[:, SDTA].rearrange("p c h -> p (c h)"),
                             start=True, stop=True).then_inc(sums, 1)

        @block.scalar
        def _(act):
            act.wait_ge(loaded, 48)
            nc.scalar.activation(alog[:], alog[:], ACT.Exp).then_inc(neg_a, 1)
            act.wait_ge(raw, 1)
            softplus_steps(nc, act, "act", dt, e[:], u[:], l[:], steps)
            act.wait_ge(weighed, 1)
            nc.scalar.activation(stats[:, SW], stats[:, SW], ACT.Exp)
            nc.scalar.activation(stats[:, SDEC], tot_ps, ACT.Exp).then_inc(weighed, 1)

        @block.vector
        def _(dve):
            dve.wait_ge(loaded, 48)
            dve.wait_ge(made, 1)
            nc.vector.tensor_tensor(stats[:, SDT], k.ps[:, 0, 0:NC * H2].rearrange("p (c h) -> p c h", h=H2),
                                    bcast(bias[:], 1, [P, NC, H2]), ALU.add).then_inc(raw, 1)
            softplus_steps(nc, dve, "dve", dt, e[:], u[:], l[:], steps)
            dve.wait_ge(neg_a, 1)
            nc.vector.scalar_tensor_tensor(stats[:, SDTA], stats[:, SDT], -1.0, bcast(alog[:], 1, [P, NC, H2]),
                                           ALU.mult, ALU.mult).then_inc(dta_ready, 1)
            dve.wait_ge(sums, 1)
            nc.vector.tensor_copy(stats[:, SACS], sum_ps)
            dve.drain()
            nc.vector.tensor_tensor(stats[:, SW], tot_ps, stats[:, SACS], ALU.subtract).then_inc(weighed, 1)
            dve.wait_ge(weighed, 2)
            nc.vector.tensor_tensor(stats[:, SW], stats[:, SW], stats[:, SDT], ALU.mult)


def ssd_groups_phase(k, stats, y):
    nc, d = k.nc, k.dram
    NW = 2
    assert STILES % NW == 0
    FWD, BWD = 0, 1
    incs = [(FWD, 0), (BWD, 3), (FWD, 1), (BWD, 2), (FWD, 2), (BWD, 1), (FWD, CTXC), (BWD, CTXC)]
    order = [(("proj", t), t % 4) for t in range(STILES)]
    order += [(("turn", c), (STILES + c) % 4) for c in range(NC)]
    order += [("cb", 3)] + [(("inc", n), 2 + n % 2) for n in range(len(incs))]
    order += [((what, r), slot) for r in range(SR) for what, slot in (("sumf", 0), ("sumb", 1))]
    order += [(("y", q), 2 + q % 2) for q in range(SXT)]
    with ExitStack() as ctx:
        sb, sem = k.stage(ctx, "ssd")
        slots = Slots(sem, order)
        w = sb("w", [P, NW, KT, P])
        convw_all, convw = sb("convw_all", [P, SG, SCONV, 4]), sb("convw", [P, SCONV, 4])
        skip_all, skip = sb("skip_all", [P, SG, SXT]), sb("skip", [P, SXT])
        st = sb("stats", [P, 5, NC, 2, SR])
        tap = sb("tap", [P, 2, T])
        xbc = sb("xbc", [P, SCONV, T])
        z = sb("z", [P, SXT, T])
        tok = sb("tok", [P, NC, (SXT + 1) * P])
        cb = sb("cb", [P, T])
        xw = sb("xw", [P, 2, SXT * P])
        state = sb("state", [P, 2, NC - 1, SXT * P])
        decayed = sb("decayed", [P, SXT * P])
        ctx_state = sb("ctx_state", [P, 2, SXT * P])
        lm = sb("lm", [P, 2, 2, T])
        ea = sb("ea", [P, 2, 2, T])
        m = sb("m", [P, 2, T])
        ysum = sb("ysum", [P, T])
        B, C = xbc[:, SXT], xbc[:, SXT + 1]

        small, w_free = sem("small_loaded"), sem("w_free")
        w_loaded = [sem(f"w{b}_loaded") for b in range(NW)]
        init_loaded, group_free, stat_ready = sem("init_loaded"), sem("group_free"), sem("stat_ready")
        centre, tapped, convolved, gated = sem("centre_ready"), sem("tapped"), sem("convolved"), sem("z_ready")
        turned, cb_ready = sem("turned"), sem("cb_ready")
        weighted, states_ready, ctx_ready, ctx_stored = (sem(s) for s in (
            "weighted", "states_ready", "ctx_ready", "ctx_stored"))
        diff, lm_ready, m_ready, m_used = sem("diff_ready"), sem("lm_ready"), sem("m_ready"), sem("m_used")
        ps = k.ps
        block = ctx.enter_context(nc.Block())

        @block.sync
        def _(sp):
            sp.dma_start(convw_all[:], d["ssd_conv"]).then_inc(small, 16)
            sp.dma_start(skip_all[:], d["ssd_skip"]).then_inc(small, 16)
            sp.sem_inc(ctx_stored, 32)
            with sp.Fori(0, SG) as i:
                for t in range(STILES):
                    if t == SCONV:
                        sp.wait_ge(group_free, i + 1)
                        for dr, first in ((FWD, 0), (BWD, NC - 2)):
                            sp.dma_start(state[:, dr, first], d["ssd_state"][bass.ds(2 * i + dr, 1)]
                                         .rearrange("o n p -> n (o p)")).then_inc(init_loaded, 16)
                    sp.wait_ge(w_free, STILES * i + t + 1)
                    sp.dma_start(w[:, t % NW], d["ssd_w_in"][bass.ds(STILES * i + t, 1)]
                                 .rearrange("o p k n -> p (o k) n")).then_inc(w_loaded[t % NW], 16)
                for dr in range(2):
                    sp.wait_ge(ctx_ready, 2 * i + dr + 1)
                    sp.dma_start(d["ssd_out"][bass.ds(2 * i + dr, 1)].rearrange("o n p -> n (o p)"),
                                 ctx_state[:, dr]).then_inc(ctx_stored, 16)
            sp.wait_ge(ctx_stored, 32 * (SG + 1))

        @block.tensor
        def _(pe):
            pe.sem_inc(w_free, NW)
            with pe.Fori(0, SG) as i:
                for t in range(STILES):
                    pe.wait_ge(w_loaded[t % NW], 16 * (STILES // NW * i + t // NW + 1))
                    slots.claim(pe, ("proj", t), i)
                    s = slots.slot(("proj", t))
                    for kt in range(KT):
                        last = both(nc, ps[:, s], w[:, t % NW, kt], k.h[:, kt], kt == 0, kt == KT - 1)
                    last.then_inc(slots.ready[s], 1)
                    slots.wait(pe, ("proj", t), i)
                    pe.sem_inc(w_free, 1)
                pe.wait_ge(convolved, SCONV * (i + 1))
                for c in range(NC):
                    slots.claim(pe, ("turn", c), i)
                    s = slots.slot(("turn", c))
                    for t in range(SXT + 1):
                        last = nc.tensor.transpose(ps[:, s, t * P:(t + 1) * P], xbc[:, t, c * P:(c + 1) * P],
                                                   k.c("ident"))
                    last.then_inc(slots.ready[s], 1)
                slots.claim(pe, "cb", i)
                s = slots.slot("cb")
                for c in range(NC):
                    last = nc.tensor.matmul(ps[:, s, c * P:(c + 1) * P], B[:, c * P:(c + 1) * P],
                                            C[:, c * P:(c + 1) * P], start=True, stop=True)
                last.then_inc(slots.ready[s], 1)
                pe.wait_ge(turned, NC * (i + 1))
                for n, (dr, c) in enumerate(incs):
                    pe.wait_ge(weighted, len(incs) * i + n + 1)
                    slots.claim(pe, ("inc", n), i)
                    s = slots.slot(("inc", n))
                    nc.tensor.matmul(ps[:, s, 0:SXT * P], tok[:, c, SXT * P:], xw[:, n % 2],
                                     start=True, stop=True).then_inc(slots.ready[s], 1)

                def sums(r):
                    for dr, what, tri in ((FWD, "sumf", "tri_f"), (BWD, "sumb", "tri_b")):
                        slots.claim(pe, (what, r), i)
                        s = slots.slot((what, r))
                        for c in range(NC):
                            last = nc.tensor.matmul(ps[:, s, c * P:(c + 1) * P],
                                                    st[:, SDTA, c, dr, r:r + 1].to_broadcast([P, P]), k.c(tri),
                                                    start=True, stop=True)
                        last.then_inc(slots.ready[s], 1)

                pe.wait_ge(stat_ready, i + 1)
                sums(0)
                for r in range(SR):
                    if r + 1 < SR:
                        sums(r + 1)
                    q, half = r // 2, (r % 2) * SP_
                    s = slots.slot(("y", q))
                    if r % 2 == 0:
                        slots.claim(pe, ("y", q), i)
                    if r == 0:
                        pe.wait_ge(states_ready, i + 1)
                        pe.wait_ge(init_loaded, 32 * (i + 1))
                    pe.wait_ge(m_ready, SR * i + r + 1)
                    hp = slice(r * SP_, (r + 1) * SP_)
                    for c in range(NC):
                        cs = slice(c * P, (c + 1) * P)
                        o = ps[half:half + SP_, s, cs]
                        last = nc.tensor.matmul(o, tok[:, c, hp], m[:, r % 2, cs], start=True, stop=(c == CTXC))
                        if c != CTXC:
                            for dr in range(2):
                                last = nc.tensor.matmul(o, state[:, dr, c, hp], ea[:, r % 2, dr, cs],
                                                        start=False, stop=(dr == 1))
                    last.then_inc(m_used, 1)
                    if r % 2:
                        pe.wait_ge(m_used, SR * i + r + 1)
                        pe.sem_inc(slots.ready[s], 1)

        @block.scalar
        def _(act):
            act.wait_ge(small, 32)
            with act.Fori(0, SG) as i:
                act.wait_ge(group_free, i + 1)
                act.wait_ge(stat_ready, i + 1)
                for t in range(SCONV + 1):
                    if t < SCONV:
                        slots.wait(act, ("proj", t), i)
                        if t >= 2:
                            act.wait_ge(convolved, SCONV * i + t - 1)
                        nc.scalar.activation(tap[:, t % 2], ps[:, slots.slot(("proj", t)), 0:T], ACT.Identity,
                                             scale=convw[:, t, 1:2], bias=convw[:, t, 3:4]).then_inc(centre, 1)
                    if t >= 1:
                        act.wait_ge(tapped, SCONV * i + t)
                        nc.scalar.activation(xbc[:, t - 1], tap[:, (t - 1) % 2], ACT.Silu).then_inc(convolved, 1)
                for t in range(SXT):
                    slots.wait(act, ("proj", SCONV + t), i)
                    s = slots.slot(("proj", SCONV + t))
                    nc.scalar.activation(z[:, t], ps[:, s, 0:T], ACT.Silu).then_inc(slots.free[s], 1)
                act.drain()
                act.sem_inc(gated, 1)
                for c in range(NC):
                    slots.wait(act, ("turn", c), i)
                    s = slots.slot(("turn", c))
                    nc.scalar.copy(tok[:, c], ps[:, s, 0:(SXT + 1) * P]).then_inc(slots.free[s], 1)
                    act.drain()
                    act.sem_inc(turned, 1)
                for r in range(SR):
                    act.wait_ge(diff, SR * i + r + 1)
                    for dr, what in ((FWD, "sumf"), (BWD, "sumb")):
                        slots.wait(act, (what, r), i)
                        s = slots.slot((what, r))
                        nc.scalar.activation(ea[:, r % 2, dr], ps[:, s, 0:T], ACT.Exp).then_inc(slots.free[s], 1)
                    nc.scalar.activation(lm[:, r % 2], lm[:, r % 2], ACT.Exp)
                    act.drain()
                    act.sem_inc(lm_ready, 1)

        @block.vector
        def _(dve):
            slots.credit(dve)
            dve.sem_inc(group_free, 1)
            dve.wait_ge(small, 32)
            with dve.Fori(0, SG) as i:
                dve.wait_ge(group_free, i + 1)
                nc.vector.tensor_copy(st[:].rearrange("p k c d r -> p (k c d) r"),
                                      stats[:].rearrange("p k c (d h) -> p (k c d) h", h=SH)[:, :, bass.ts(i, SR)])
                nc.vector.tensor_copy(skip[:], skip_all[:, bass.ds(i, 1)].rearrange("p o t -> p (o t)"))
                nc.vector.tensor_copy(convw[:], convw_all[:, bass.ds(i, 1)].rearrange("p o t n -> p (o t) n"))
                dve.drain()
                dve.sem_inc(stat_ready, 1)
                for t in range(SCONV):
                    dve.wait_ge(centre, SCONV * i + t + 1)
                    s = slots.slot(("proj", t))
                    conv_taps(nc, tap[:, t % 2], ps[:, s], convw[:, t, 0:1], convw[:, t, 2:3]
                              ).then_inc(slots.free[s], 1)
                    dve.drain()
                    dve.sem_inc(tapped, 1)
                slots.wait(dve, "cb", i)
                s = slots.slot("cb")
                nc.vector.tensor_copy(cb[:], ps[:, s, 0:T]).then_inc(slots.free[s], 1)
                dve.wait_ge(turned, NC * (i + 1))
                dve.wait_ge(init_loaded, 32 * (i + 1))

                def weigh(n):
                    dr, c = incs[n]
                    nc.vector.tensor_tensor(xw[:, n % 2].rearrange("p (r q) -> p r q", q=SP_),
                                            tok[:, c, 0:SXT * P].rearrange("p (r q) -> p r q", q=SP_),
                                            bcast(st[:, SW, c, dr], 2, [P, SR, SP_]), ALU.mult
                                            ).then_inc(weighted, 1)

                weigh(0)
                for n, (dr, c) in enumerate(incs):
                    if n + 1 < len(incs):
                        if n >= 1:
                            slots.wait(dve, ("inc", n - 1), i)
                        weigh(n + 1)
                    s = slots.slot(("inc", n))
                    if c == CTXC:
                        if dr == FWD:
                            dve.wait_ge(ctx_stored, 32 * i + 32)
                        slots.wait(dve, ("inc", n), i)
                        nc.vector.tensor_copy(ctx_state[:, dr], ps[:, s, 0:SXT * P]).then_inc(slots.free[s], 1)
                        dve.drain()
                        dve.sem_inc(ctx_ready, 1)
                        continue
                    nc.vector.tensor_tensor(decayed[:].rearrange("p (r q) -> p r q", q=SP_),
                                            state[:, dr, c].rearrange("p (r q) -> p r q", q=SP_),
                                            bcast(st[:, SDEC, c, dr], 2, [P, SR, SP_]), ALU.mult)
                    dve.drain()
                    slots.wait(dve, ("inc", n), i)
                    nc.vector.tensor_tensor(state[:, dr, c + 1 if dr == FWD else c - 1], ps[:, s, 0:SXT * P],
                                            decayed[:], ALU.add).then_inc(slots.free[s], 1)
                    dve.drain()
                dve.sem_inc(states_ready, 1)

                def differences(r):
                    for dr, what, neg in ((FWD, "sumf", "neg_f"), (BWD, "sumb", "neg_b")):
                        slots.wait(dve, (what, r), i)
                        s = slots.slot((what, r))
                        for c in range(NC):
                            cs = slice(c * P, (c + 1) * P)
                            last = nc.vector.scalar_tensor_tensor(
                                lm[:, r % 2, dr, cs], ps[:, s, cs], st[:, SACS, c, dr, r:r + 1], k.c(neg),
                                ALU.subtract, ALU.add)
                    last.then_inc(diff, 1)

                def heads_out(q):
                    slots.wait(dve, ("y", q), i)
                    s = slots.slot(("y", q))
                    nc.vector.scalar_tensor_tensor(ysum[:], xbc[:, q], skip[:, q:q + 1], ps[:, s, 0:T],
                                                   ALU.mult, ALU.add).then_inc(slots.free[s], 1)
                    dve.drain()
                    nc.vector.tensor_tensor(y[:, bass.ds(SXT * i + q, 1)].rearrange("p o t -> p (o t)"),
                                            ysum[:], z[:, q], ALU.mult)
                    dve.drain()

                dve.wait_ge(gated, i + 1)
                differences(0)
                for r in range(SR):
                    if r + 1 < SR:
                        if r >= 1:
                            dve.wait_ge(m_used, SR * i + r)
                        differences(r + 1)
                    if r >= 2 and r % 2 == 0:
                        heads_out(r // 2 - 1)
                    dve.wait_ge(lm_ready, SR * i + r + 1)
                    nc.vector.tensor_tensor(ea[:, r % 2], ea[:, r % 2], bcast(C, 1, [P, 2, T]), ALU.mult)
                    for c in range(NC):
                        cs = slice(c * P, (c + 1) * P)
                        nc.vector.tensor_scalar(lm[:, r % 2, BWD, cs], lm[:, r % 2, BWD, cs],
                                                st[:, SDT, c, BWD, r:r + 1], None, ALU.mult)
                    dve.drain()
                    for c in range(NC):
                        cs = slice(c * P, (c + 1) * P)
                        nc.vector.scalar_tensor_tensor(m[:, r % 2, cs], lm[:, r % 2, FWD, cs],
                                                       st[:, SDT, c, FWD, r:r + 1], lm[:, r % 2, BWD, cs],
                                                       ALU.mult, ALU.add)
                    dve.drain()
                    nc.vector.tensor_tensor(m[:, r % 2], m[:, r % 2], cb[:], ALU.mult)
                    dve.drain()
                    dve.sem_inc(m_ready, 1)
                heads_out(SXT - 1)
                dve.sem_inc(group_free, 1)


def ssd_mixer(k):
    nc = k.nc
    with ExitStack() as ctx:
        y = ctx.enter_context(nc.sbuf_tensor("ssd_y", [P, SINNER // P, T], F32))
        with ExitStack() as inner:
            stats = inner.enter_context(nc.sbuf_tensor("ssd_stats_all", [P, 5, NC, 2 * SH], F32))
            ssd_steps_phase(k, stats)
            ssd_groups_phase(k, stats, y)
        gain = ctx.enter_context(nc.sbuf_tensor("ssd_gain", [P, SINNER // P], F32))
        with ExitStack() as inner:
            _, sem = k.stage(inner, "ssd_gain")
            got = sem("loaded")
            block = inner.enter_context(nc.Block())

            @block.sync
            def _(sp):
                sp.dma_start(gain[:], k.dram["ssd_norm"]).then_inc(got, 16)
                sp.wait_ge(got, 16)

        def finish(dve, rstd):
            for t in range(SINNER // P):
                nc.vector.scalar_tensor_tensor(y[:, t], y[:, t], gain[:, t:t + 1], rstd[:], ALU.mult, ALU.mult)

        norm_phase(k, "ssd_norm", y, SINNER // P, finish)
        out_projection_phase(k, "ssd_out", k.dram["ssd_w_out"], y, SINNER // P, 0)



GB, GG, GC, GNBE, GKW, GDEC = range(6)


def gdn_steps_phase(k, stats):
    nc, d = k.nc, k.dram
    H2 = 2 * GH
    with ExitStack() as ctx:
        sb, sem = k.stage(ctx, "gdn_g")
        w, bias, alog = sb("w", [P, KT, 2 * H2]), sb("bias", [P, H2]), sb("alog", [P, H2])
        e, u, l = (sb(n, [P, NC * H2]) for n in ("e", "u", "l"))
        loaded, made, raw, steps, neg_a = (sem(s) for s in ("loaded", "product_ready", "raw", "softplus", "minus_a"))
        g_ready, sums, weighed = sem("g_ready"), sem("sums_ready"), sem("exponents")
        g = stats[:, GG].rearrange("p c h -> p (c h)")
        block = ctx.enter_context(nc.Block())
        raw_ps = k.ps[:, 0, 0:NC * 2 * H2].rearrange("p (c w h) -> p c w h", w=2, h=H2)
        sum_ps = k.ps[:, 1, 0:NC * H2].rearrange("p (c h) -> p c h", h=H2)
        tot_ps = k.ps[:, 2, 0:NC * H2].rearrange("p (c h) -> p c h", h=H2)

        @block.sync
        def _(sp):
            sp.dma_start(w[:], d["gdn_w_ab"]).then_inc(loaded, 16)
            sp.dma_start(bias[:], d["gdn_dt_bias"]).then_inc(loaded, 16)
            sp.dma_start(alog[:], d["gdn_a_log"]).then_inc(loaded, 16)

        @block.tensor
        def _(pe):
            pe.wait_ge(loaded, 48)
            for c in range(NC):
                for t in range(KT):
                    last = nc.tensor.matmul(k.ps[:, 0, c * 2 * H2:(c + 1) * 2 * H2], k.h[:, t, c * P:(c + 1) * P],
                                            w[:, t], start=(t == 0), stop=(t == KT - 1))
            last.then_inc(made, 1)
            pe.wait_ge(g_ready, 1)
            for i, tri in enumerate(("tri_f", "tri_b")):
                for c in range(NC):
                    nc.tensor.matmul(sum_ps[:, c, i * GH:(i + 1) * GH], k.c(tri),
                                     stats[:, GG, c, i * GH:(i + 1) * GH], start=True, stop=True)
            nc.tensor.matmul(k.ps[:, 2, 0:NC * H2], k.c("ones"), g, start=True, stop=True).then_inc(sums, 1)

        @block.scalar
        def _(act):
            act.wait_ge(loaded, 48)
            nc.scalar.activation(alog[:], alog[:], ACT.Exp).then_inc(neg_a, 1)
            act.wait_ge(raw, 1)
            nc.scalar.activation(stats[:, GB], raw_ps[:, :, 0], ACT.Sigmoid)
            softplus_steps(nc, act, "act", g, e[:], u[:], l[:], steps)
            act.wait_ge(weighed, 1)
            nc.scalar.activation(stats[:, GKW], stats[:, GKW], ACT.Exp)
            nc.scalar.activation(stats[:, GNBE], stats[:, GC], ACT.Exp)
            nc.scalar.activation(stats[:, GDEC], tot_ps, ACT.Exp)
            act.drain()
            act.sem_inc(weighed, 1)

        @block.vector
        def _(dve):
            dve.wait_ge(loaded, 48)
            dve.wait_ge(made, 1)
            nc.vector.tensor_tensor(stats[:, GG], raw_ps[:, :, 1], bcast(bias[:], 1, [P, NC, H2]), ALU.add
                                    ).then_inc(raw, 1)
            softplus_steps(nc, dve, "dve", g, e[:], u[:], l[:], steps)
            dve.wait_ge(neg_a, 1)
            nc.vector.scalar_tensor_tensor(stats[:, GG], stats[:, GG], -1.0, bcast(alog[:], 1, [P, NC, H2]),
                                           ALU.mult, ALU.mult).then_inc(g_ready, 1)
            dve.wait_ge(sums, 1)
            nc.vector.tensor_copy(stats[:, GC], sum_ps)
            dve.drain()
            nc.vector.tensor_tensor(stats[:, GKW], tot_ps, stats[:, GC], ALU.subtract).then_inc(weighed, 1)
            dve.wait_ge(weighed, 2)
            nc.vector.scalar_tensor_tensor(stats[:, GNBE], stats[:, GNBE], -1.0, stats[:, GB], ALU.mult, ALU.mult)


def gdn_heads_phase(k, stats, y, gain):
    nc, d = k.nc, k.dram
    NW = 2
    FWD, BWD = 0, 1
    NEGS = (("sneg_f", "neg_f", "tri_f"), ("sneg_b", "neg_b", "tri_b"))
    steps = [(FWD, 0), (BWD, 3), (FWD, CTXC), (BWD, CTXC), (FWD, 1), (BWD, 2), (FWD, 2), (BWD, 1), (FWD, 3), (BWD, 0)]
    last_of = {FWD: NC - 2, BWD: 0}
    order = [(("proj", t), t % 4) for t in range(GTILES)] + [("qsum", 2), ("ksum", 3)]
    order += [(("turn", c), c % 2) for c in range(NC)] + [("kk", 2), ("qk", 3), (("g", 0), 0), (("g", 1), 1)]
    for n in range(LEVELS):
        for dr in range(2):
            if n:
                order += [(("lx", n, dr), 2 * dr)]
            order += [(("xt", n, dr), 2 * dr + 1)]
            if 0 < n < LEVELS - 1:
                order += [(("xi", n, dr), 2 * dr)]
    for dr, c in steps:
        if c != CTXC:
            order += [(("ks", dr, c), 2 * dr)]
        order += [(("vn", dr, c), 2 * dr + 1)]
        if c != last_of[dr]:
            order += [(("kv", dr, c), 2 * dr)]
    order += [(("o", v), v) for v in range(GVT)] + [("osum", 2)]
    with ExitStack() as ctx:
        sb, sem = k.stage(ctx, "gdn")
        slots = Slots(sem, order)
        w = sb("w", [P, NW, KT, P])
        masks = sb("level_masks", [P, 2, LEVELS, P])
        convw_all, convw = sb("convw_all", [P, GH, GCONV, 3]), sb("convw", [P, GCONV, 3])
        st = sb("stats", [P, 6, NC, 2])
        epsc = sb("eps", [P, 1])
        tap = sb("tap", [P, 2, T])
        qkv = sb("qkv", [P, GCONV, T])
        z = sb("z", [P, GVT, T])
        sq = sb("squares", [P, GVT, T])
        root = sb("roots", [P, GVT, T])
        tok = sb("tok", [P, NC, (1 + GVT) * P])
        kk = sb("kk", [P, T])
        qk = sb("qk", [P, T])
        ba = sb("ba", [P, 2, T])
        aqk = sb("aqk", [P, 2, T])
        qg = sb("qg", [P, 2, T])
        level = sb("level", [P, 2, T])
        xi, xt, lx = sb("xi", [P, 2, T]), sb("xt", [P, 2, T]), sb("lx", [P, 2, T])
        kg = sb("kg", [P, 2, P])
        rhs = sb("rhs", [P, 2, GDV])
        state = sb("state", [P, 2, NC - 1, GDV])
        ctx_state = sb("ctx_state", [P, 2, GDV])
        vn = sb("vn", [P, 2, NC, GDV])

        small, w_free = sem("small_loaded"), sem("w_free")
        w_loaded = [sem(f"w{b}_loaded") for b in range(NW)]
        init_loaded, head_free, stat_ready = sem("init_loaded"), sem("head_free"), sem("stat_ready")
        centre, tapped, convolved, gated = sem("centre_ready"), sem("tapped"), sem("convolved"), sem("z_ready")
        squared, rooted, unit = sem("squared"), sem("rooted"), sem("q_k_unit_length")
        turned, kk_ready, diff, decays = sem("turned"), sem("kk_ready"), sem("diff_ready"), sem("decays_ready")
        level_ready = [sem(f"level_ready{b}") for b in range(2)]
        lx_ready = [sem(f"lx_ready{b}") for b in range(2)]
        x_ready = [sem(f"x_ready{b}") for b in range(2)]
        rhs_ready = [sem(f"rhs_ready{b}") for b in range(2)]
        vn_ready = [sem(f"vn_ready{b}") for b in range(2)]
        state_ready = [sem(f"state_ready{b}") for b in range(2)]
        aqk_ready, ctx_stored = sem("aqk_ready"), sem("ctx_stored")
        osq, oroot, o_in_psum_read = sem("o_squared"), sem("o_rooted"), sem("o_read")
        ps = k.ps
        q, kf, v0 = qkv[:, 0], qkv[:, 1], 2
        NS = len(steps) // 2
        block = ctx.enter_context(nc.Block())

        def cs(c):
            return slice(c * P, (c + 1) * P)

        @block.sync
        def _(sp):
            sp.dma_start(convw_all[:], d["gdn_conv"]).then_inc(small, 16)
            sp.dma_start(masks[:], d["levels"]).then_inc(small, 16)
            sp.sem_inc(ctx_stored, 32)
            with sp.Fori(0, GH) as i:
                for t in range(GTILES):
                    if t == GCONV:
                        sp.wait_ge(head_free, i + 1)
                        for dr, first in ((FWD, 0), (BWD, NC - 2)):
                            sp.dma_start(state[:, dr, first], d["gdn_state"][bass.ds(2 * i + dr, 1)]
                                         .rearrange("o n p -> n (o p)")).then_inc(init_loaded, 16)
                    sp.wait_ge(w_free, GTILES * i + t + 1)
                    sp.dma_start(w[:, t % NW], d["gdn_w_in"][bass.ds(GTILES * i + t, 1)]
                                 .rearrange("o p k n -> p (o k) n")).then_inc(w_loaded[t % NW], 16)
                for dr in range(2):
                    sp.wait_ge(state_ready[dr], (NS - 1) * i + 2)
                    sp.dma_start(d["gdn_out"][bass.ds(2 * i + dr, 1)].rearrange("o n p -> n (o p)"),
                                 ctx_state[:, dr]).then_inc(ctx_stored, 16)
            sp.wait_ge(ctx_stored, 32 * (GH + 1))

        @block.tensor
        def _(pe):
            pe.sem_inc(w_free, NW)
            with pe.Fori(0, GH) as i:
                def use(key):
                    slots.claim(pe, key, i)
                    return slots.slot(key)

                def done(key, last):
                    last.then_inc(slots.ready[slots.slot(key)], 1)

                for t in range(GTILES):
                    pe.wait_ge(w_loaded[t % NW], 16 * (GTILES // NW * i + t // NW + 1))
                    s = use(("proj", t))
                    for kt in range(KT):
                        last = both(nc, ps[:, s], w[:, t % NW, kt], k.h[:, kt], kt == 0, kt == KT - 1)
                    done(("proj", t), last)
                    slots.wait(pe, ("proj", t), i)
                    pe.sem_inc(w_free, 1)
                for n, key in enumerate(("qsum", "ksum")):
                    pe.wait_ge(squared, 2 * i + n + 1)
                    s = use(key)
                    done(key, both(nc, ps[:, s], k.c("ones"), sq[:, n], True, True))
                pe.wait_ge(unit, i + 1)
                for c in range(NC):
                    s = use(("turn", c))
                    for t in range(1 + GVT):
                        last = nc.tensor.transpose(ps[:, s, t * P:(t + 1) * P], qkv[:, 1 + t, cs(c)], k.c("ident"))
                    done(("turn", c), last)
                for key, moving in (("kk", kf), ("qk", q)):
                    s = use(key)
                    for c in range(NC):
                        last = nc.tensor.matmul(ps[:, s, cs(c)], kf[:, cs(c)], moving[:, cs(c)],
                                                start=True, stop=True)
                    done(key, last)
                pe.wait_ge(stat_ready, i + 1)
                for dr in range(2):
                    s = use(("g", dr))
                    for c in range(NC):
                        last = nc.tensor.matmul(ps[:, s, cs(c)], st[:, GG, c, dr:dr + 1].to_broadcast([P, P]),
                                                k.c(NEGS[dr][2]), start=True, stop=True)
                    done(("g", dr), last)
                NX = LEVELS - 1
                for n in range(LEVELS):
                    for dr in range(2):
                        pe.wait_ge(level_ready[dr], LEVELS * i + n + 1)
                        if n:
                            pe.wait_ge(x_ready[dr], LEVELS * i + n)
                            s = use(("lx", n, dr))
                            for c in range(NC):
                                last = nc.tensor.matmul(ps[:, s, cs(c)], level[:, dr, cs(c)], xt[:, dr, cs(c)],
                                                        start=True, stop=True)
                            done(("lx", n, dr), last)
                    for dr in range(2):
                        s = use(("xt", n, dr))
                        if n:
                            pe.wait_ge(lx_ready[dr], NX * i + n)
                        for c in range(NC):
                            last = nc.tensor.matmul(ps[:, s, cs(c)], xi[:, dr, cs(c)] if n else level[:, dr, cs(c)],
                                                    lx[:, dr, cs(c)] if n else k.c("ident"), start=True, stop=True)
                        done(("xt", n, dr), last)
                        if 0 < n < LEVELS - 1:
                            s = use(("xi", n, dr))
                            for c in range(NC):
                                last = nc.tensor.matmul(ps[:, s, cs(c)], lx[:, dr, cs(c)], xi[:, dr, cs(c)],
                                                        start=True, stop=True)
                            done(("xi", n, dr), last)
                pe.wait_ge(init_loaded, 32 * (i + 1))
                for m in range(NS):
                    pair = steps[2 * m:2 * m + 2]
                    for dr, c in pair:
                        if c != CTXC:
                            if m:
                                pe.wait_ge(state_ready[dr], (NS - 1) * i + m)
                            s = use(("ks", dr, c))
                            done(("ks", dr, c), nc.tensor.matmul(ps[:, s, 0:GDV], kf[:, cs(c)], state[:, dr, c],
                                                                 start=True, stop=True))
                    for dr, c in pair:
                        if m == 0:
                            pe.wait_ge(x_ready[dr], LEVELS * (i + 1))
                        pe.wait_ge(rhs_ready[dr], NS * i + m + 1)
                        s = use(("vn", dr, c))
                        done(("vn", dr, c), nc.tensor.matmul(ps[:, s, 0:GDV], xt[:, dr, cs(c)], rhs[:, dr],
                                                             start=True, stop=True))
                    for dr, c in pair:
                        if c != last_of[dr]:
                            pe.wait_ge(vn_ready[dr], NS * i + m + 1)
                            s = use(("kv", dr, c))
                            done(("kv", dr, c), nc.tensor.matmul(ps[:, s, 0:GDV], kg[:, dr], vn[:, dr, c],
                                                                 start=True, stop=True))
                pe.wait_ge(aqk_ready, i + 1)
                for dr in range(2):
                    pe.wait_ge(vn_ready[dr], NS * (i + 1))
                for v in range(GVT):
                    s = use(("o", v))
                    for c in range(NC):
                        pairs = []
                        for dr in range(2):
                            if c != CTXC:
                                pairs.append((state[:, dr, c, v * P:(v + 1) * P], qg[:, dr, cs(c)]))
                            pairs.append((vn[:, dr, c, v * P:(v + 1) * P], aqk[:, dr, cs(c)]))
                        for n, (a, b) in enumerate(pairs):
                            last = nc.tensor.matmul(ps[:, s, cs(c)], a, b, start=(n == 0), stop=(n == len(pairs) - 1))
                    done(("o", v), last)
                s = use("osum")
                for v in range(GVT):
                    pe.wait_ge(osq, GVT * i + v + 1)
                    last = both(nc, ps[:, s], k.c("ones"), sq[:, v], v == 0, v == GVT - 1)
                done("osum", last)

        @block.scalar
        def _(act):
            act.wait_ge(small, 32)
            with act.Fori(0, GH) as i:
                act.wait_ge(head_free, i + 1)
                act.wait_ge(stat_ready, i + 1)
                for t in range(GCONV + 1):
                    if t < GCONV:
                        slots.wait(act, ("proj", t), i)
                        if t >= 2:
                            act.wait_ge(convolved, GCONV * i + t - 1)
                        nc.scalar.activation(tap[:, t % 2], ps[:, slots.slot(("proj", t)), 0:T], ACT.Copy,
                                             scale=convw[:, t, 1:2]).then_inc(centre, 1)
                    if t >= 1:
                        act.wait_ge(tapped, GCONV * i + t)
                        nc.scalar.activation(qkv[:, t - 1], tap[:, (t - 1) % 2], ACT.Silu).then_inc(convolved, 1)
                for t in range(GVT):
                    slots.wait(act, ("proj", GCONV + t), i)
                    s = slots.slot(("proj", GCONV + t))
                    nc.scalar.activation(z[:, t], ps[:, s, 0:T], ACT.Silu).then_inc(slots.free[s], 1)
                act.drain()
                act.sem_inc(gated, 1)
                for n in range(2):
                    nc.scalar.activation(sq[:, n], qkv[:, n], ACT.Square).then_inc(squared, 1)
                for n, key in enumerate(("qsum", "ksum")):
                    slots.wait(act, key, i)
                    s = slots.slot(key)
                    nc.scalar.activation(root[:, n], ps[:, s, 0:T], ACT.Sqrt, bias=epsc[:]
                                         ).then_inc(slots.free[s], 1)
                act.drain()
                act.sem_inc(rooted, 1)
                for c in range(NC):
                    slots.wait(act, ("turn", c), i)
                    s = slots.slot(("turn", c))
                    nc.scalar.copy(tok[:, c], ps[:, s, 0:(1 + GVT) * P]).then_inc(slots.free[s], 1)
                act.drain()
                act.sem_inc(turned, 1)
                for dr in range(2):
                    act.wait_ge(diff, 2 * i + dr + 1)
                    s = slots.slot(("g", dr))
                    nc.scalar.activation(qg[:, dr], ps[:, s, 0:T], ACT.Exp).then_inc(slots.free[s], 1)
                    nc.scalar.activation(ba[:, dr], ba[:, dr], ACT.Exp, scale=-1.0)
                    nc.scalar.activation(aqk[:, dr], aqk[:, dr], ACT.Exp)
                    act.drain()
                    act.sem_inc(decays, 1)
                for n in range(1, LEVELS):
                    for dr in range(2):
                        slots.wait(act, ("lx", n, dr), i)
                        s = slots.slot(("lx", n, dr))
                        nc.scalar.copy(lx[:, dr], ps[:, s, 0:T]).then_inc(slots.free[s], 1)
                        act.drain()
                        act.sem_inc(lx_ready[dr], 1)
                for v in range(GVT):
                    slots.wait(act, ("o", v), i)
                    nc.scalar.activation(sq[:, v], ps[:, slots.slot(("o", v)), 0:T], ACT.Square).then_inc(osq, 1)
                slots.wait(act, "osum", i)
                s = slots.slot("osum")
                nc.scalar.activation(root[:, 0], ps[:, s, 0:T], ACT.Sqrt, scale=1.0 / GDV, bias=epsc[:]
                                     ).then_inc(slots.free[s], 1)
                act.drain()
                act.sem_inc(oroot, 1)

        @block.vector
        def _(dve):
            slots.credit(dve)
            nc.vector.memset(epsc[:], EPS)
            dve.drain()
            dve.sem_inc(head_free, 1)
            dve.wait_ge(small, 32)
            with dve.Fori(0, GH) as i:
                def result(key):
                    slots.wait(dve, key, i)
                    return ps[:, slots.slot(key)], slots.free[slots.slot(key)]

                dve.wait_ge(head_free, i + 1)
                nc.vector.tensor_copy(st[:].rearrange("p k c (d o) -> p (k c d) o", o=1),
                                      stats[:].rearrange("p k c (d h) -> p (k c d) h", h=GH)[:, :, bass.ds(i, 1)])
                nc.vector.tensor_copy(convw[:], convw_all[:, bass.ds(i, 1)].rearrange("p o t n -> p (o t) n"))
                dve.drain()
                dve.sem_inc(stat_ready, 1)
                for t in range(GCONV):
                    dve.wait_ge(centre, GCONV * i + t + 1)
                    s = slots.slot(("proj", t))
                    conv_taps(nc, tap[:, t % 2], ps[:, s], convw[:, t, 0:1], convw[:, t, 2:3]
                              ).then_inc(slots.free[s], 1)
                    dve.drain()
                    dve.sem_inc(tapped, 1)
                dve.wait_ge(rooted, i + 1)
                nc.vector.reciprocal(root[:, 0:2], root[:, 0:2])
                dve.drain()
                nc.vector.scalar_tensor_tensor(q, q, float(GDK) ** -0.5, root[:, 0], ALU.mult, ALU.mult)
                nc.vector.tensor_tensor(kf, kf, root[:, 1], ALU.mult)
                dve.drain()
                dve.sem_inc(unit, 1)
                src, free = result("kk")
                nc.vector.tensor_copy(kk[:], src[:, 0:T]).then_inc(free, 1)
                src, free = result("qk")
                nc.vector.tensor_copy(qk[:], src[:, 0:T]).then_inc(free, 1)
                for dr in range(2):
                    src, _ = result(("g", dr))
                    for c in range(NC):
                        gc = st[:, GC, c, dr:dr + 1]
                        nc.vector.scalar_tensor_tensor(ba[:, dr, cs(c)], src[:, cs(c)], gc, k.c(NEGS[dr][0]),
                                                       ALU.subtract, ALU.subtract)
                        nc.vector.scalar_tensor_tensor(aqk[:, dr, cs(c)], src[:, cs(c)], gc, k.c(NEGS[dr][1]),
                                                       ALU.subtract, ALU.add)
                    dve.drain()
                    dve.sem_inc(diff, 1)

                def next_level(n, dr):
                    nc.vector.tensor_tensor(level[:, dr].rearrange("p (c j) -> p c j", j=P),
                                            ba[:, dr].rearrange("p (c j) -> p c j", j=P),
                                            bcast(masks[:, dr, n], 1, [P, NC, P]), ALU.mult)
                    dve.drain()
                    dve.sem_inc(level_ready[dr], 1)

                for dr in range(2):
                    dve.wait_ge(decays, 2 * i + dr + 1)
                    for c in range(NC):
                        nc.vector.scalar_tensor_tensor(ba[:, dr, cs(c)], kk[:, cs(c)], st[:, GB, c, dr:dr + 1],
                                                       ba[:, dr, cs(c)], ALU.mult, ALU.mult)
                    dve.drain()
                    next_level(0, dr)
                nc.vector.tensor_tensor(aqk[:], aqk[:], bcast(qk[:], 1, [P, 2, T]), ALU.mult)
                nc.vector.tensor_tensor(qg[:], qg[:], bcast(q, 1, [P, 2, T]), ALU.mult)
                dve.drain()
                dve.sem_inc(aqk_ready, 1)
                eye = bcast(k.c("ident"), 1, [P, NC, P])
                for n in range(LEVELS):
                    for dr in range(2):
                        src, free = result(("xt", n, dr))
                        if n == 0:
                            nc.vector.tensor_tensor(xt[:, dr].rearrange("p (c j) -> p c j", j=P), eye,
                                                    src[:, 0:T].rearrange("p (c j) -> p c j", j=P), ALU.subtract
                                                    ).then_inc(free, 1)
                            nc.vector.tensor_tensor(xi[:, dr].rearrange("p (c j) -> p c j", j=P), eye,
                                                    level[:, dr].rearrange("p (c j) -> p c j", j=P), ALU.subtract)
                        else:
                            nc.vector.tensor_tensor(xt[:, dr], xt[:, dr], src[:, 0:T], ALU.subtract
                                                    ).then_inc(free, 1)
                            if n < LEVELS - 1:
                                src, free = result(("xi", n, dr))
                                nc.vector.tensor_tensor(xi[:, dr], xi[:, dr], src[:, 0:T], ALU.subtract
                                                        ).then_inc(free, 1)
                        dve.drain()
                        dve.sem_inc(x_ready[dr], 1)
                        if n + 1 < LEVELS:
                            next_level(n + 1, dr)
                dve.wait_ge(turned, i + 1)
                dve.wait_ge(init_loaded, 32 * (i + 1))
                dve.wait_ge(ctx_stored, 32 * i + 32)
                for m in range(NS):
                    pair = steps[2 * m:2 * m + 2]
                    for dr, c in pair:
                        nc.vector.tensor_scalar(kg[:, dr], tok[:, c, 0:P], st[:, GKW, c, dr:dr + 1], None, ALU.mult)
                        nc.vector.tensor_scalar(rhs[:, dr], tok[:, c, P:], st[:, GB, c, dr:dr + 1], None, ALU.mult)
                    dve.drain()
                    for dr, c in pair:
                        if c != CTXC:
                            src, free = result(("ks", dr, c))
                            nc.vector.scalar_tensor_tensor(rhs[:, dr], src[:, 0:GDV], st[:, GNBE, c, dr:dr + 1],
                                                           rhs[:, dr], ALU.mult, ALU.add).then_inc(free, 1)
                            dve.drain()
                        dve.sem_inc(rhs_ready[dr], 1)
                    for dr, c in pair:
                        src, free = result(("vn", dr, c))
                        nc.vector.tensor_copy(vn[:, dr, c], src[:, 0:GDV]).then_inc(free, 1)
                        dve.drain()
                        dve.sem_inc(vn_ready[dr], 1)
                    for dr, c in pair:
                        if c == last_of[dr]:
                            continue
                        src, free = result(("kv", dr, c))
                        if c == CTXC:
                            nc.vector.tensor_copy(ctx_state[:, dr], src[:, 0:GDV]).then_inc(free, 1)
                        else:
                            nc.vector.scalar_tensor_tensor(state[:, dr, c + 1 if dr == FWD else c - 1],
                                                           state[:, dr, c], st[:, GDEC, c, dr:dr + 1],
                                                           src[:, 0:GDV], ALU.mult, ALU.add).then_inc(free, 1)
                        dve.drain()
                        dve.sem_inc(state_ready[dr], 1)
                dve.wait_ge(oroot, i + 1)
                dve.wait_ge(gated, i + 1)
                nc.vector.reciprocal(root[:, 0], root[:, 0])
                dve.drain()
                for v in range(GVT):
                    src, free = result(("o", v))
                    nc.vector.scalar_tensor_tensor(root[:, 1], root[:, 0], gain[:, v:v + 1], src[:, 0:T],
                                                   ALU.mult, ALU.mult).then_inc(free, 1)
                    dve.drain()
                    nc.vector.tensor_tensor(y[:, bass.ds(GVT * i + v, 1)].rearrange("p o t -> p (o t)"),
                                            root[:, 1], z[:, v], ALU.mult)
                    dve.drain()
                dve.sem_inc(head_free, 1)


def gdn_mixer(k):
    nc = k.nc
    with ExitStack() as ctx:
        y = ctx.enter_context(nc.sbuf_tensor("gdn_y", [P, GH * GVT, T], F32))
        stats = ctx.enter_context(nc.sbuf_tensor("gdn_stats_all", [P, 6, NC, 2 * GH], F32))
        gain = ctx.enter_context(nc.sbuf_tensor("gdn_gain", [P, GVT], F32))
        with ExitStack() as inner:
            _, sem = k.stage(inner, "gdn_gain")
            got = sem("loaded")
            block = inner.enter_context(nc.Block())

            @block.sync
            def _(sp):
                sp.dma_start(gain[:], k.dram["gdn_norm"]).then_inc(got, 16)
                sp.wait_ge(got, 16)

        gdn_steps_phase(k, stats)
        gdn_heads_phase(k, stats, y, gain)
        out_projection_phase(k, "gdn_out", k.dram["gdn_w_out"], y, GH * GVT, 1)



HALF = P // 2
NHALF = T // HALF
TG = 8


def top16(nc, dve, values, spare, best, index):
    for c in range(NC):
        nc.vector.max(best[:, c, 0:8], values[:, c])
    dve.drain()
    for c in range(NC):
        nc.vector.match_replace(spare[:, c], best[:, c, 0:8], values[:, c], 4 * NEG)
        nc.vector.max_index(index[:, c, 0:8], best[:, c, 0:8], values[:, c])
    dve.drain()
    for c in range(NC):
        nc.vector.max(best[:, c, 8:16], spare[:, c])
    dve.drain()
    for c in range(NC):
        nc.vector.max_index(index[:, c, 8:16], best[:, c, 8:16], spare[:, c])
    dve.drain()


def peer_retrieval_phase(k, layer, picks):
    nc, d = k.nc, k.dram
    order = [(("proj", s), s) for s in range(2)] + [(("score", s), 2 + s) for s in range(2)]
    K2 = TOPK * TOPK
    with ExitStack() as ctx:
        sb, sem = k.stage(ctx, f"top{layer}")
        slots = Slots(sem, order)
        w, keys = sb("w", [P, 2, KT, P]), sb("keys", [P, 2, NK])
        q = sb("q", [P, 2, T])
        score, spare = sb("score", [P, 2, NC, NK]), sb("spare", [P, NC, K2])
        best, index = sb("best", [P, 2, NC, TOPK]), sb("index", [P, 2, NC, TOPK], U32)
        comb = sb("comb", [P, NC, K2])
        cv, ci = sb("cv", [P, NC, TOPK]), sb("ci", [P, NC, TOPK], U32)
        place = sb("place", [P, 2, NC, TOPK], U32)
        placef, indexf = sb("placef", [P, 2, NC, TOPK]), sb("indexf", [P, 2, NC, TOPK])
        hit = sb("hit", [P, NC * TOPK, TOPK])
        out = sb("out", [P, 3, NC, TOPK])
        total = sb("total", [P, NC])
        w_loaded, k_loaded = [sem(f"w{s}_loaded") for s in range(2)], [sem(f"keys{s}_loaded") for s in range(2)]
        w_free, q_ready, score_ready, score_free = sem("w_free"), sem("q_ready"), sem("score_ready"), sem("score_free")
        seen, centred, powered = sem("scores_seen"), sem("centred"), sem("exp_ready")
        ps = k.ps
        block = ctx.enter_context(nc.Block())

        @block.sync
        def _(sp):
            with sp.Fori(0, PH) as i:
                for s in range(2):
                    sp.wait_ge(w_free, 2 * i + s + 1)
                    sp.dma_start(w[:, s], d[f"peer_w_q{layer}"][bass.ds(2 * i + s, 1)]
                                 .rearrange("o p k n -> p (o k) n")).then_inc(w_loaded[s], 16)
                    sp.dma_start(keys[:, s], d[f"peer_keys{layer}"][bass.ds(2 * i + s, 1)]
                                 .rearrange("o p n -> p (o n)")).then_inc(k_loaded[s], 16)

        @block.tensor
        def _(pe):
            pe.sem_inc(w_free, 2)
            with pe.Fori(0, PH) as i:
                for s in range(2):
                    pe.wait_ge(w_loaded[s], 16 * (i + 1))
                    slots.claim(pe, ("proj", s), i)
                    for kt in range(KT):
                        last = both(nc, ps[:, s], w[:, s, kt], k.h[:, kt], kt == 0, kt == KT - 1)
                    last.then_inc(slots.ready[s], 1)
                for s in range(2):
                    pe.wait_ge(k_loaded[s], 16 * (i + 1))
                    pe.wait_ge(q_ready, 2 * i + s + 1)
                    slots.claim(pe, ("score", s), i)
                    for c in range(NC):
                        last = nc.tensor.matmul(ps[:, 2 + s, c * NK:(c + 1) * NK], q[:, s, c * P:(c + 1) * P],
                                                keys[:, s], start=True, stop=True)
                    last.then_inc(slots.ready[2 + s], 1)
                    slots.wait(pe, ("score", s), i)
                    pe.sem_inc(w_free, 1)

        @block.scalar
        def _(act):
            act.sem_inc(slots.free[0], 1)
            act.sem_inc(slots.free[1], 1)
            act.sem_inc(slots.free[2], 1)
            act.sem_inc(slots.free[3], 1)
            with act.Fori(0, PH) as i:
                for s in range(2):
                    slots.wait(act, ("proj", s), i)
                    nc.scalar.copy(q[:, s], ps[:, s, 0:T]).then_inc(slots.free[s], 1)
                    act.drain()
                    act.sem_inc(q_ready, 1)
                for s in range(2):
                    slots.wait(act, ("score", s), i)
                    act.wait_ge(score_free, 2 * i + s + 1)
                    nc.scalar.copy(score[:, s].rearrange("p c n -> p (c n)"), ps[:, 2 + s, 0:T]
                                   ).then_inc(slots.free[2 + s], 1)
                    act.drain()
                    act.sem_inc(score_ready, 1)
                act.wait_ge(centred, i + 1)
                nc.scalar.activation(out[:, 2], out[:, 2], ACT.Exp).then_inc(powered, 1)

        @block.vector
        def _(dve):
            dve.sem_inc(score_free, 2)
            with dve.Fori(0, PH) as i:
                for s in range(2):
                    dve.wait_ge(score_ready, 2 * i + s + 1)
                    dve.sem_inc(seen, 1)
                    top16(nc, dve, score[:, s], spare[:, :, 0:NK], best[:, s], index[:, s])
                    dve.sem_inc(score_free, 1)
                c4 = comb[:].rearrange("p c (a b) -> p c a b", b=TOPK)
                nc.vector.tensor_tensor(c4, bcast(best[:, 0], 3, [P, NC, TOPK, TOPK]),
                                        bcast(best[:, 1], 2, [P, NC, TOPK, TOPK]), ALU.add)
                nc.vector.tensor_copy(indexf[:], index[:])
                dve.drain()
                top16(nc, dve, comb[:], spare[:], cv[:], ci[:])
                nc.vector.tensor_scalar(place[:, 0], ci[:], 4, None, ALU.logical_shift_right)
                nc.vector.tensor_scalar(place[:, 1], ci[:], TOPK - 1, None, ALU.bitwise_and)
                nc.vector.tensor_tensor(out[:, 2], cv[:], cv[:, :, 0:1].to_broadcast([P, NC, TOPK]), ALU.subtract
                                        ).then_inc(centred, 1)
                dve.drain()
                nc.vector.tensor_copy(placef[:], place[:])
                dve.drain()
                for s in range(2):
                    nc.vector.tensor_tensor(hit[:], bcast(placef[:, s].rearrange("p c r -> p (c r)"), 2,
                                                          [P, NC * TOPK, TOPK]),
                                            bcast(k.c("iota")[:, 0:TOPK], 1, [P, NC * TOPK, TOPK]), ALU.is_equal)
                    dve.drain()
                    h4 = hit[:].rearrange("p (c r) a -> p c r a", c=NC)
                    nc.vector.tensor_tensor(h4, h4, bcast(indexf[:, s], 2, [P, NC, TOPK, TOPK]), ALU.mult)
                    dve.drain()
                    nc.vector.tensor_reduce(out[:, s].rearrange("p c r -> p (c r)"), hit[:], AX.X, ALU.add)
                    dve.drain()
                dve.wait_ge(powered, i + 1)
                nc.vector.tensor_reduce(total[:], out[:, 2], AX.X, ALU.add)
                dve.drain()
                nc.vector.reciprocal(total[:], total[:])
                dve.drain()
                nc.vector.tensor_tensor(out[:, 2], out[:, 2], bcast(total[:], 2, [P, NC, TOPK]), ALU.mult)
                dve.drain()
                for n in range(3):
                    nc.vector.tensor_copy(picks[:, :, n, bass.ts(i, TOPK)], out[:, n])
                dve.drain()


def peer_gates_phase(k, layer, picks, gates):
    nc = k.nc
    with ExitStack() as ctx:
        sb, sem = k.stage(ctx, f"gate{layer}")
        turned = sb("turned", [P, 3, T])
        now = sb("now", [P, 3, 2 * TG])
        first, second = sb("first", [P, 2, TG, NK]), sb("second", [P, 2, TG, NK])
        stage = sb("stage", [P, 2, NK, HALF])
        turn_made, turn_taken = sem("turn_ready"), sem("turn_taken")
        hot, used = [sem(f"one_hot{j}_ready") for j in range(2)], [sem(f"product{j}_ready") for j in range(2)]
        hot_free, ps_free = [sem(f"one_hot{j}_free") for j in range(2)], [sem(f"product{j}_taken") for j in range(2)]
        staged, stored = [sem(f"staged{b}") for b in range(2)], [sem(f"stored{b}") for b in range(2)]
        ps = k.ps
        PER = HALF // (2 * TG)
        block = ctx.enter_context(nc.Block())

        @block.sync
        def _(sp):
            for b in range(2):
                sp.sem_inc(stored[b], 16)
            with sp.Fori(0, NC) as c:
                for b in range(2):
                    sp.wait_ge(staged[b], 2 * PER * (c + 1))
                    sp.dma_start(gates[bass.ds(2 * c + b, 1)].rearrange("o p k t -> p (o k) t"), stage[:, b]
                                 ).then_inc(stored[b], 16)
            for b in range(2):
                sp.wait_ge(stored[b], 16 * (NC + 1))

        @block.tensor
        def _(pe):
            for c in range(NC):
                if c >= 2:
                    pe.wait_ge(turn_taken, c - 1)
                for n in range(3):
                    last = nc.tensor.transpose(ps[:, 2 + c % 2, n * P:(n + 1) * P], picks[:, c, n], k.c("ident"))
                last.then_inc(turn_made, 1)
            with pe.Fori(0, NC) as c:
                for b in range(2):
                    with pe.Fori(0, PER) as g:
                        n = (2 * c + b) * PER + g
                        for j in range(2):
                            pe.wait_ge(hot[j], n + 1)
                            pe.wait_ge(ps_free[j], n + 1)
                            for u in range(TG):
                                last = nc.tensor.matmul(ps[:, j, u * NK:(u + 1) * NK], second[:, j, u],
                                                        first[:, j, u], start=True, stop=True)
                            last.then_inc(used[j], 1)

        @block.scalar
        def _(act):
            for j in range(2):
                act.sem_inc(ps_free[j], 1)
            with act.Fori(0, NC) as c:
                for b in range(2):
                    act.wait_ge(stored[b], 16 * (c + 1))
                    with act.Fori(0, PER) as g:
                        n = (2 * c + b) * PER + g
                        for j in range(2):
                            act.wait_ge(used[j], n + 2)
                            nc.scalar.copy(stage[:, b].rearrange("p k t -> p t k")[:, bass.ds(2 * TG * g + TG * j, TG)],
                                           ps[:, j].rearrange("p (t k) -> p t k", k=NK)).then_inc(ps_free[j], 1)
                            act.drain()
                            act.sem_inc(staged[b], 1)

        @block.vector
        def _(dve):
            for c in range(NC):
                dve.wait_ge(turn_made, c + 1)
                nc.vector.tensor_copy(turned[:, :, c * P:(c + 1) * P],
                                      ps[:, 2 + c % 2, 0:3 * P].rearrange("p (n t) -> p n t", n=3)
                                      ).then_inc(turn_taken, 1)
            dve.drain()
            for j in range(2):
                dve.sem_inc(used[j], 1)
            with dve.Fori(0, NC) as c:
                for b in range(2):
                    with dve.Fori(0, PER) as g:
                        n = (2 * c + b) * PER + g
                        nc.vector.tensor_copy(now[:], turned[:, :, bass.ds(2 * TG * n, 2 * TG)])
                        dve.drain()
                        for j in range(2):
                            dve.wait_ge(used[j], n + 1)
                            for u in range(TG):
                                at = j * TG + u
                                nc.vector.tensor_scalar(first[:, j, u], k.c("iota"), now[:, 0, at:at + 1],
                                                        now[:, 2, at:at + 1], ALU.is_equal, ALU.mult)
                                nc.vector.tensor_scalar(second[:, j, u], k.c("iota"), now[:, 1, at:at + 1], None,
                                                        ALU.is_equal)
                            dve.drain()
                            dve.sem_inc(hot[j], 1)


def peer_experts_phase(k, layer, gates):
    nc, d = k.nc, k.dram
    u_dram, v_dram = d[f"peer_u{layer}"], d[f"peer_v{layer}"]
    g_dram = gates.rearrange("n p (b e) t -> b p n e t", e=EB)
    with ExitStack() as ctx:
        sb, sem = k.stage(ctx, f"dense{layer}")
        u, v = sb("u", [P, 2, EB, KT, P]), sb("v", [P, 2, EB, D])
        g = sb("g", [P, 2, NHALF, EB, HALF])
        a = sb("a", [P, 2, EB, T])
        u_loaded, v_loaded, g_loaded = ([sem(f"{n}{b}_loaded") for b in range(2)] for n in "uvg")
        s_ready, s_free = [sem(f"s{j}_ready") for j in range(2)], [sem(f"s{j}_free") for j in range(2)]
        o_ready, o_free = [sem(f"o{j}_ready") for j in range(2)], [sem(f"o{j}_free") for j in range(2)]
        activated, gated = sem("activated"), sem("gated")
        ps = k.ps
        S_PER, O_PER = EB // 2, KT // 2
        block = ctx.enter_context(nc.Block())

        @block.sync
        def _(sp):
            with sp.Fori(0, NB // 2) as i:
                for b in range(2):
                    n = 2 * i + b
                    sp.wait_ge(s_ready[1], S_PER * (n + 1))
                    sp.dma_start(u[:, b], u_dram[bass.ds(n, 1)].rearrange("o p e k n -> p (o e) k n")
                                 ).then_inc(u_loaded[b], 16)
                    sp.wait_ge(gated, EB * (n + 1))
                    sp.dma_start(g[:, b].rearrange("p n e t -> p n (e t)"),
                                 g_dram[bass.ds(n, 1)].rearrange("o p n e t -> p (o n) (e t)")
                                 ).then_inc(g_loaded[b], 16)
                    sp.wait_ge(o_ready[1], O_PER * (n + 1))
                    sp.dma_start(v[:, b], v_dram[bass.ds(n, 1)].rearrange("o p e n -> p (o e) n")
                                 ).then_inc(v_loaded[b], 16)

        @block.tensor
        def _(pe):
            pe.sem_inc(s_ready[0], 2 * S_PER)
            pe.sem_inc(s_ready[1], 2 * S_PER)
            pe.sem_inc(o_ready[0], 2 * O_PER)
            pe.sem_inc(o_ready[1], 2 * O_PER)

            def score(n, b, i):
                pe.wait_ge(u_loaded[b], 16 * (i + 1))
                for e in range(EB):
                    pe.wait_ge(s_free[e % 2], S_PER * n + e // 2 + 1)
                    for kt in range(KT):
                        last = both(nc, ps[:, e % 2], u[:, b, e, kt], k.h[:, kt], kt == 0, kt == KT - 1)
                    last.then_inc(s_ready[e % 2], 1)

            def output(n, b, i):
                pe.wait_ge(v_loaded[b], 16 * (i + 1))
                pe.wait_ge(gated, EB * (n + 3))
                for t in range(KT):
                    pe.wait_ge(o_free[t % 2], O_PER * n + t // 2 + 1)
                    for e in range(EB):
                        last = both(nc, ps[:, 2 + t % 2], v[:, b, e, t * P:(t + 1) * P], a[:, b, e],
                                    e == 0, e == EB - 1)
                    last.then_inc(o_ready[t % 2], 1)

            score(0, 0, 0)
            with pe.Fori(0, NB // 2 - 1) as i:
                score(2 * i + 1, 1, i)
                output(2 * i, 0, i)
                score(2 * i + 2, 0, i + 1)
                output(2 * i + 1, 1, i)
            i = NB // 2 - 1
            score(2 * i + 1, 1, i)
            output(2 * i, 0, i)
            output(2 * i + 1, 1, i)

        @block.scalar
        def _(act):
            for j in range(2):
                act.sem_inc(s_free[j], 1)
            with act.Fori(0, NB // 2) as i:
                for b in range(2):
                    n = 2 * i + b
                    act.wait_ge(o_ready[1], O_PER * (n + 1))
                    for e in range(EB):
                        act.wait_ge(s_ready[e % 2], S_PER * (n + 2) + e // 2 + 1)
                        nc.scalar.activation(a[:, b, e], ps[:, e % 2, 0:T], ACT.Gelu).then_inc(s_free[e % 2], 1)
                        act.drain()
                        act.sem_inc(activated, 1)

        @block.vector
        def _(dve):
            dve.sem_inc(gated, 2 * EB)
            for j in range(2):
                dve.sem_inc(o_free[j], 1)

            def gate(n, b, i):
                dve.wait_ge(g_loaded[b], 16 * (i + 1))
                for e in range(EB):
                    dve.wait_ge(activated, EB * n + e + 1)
                    ae = a[:, b, e].rearrange("p (n t) -> p n t", t=HALF)
                    nc.vector.tensor_tensor(ae, ae, g[:, b, :, e], ALU.mult).then_inc(gated, 1)

            def add(n):
                for t in range(KT):
                    dve.wait_ge(o_ready[t % 2], O_PER * (n + 2) + t // 2 + 1)
                    for s, (lo, hi) in enumerate(SEG):
                        x = k.x[:, t, lo:hi]
                        last = nc.vector.scalar_tensor_tensor(x, ps[:, 2 + t % 2, lo:hi],
                                                              k.mod[:, layer, 5, t, s:s + 1], x, ALU.mult, ALU.add)
                    last.then_inc(o_free[t % 2], 1)

            gate(0, 0, 0)
            with dve.Fori(0, NB // 2 - 1) as i:
                gate(2 * i + 1, 1, i)
                add(2 * i)
                gate(2 * i + 2, 0, i + 1)
                add(2 * i + 1)
            i = NB // 2 - 1
            gate(2 * i + 1, 1, i)
            add(2 * i)
            add(2 * i + 1)


def peer_mixer(k, layer):
    nc = k.nc
    gates = nc.dram_tensor(f"gate_matrix{layer}", (NHALF, P, NK, HALF), F32, kind="Internal").ap()
    with ExitStack() as ctx:
        picks = ctx.enter_context(nc.sbuf_tensor(f"picks{layer}", [P, NC, 3, P], F32))
        peer_retrieval_phase(k, layer, picks)
        peer_gates_phase(k, layer, picks, gates)
    peer_experts_phase(k, layer, gates)



def build(nc, dram):
    with ExitStack() as ctx:
        k = Core(nc, ctx, dram)
        load_phase(k)
        modulation_phase(k)
        for layer, mixer in enumerate((ssd_mixer, gdn_mixer)):
            adaln_phase(k, layer, 0)
            mixer(k)
            adaln_phase(k, layer, 1)
            peer_mixer(k, layer)
        final_phase(k)


def grid_positions():
    width, quarter = 64, D // 4
    omega = (1.0 / (np.float32(10000.0) ** (np.arange(quarter, dtype=np.float32) / quarter))).astype(np.float32)

    def enc(p):
        ang = p.astype(np.float32)[:, None] * omega[None, :]
        return np.concatenate([np.sin(ang), np.cos(ang)], -1)

    t = np.arange(LAT)
    return np.concatenate([enc(t // width), enc(t % width)], -1).astype(np.float32)


def features_first(a):
    n, f = a.shape
    return np.ascontiguousarray(a.reshape(n, f // P, P).transpose(2, 1, 0))


def weight_tiles(w, columns=None):
    if columns is not None:
        w = w[:, columns]
    kk, n = w.shape
    return np.ascontiguousarray(w.reshape(kk // P, P, n // P, P).transpose(2, 1, 0, 3))


def lay_out(a):
    a = {n: np.asarray(v) for n, v in a.items()}
    out = {"consts": constants(), "levels": level_masks(), "pos": features_first(grid_positions())}
    out["x"] = features_first(np.concatenate([a["x_sample"][0], a["x_prompt"][0]], 0))
    out["cond"] = features_first(np.stack([a["c"][0], a["c_ctx"]], 0))
    out["b_mod"] = np.repeat(a["b_mod"].reshape(DEPTH * 6 * KT, P).T[:, :, None], 2, 2)
    w = a["w_mod"].reshape(DEPTH, KT, P, 6 * KT // 4, 4 * P)
    out["w_mod"] = w.transpose(0, 3, 2, 1, 4).reshape(DEPTH * 6 * KT // 4, P, KT, 4 * P)
    gains = np.concatenate([a["norm_mix_g"], a["norm_ffn_g"], a["final_norm_g"][None]], 0)
    out["gains"] = np.repeat(gains.reshape(2 * DEPTH + 1, KT, P).transpose(2, 0, 1)[..., None], 2, 3)

    z0, x0, b0 = 0, SINNER, 2 * SINNER
    c0, dt0 = b0 + SG * SN, b0 + 2 * SG * SN
    xw = SXT * P
    cols, conv_cols = [], []
    for g in range(SG):
        conv = np.concatenate([np.arange(x0 + g * xw, x0 + (g + 1) * xw), np.arange(b0 + g * SN, b0 + (g + 1) * SN),
                               np.arange(c0 + g * SN, c0 + (g + 1) * SN)])
        conv_cols.append(conv - x0)
        cols += [conv, np.arange(z0 + g * xw, z0 + (g + 1) * xw)]
    w_in = a["ssd_w_in"][0]
    out["ssd_w_in"] = weight_tiles(w_in, np.concatenate(cols))
    out["ssd_w_dt"] = w_in[:, dt0:].reshape(KT, P, 2 * SH).transpose(1, 0, 2)
    conv = np.concatenate([a["ssd_conv_w"][0], a["ssd_conv_b"]], 0)[:, np.concatenate(conv_cols)]
    out["ssd_conv"] = conv.reshape(4, SG, SCONV, P).transpose(3, 1, 2, 0)
    out["ssd_skip"] = np.repeat(a["ssd_d"][0], SP_).reshape(SG, SXT, P).transpose(2, 0, 1)
    out["ssd_dt_bias"] = np.broadcast_to(a["ssd_dt_bias"].reshape(1, 2 * SH), (P, 2 * SH))
    out["ssd_a_log"] = np.broadcast_to(a["ssd_a_log"].reshape(1, 2 * SH), (P, 2 * SH))
    st = np.stack([a["state_ssd_fwd"][0, 0], a["state_ssd_bwd"][0, 0]], 0).reshape(2, SG, xw, SN)
    out["ssd_state"] = st.transpose(1, 0, 3, 2).reshape(SG * 2, SN, xw)
    out["ssd_norm"] = a["ssd_norm_g"].reshape(SINNER // P, P).T
    out["ssd_w_out"] = weight_tiles(a["ssd_w_out"][0])

    cols, conv_cols = [], []
    q0, k0, v0, z0 = 0, GH * GDK, 2 * GH * GDK, 2 * GH * GDK + GH * GDV
    ab0 = z0 + GH * GDV
    for h in range(GH):
        conv = np.concatenate([np.arange(q0 + h * GDK, q0 + (h + 1) * GDK), np.arange(k0 + h * GDK, k0 + (h + 1) * GDK),
                               np.arange(v0 + h * GDV, v0 + (h + 1) * GDV)])
        conv_cols.append(conv)
        cols += [conv, np.arange(z0 + h * GDV, z0 + (h + 1) * GDV)]
    w_in = a["gdn_w_in"][0]
    out["gdn_w_in"] = weight_tiles(w_in, np.concatenate(cols))
    out["gdn_w_ab"] = w_in[:, ab0:].reshape(KT, P, 4 * GH).transpose(1, 0, 2)
    conv = a["gdn_conv_w"][0][:, np.concatenate(conv_cols)]
    out["gdn_conv"] = conv.reshape(3, GH, GCONV, P).transpose(3, 1, 2, 0)
    out["gdn_dt_bias"] = np.broadcast_to(a["gdn_dt_bias"].reshape(1, 2 * GH), (P, 2 * GH))
    out["gdn_a_log"] = np.broadcast_to(a["gdn_a_log"].reshape(1, 2 * GH), (P, 2 * GH))
    st = np.stack([a["state_gdn_fwd"][0, 0], a["state_gdn_bwd"][0, 0]], 1)
    out["gdn_state"] = st.reshape(GH * 2, GDK, GDV)
    out["gdn_norm"] = a["gdn_norm_g"].reshape(GVT, P).T
    out["gdn_w_out"] = weight_tiles(a["gdn_w_out"][0])

    for l in range(DEPTH):
        out[f"peer_w_q{l}"] = weight_tiles(a["peer_w_q"][l])
        out[f"peer_keys{l}"] = a["peer_keys"][l].transpose(1, 0, 3, 2).reshape(2 * PH, PHALF, NK)
        out[f"peer_u{l}"] = a["peer_u"][l].reshape(NB, EB, P, KT, P).transpose(0, 4, 1, 3, 2)
        out[f"peer_v{l}"] = a["peer_v"][l].reshape(NB, EB, P, D).transpose(0, 2, 1, 3)
    return {n: np.ascontiguousarray(v) for n, v in out.items()}


def kernel(**inputs):
    import concourse.bacc as bacc
    from concourse.bass_utils import run_bass_kernel_spmd

    nc = bacc.Bacc("TRN2", target_bir_lowering=False, num_devices=1)
    arrays = lay_out(inputs)
    dram = {n: nc.dram_tensor(f"in_{n}", v.shape, mybir.dt.from_np(v.dtype), kind="ExternalInput").ap()
            for n, v in arrays.items()}
    outputs = {"y": (P, KT, T), "ssd_out": (2 * SG, SN, SXT * P), "gdn_out": (2 * GH, GDK, GDV)}
    for n, shape in outputs.items():
        dram[n] = nc.dram_tensor(f"out_{n}", shape, F32, kind="ExternalOutput").ap()
    build(nc, dram)
    got = run_bass_kernel_spmd(nc, [{f"in_{n}": v for n, v in arrays.items()}], core_ids=[0]).results[0]
    y = got["out_y"].transpose(2, 1, 0).reshape(T, D)
    ssd = got["out_ssd_out"].reshape(SG, 2, SN, SR, SP_).transpose(1, 0, 3, 4, 2).reshape(2, 1, 1, SH, SP_, SN)
    gdn = got["out_gdn_out"].reshape(GH, 2, GDK, GDV).transpose(1, 0, 2, 3).reshape(2, 1, 1, GH, GDK, GDV)
    return (np.ascontiguousarray(y[None, LAT:]), np.ascontiguousarray(y[None, :LAT]),
            np.ascontiguousarray(ssd[0]), np.ascontiguousarray(ssd[1]),
            np.ascontiguousarray(gdn[0]), np.ascontiguousarray(gdn[1]))
```

```python
from contextlib import ExitStack

import concourse.bass as bass
import numpy as np
from concourse import mybir

ALU = mybir.AluOpType
ACT = mybir.ActivationFunctionType
AX = mybir.AxisListType
F32 = mybir.dt.float32
U32 = mybir.dt.uint32
F16 = mybir.dt.float16
F32R = mybir.dt.float32r

P = 128
D = 1024
KT = D // P
CTX, LAT = 128, 512
T = CTX + LAT
NC = T // P
SEG = ((0, LAT), (LAT, T))
CTXC = NC - 1
DEPTH = 2
EPS = 1e-6
NEG = -1.0e30
BANKED = T // 2
PIECES = ((0, 0, BANKED, 0), (0, BANKED, LAT, 512), (1, LAT, T, 512 + LAT - BANKED))
STARTS, ENDS = [lo for lo, _ in SEG], [hi for _, hi in SEG]
SLOT = 1024
NSLOT = 4

SG, SR, SP_, SN = 4, 8, 64, 128
SH = SG * SR
SXT = SR * SP_ // P
SCONV = SXT + 2
STILES = SCONV + SXT
SINNER = SH * SP_
GH, GDK, GDV = 8, 128, 256
GVT = GDV // P
GCONV = 2 + GVT
GTILES = GCONV + GVT
LEVELS = 7
PH, NK, TOPK, PHALF = 8, 128, 16, 128
NE = NK * NK
EB = 2
NB = NK // EB

CONSTS = ("ident", "ones", "tri_f", "tri_b", "neg_f", "neg_b", "sneg_f", "sneg_b", "iota")


def constants():
    r, c = np.arange(P)[:, None], np.arange(P)[None, :]
    out = {
        "ident": r == c,
        "ones": np.ones((P, P)),
        "tri_f": r <= c,
        "tri_b": r >= c,
        "neg_f": np.where(c >= r, 0.0, NEG),
        "neg_b": np.where(c <= r, 0.0, NEG),
        "sneg_f": np.where(c < r, 0.0, NEG),
        "sneg_b": np.where(c > r, 0.0, NEG),
        "iota": c + 0 * r,
    }
    return np.ascontiguousarray(np.stack([out[n] for n in CONSTS], 1).astype(np.float32))


def level_masks():
    r, c = np.arange(P)[:, None], np.arange(P)[None, :]
    low = [(r // s % 2 == 1) & (c // s == r // s - 1) for s in (1 << n for n in range(LEVELS))]
    return np.stack([np.stack(low, 1), np.stack([m.T for m in low], 1)], 1).astype(np.float32)


class Slots:

    def __init__(self, sem, order):
        self.ready = [sem(f"psum{s}_ready") for s in range(NSLOT)]
        self.free = [sem(f"psum{s}_free") for s in range(NSLOT)]
        self.per = [0] * NSLOT
        self.at = {}
        for key, slot in order:
            self.at[key] = (slot, self.per[slot])
            self.per[slot] += 1

    def slot(self, key):
        return self.at[key][0]

    def credit(self, engine):
        for s in range(NSLOT):
            if self.per[s]:
                engine.sem_inc(self.free[s], 1)

    def claim(self, pe, key, i=0):
        s, n = self.at[key]
        pe.wait_ge(self.free[s], i * self.per[s] + n + 1)

    def wait(self, engine, key, i=0):
        s, n = self.at[key]
        engine.wait_ge(self.ready[s], i * self.per[s] + n + 1)


class Core:

    def __init__(self, nc, ctx, dram):
        self.nc, self.dram = nc, dram

        def sb(name, shape, dtype=F32):
            return ctx.enter_context(nc.sbuf_tensor(name, shape, dtype))

        self.x = sb("residual", [P, KT, T])
        self.h = None
        self.const = sb("consts", [P, len(CONSTS), P])
        self.mod = sb("modulation", [P, DEPTH, 6, KT, 2])
        self.gains = sb("norm_gains", [P, 2 * DEPTH + 1, KT, 2])
        self.ps = ctx.enter_context(nc.psum_tensor("psum", [P, NSLOT, SLOT], F32))

    def hidden(self, ctx, name):
        self.h = ctx.enter_context(self.nc.sbuf_tensor(name, [P, KT, T], F32))

    def c(self, name):
        return self.const[:, CONSTS.index(name), :]

    def stage(self, ctx, name):
        nc = self.nc
        sems = []

        def clear():
            nc.clear_and_free_semaphores(sems)
            nc.all_engine_barrier()

        ctx.callback(clear)

        def sb(label, shape, dtype=F32):
            return ctx.enter_context(nc.sbuf_tensor(f"{name}_{label}", shape, dtype))

        def sem(label):
            sems.append(nc.alloc_semaphore(f"{name}_{label}"))
            return sems[-1]

        return sb, sem


def one(ap, i):
    return ap[:, bass.ds(i, 1)]


def both(nc, out, lhsT, rhs, start, stop):
    nc.tensor.matmul(out[:, 0:LAT], lhsT, rhs[:, 0:LAT], start=start, stop=stop)
    return nc.tensor.matmul(out[:, LAT:T], lhsT, rhs[:, LAT:T], start=start, stop=stop)


def banked(slot):
    return slot.rearrange("p (b t) -> p b t", b=2)[:, :, 0:BANKED]


def three_passes(nc, slot, w, x, start, stop):
    out = banked(slot)
    for n, (lhsT, rhs) in enumerate(((w[0], x[0]), (w[0], x[1]), (w[1], x[0]))):
        for b in range(2):
            last = nc.tensor.matmul(out[:, b], lhsT, rhs[:, b * BANKED:(b + 1) * BANKED],
                                    start=start and n == 0, stop=stop and n == 2)
    return last


def halves(ap):
    return ap.rearrange("p (b t) -> p b t", b=2)


def bcast(ap, axis, shape):
    return ap.unsqueeze(axis).to_broadcast(shape)



def load_phase(k):
    nc, d = k.nc, k.dram
    with ExitStack() as ctx:
        sb, sem = k.stage(ctx, "load")
        pos = sb("pos", [P, KT, LAT])
        loaded, added = sem("loaded"), sem("added")
        block = ctx.enter_context(nc.Block())

        @block.sync
        def _(sp):
            sp.dma_start(k.x[:], d["x"]).then_inc(loaded, 16)
            sp.dma_start(pos[:], d["pos"]).then_inc(loaded, 16)
            sp.dma_start(k.const[:], d["consts"]).then_inc(loaded, 16)
            sp.dma_start(k.gains[:], d["gains"]).then_inc(loaded, 16)

        @block.vector
        def _(dve):
            dve.wait_ge(loaded, 64)
            nc.vector.tensor_tensor(k.x[:, :, 0:LAT], k.x[:, :, 0:LAT], pos[:], ALU.add).then_inc(added, 1)
            dve.wait_ge(added, 1)


def modulation_phase(k):
    nc, d = k.nc, k.dram
    N = DEPTH * 6 * KT // 4
    TILES = DEPTH * 6 * KT
    with ExitStack() as ctx:
        sb, sem = k.stage(ctx, "mod")
        cond, silu = sb("cond", [P, KT, 2]), sb("silu", [P, KT, 2])
        bias = sb("bias", [P, TILES, 2])
        w = sb("w", [P, 2, KT, 4 * P])
        rows = sb("rows", [2, TILES * P])
        out = k.mod[:].rearrange("p l s k g -> p (l s k) g")
        small, activated = sem("small_loaded"), sem("silu_ready")
        w_loaded = [sem(f"w{b}_loaded") for b in range(2)]
        made, taken, turned = [sem(f"row{b}_ready") for b in range(2)], sem("rows_taken"), sem("turned")
        block = ctx.enter_context(nc.Block())

        @block.sync
        def _(sp):
            sp.dma_start(cond[:], d["cond"]).then_inc(small, 16)
            sp.dma_start(bias[:], d["b_mod"]).then_inc(small, 16)
            for b in range(2):
                sp.sem_inc(made[b], 1)
            with sp.Fori(0, N // 2) as i:
                for b in range(2):
                    sp.wait_ge(made[b], i + 1)
                    sp.dma_start(w[:, b], d["w_mod"][bass.ds(2 * i + b, 1)].rearrange("o p k n -> p (o k) n")
                                 ).then_inc(w_loaded[b], 16)

        @block.scalar
        def _(act):
            act.wait_ge(small, 32)
            nc.scalar.activation(silu[:], cond[:], ACT.Silu).then_inc(activated, 1)

        @block.tensor
        def _(pe):
            pe.wait_ge(activated, 1)
            with pe.Fori(0, N // 2) as i:
                for b in range(2):
                    pe.wait_ge(w_loaded[b], 16 * (i + 1))
                    pe.wait_ge(taken, 2 * i + b + 1)
                    for kt in range(KT):
                        last = nc.tensor.matmul(k.ps[0:2, b, 0:4 * P], silu[:, kt, :], w[:, b, kt],
                                                start=(kt == 0), stop=(kt == KT - 1))
                    last.then_inc(made[b], 1)
            pe.wait_ge(taken, N + 2)
            for t in range(TILES):
                last = nc.tensor.transpose(k.ps[:, 2, 2 * t:2 * t + 2], rows[:, t * P:(t + 1) * P],
                                           k.c("ident")[0:2, 0:2])
            last.then_inc(turned, 1)

        @block.vector
        def _(dve):
            dve.sem_inc(taken, 2)
            with dve.Fori(0, N // 2) as i:
                for b in range(2):
                    dve.wait_ge(made[b], i + 2)
                    nc.vector.tensor_copy(rows[:, bass.ds((2 * i + b) * 4 * P, 4 * P)], k.ps[0:2, b, 0:4 * P]
                                          ).then_inc(taken, 1)
            dve.wait_ge(small, 32)
            dve.wait_ge(turned, 1)
            nc.vector.tensor_tensor(out, k.ps[:, 2, 0:2 * TILES].rearrange("p (q g) -> p q g", g=2), bias[:], ALU.add)



def norm_phase(k, name, src, tiles, finish, out_dram=None):
    nc = k.nc
    with ExitStack() as ctx:
        sb, sem = k.stage(ctx, name)
        sq, rms, rstd = sb("squares", [P, 2, T]), sb("rms", [P, T]), sb("rstd", [P, T])
        epsc = sb("eps", [P, 1])
        squared, summed, rooted, normed, stored = (sem(s) for s in ("squared", "summed", "rooted", "normed", "stored"))
        eps_set = sem("eps_set")
        block = ctx.enter_context(nc.Block())
        out = k.ps[:, 0, 0:T]

        @block.scalar
        def _(act):
            for t in range(tiles):
                if t >= 2:
                    act.wait_ge(summed, t - 1)
                nc.scalar.activation(sq[:, t % 2], src[:, t], ACT.Square).then_inc(squared, 1)
            act.wait_ge(summed, tiles)
            act.wait_ge(eps_set, 1)
            nc.scalar.activation(rms[:], out, ACT.Sqrt, scale=1.0 / (tiles * P), bias=epsc[:]).then_inc(rooted, 1)

        @block.tensor
        def _(pe):
            for t in range(tiles):
                pe.wait_ge(squared, t + 1)
                both(nc, out, k.c("ones"), sq[:, t % 2], t == 0, t == tiles - 1).then_inc(summed, 1)

        @block.vector
        def _(dve):
            nc.vector.memset(epsc[:], EPS).then_inc(eps_set, 1)
            dve.wait_ge(rooted, 1)
            nc.vector.reciprocal(rstd[:], rms[:])
            dve.drain()
            finish(dve, rstd)
            dve.drain()
            dve.sem_inc(normed, 1)

        @block.sync
        def _(sp):
            sp.wait_ge(normed, 1)
            if out_dram is not None:
                sp.dma_start(out_dram, k.h[:]).then_inc(stored, 16)
                sp.wait_ge(stored, 16)


def split_weights(nc, dve, hi, lo, w):
    hi, lo, w = (ap.rearrange("p k n -> p (k n)") for ap in (hi, lo, w))
    nc.vector.tensor_copy(hi, w)
    dve.drain()
    return nc.vector.tensor_tensor(lo, w, hi.bitcast(F32), ALU.subtract)


def split(nc, engine, hi, lo, src):
    nc.vector.tensor_copy(hi, src)
    engine.drain()
    nc.vector.tensor_tensor(lo, src, hi.bitcast(F32), ALU.subtract)


def adaln_phase(k, layer, half, parts=None):
    nc = k.nc
    with ExitStack() as ctx:
        gain = ctx.enter_context(nc.sbuf_tensor(f"adaln_gain{layer}{half}", [P, KT, 2], F32))

        def finish(dve, rstd):
            nc.vector.scalar_tensor_tensor(gain[:], k.mod[:, layer, 3 * half + 1], 1.0, k.gains[:, 2 * half + layer],
                                           ALU.add, ALU.mult)
            for t in range(KT):
                nc.vector.tensor_tensor(k.h[:, t], k.x[:, t], rstd[:], ALU.mult)
            dve.drain()
            for t in range(KT):
                for g, (a, b) in enumerate(SEG):
                    nc.vector.tensor_scalar(k.h[:, t, a:b], k.h[:, t, a:b], gain[:, t, g:g + 1],
                                            k.mod[:, layer, 3 * half, t, g:g + 1], ALU.mult, ALU.add)
            if parts is not None:
                dve.drain()
                split(nc, dve, parts[0][:], parts[1][:], k.h[:])

        norm_phase(k, f"adaln{layer}{half}", k.x, KT, finish)


def final_phase(k):
    nc = k.nc

    def finish(dve, rstd):
        for t in range(KT):
            nc.vector.scalar_tensor_tensor(k.h[:, t], k.x[:, t], k.gains[:, 2 * DEPTH, t, 0:1], rstd[:],
                                           ALU.mult, ALU.mult)

    norm_phase(k, "final", k.x, KT, finish, out_dram=k.dram["y"])



def softplus_steps(nc, engine, which, v, e, u, l, done):
    if which == "act":
        nc.scalar.activation(e, v, ACT.Abs)
        engine.drain()
        nc.scalar.activation(e, e, ACT.Exp, scale=-1.0).then_inc(done, 1)
        engine.wait_ge(done, 2)
        nc.scalar.activation(l, u, ACT.Ln).then_inc(done, 1)
        return
    engine.wait_ge(done, 1)
    nc.vector.tensor_scalar(u, e, 1.0, None, ALU.add).then_inc(done, 1)
    engine.wait_ge(done, 3)
    nc.vector.tensor_scalar(u, u, 1.0, None, ALU.subtract)
    engine.drain()
    nc.vector.scalar_tensor_tensor(l, u, 0.0, l, ALU.is_equal, ALU.add)
    engine.drain()
    nc.vector.scalar_tensor_tensor(u, u, 0.0, u, ALU.is_equal, ALU.add)
    engine.drain()
    nc.vector.reciprocal(u, u)
    engine.drain()
    nc.vector.tensor_tensor(l, l, u, ALU.mult)
    engine.drain()
    nc.vector.tensor_tensor(l, l, e, ALU.mult)
    engine.drain()
    nc.vector.scalar_tensor_tensor(v, v, 0.0, l, ALU.max, ALU.add)
    engine.drain()


def conv_taps(nc, out, slot, w0, w2):
    def add(shift, w):
        for _, lo, hi, at in PIECES:
            a = lo + (shift < 0 and lo in STARTS)
            b = hi - (shift > 0 and hi in ENDS)
            to = out[:, a + shift:b + shift]
            last = nc.vector.scalar_tensor_tensor(to, slot[:, at + a - lo:at + b - lo], w, to, ALU.mult, ALU.add)
        return last

    add(1, w0)
    nc.vector.drain()
    return add(-1, w2)


def out_projection_phase(k, name, w_dram, src, tiles, layer):
    nc = k.nc
    with ExitStack() as ctx:
        sb, sem = k.stage(ctx, name)
        w = sb("w", [P, 2, tiles, P])
        whi, wlo = sb("w_hi", [P, 2, tiles, P], F32R), sb("w_lo", [P, 2, tiles, P], F32R)
        shi, slo = sb("src_hi", [P, tiles, T], F32R), sb("src_lo", [P, tiles, T], F32R)
        w_loaded = [sem(f"w{b}_loaded") for b in range(2)]
        w_hi_ready, w_split, src_hi_ready, src_split = (sem(s) for s in (
            "w_hi_ready", "w_split", "src_hi_ready", "src_split"))
        made, taken = sem("product_ready"), sem("product_taken")
        block = ctx.enter_context(nc.Block())

        @block.sync
        def _(sp):
            with sp.Fori(0, KT // 2) as i:
                for b in range(2):
                    sp.wait_ge(w_split, 2 * i + b + 1)
                    sp.dma_start(w[:, b], w_dram[bass.ds(2 * i + b, 1)].rearrange("o p k n -> p (o k) n")
                                 ).then_inc(w_loaded[b], 16)

        @block.tensor
        def _(pe):
            pe.sem_inc(made, 2)

            def product(n, b, first=False):
                pe.wait_ge(w_split, n + 3)
                pe.wait_ge(taken, n + 1)
                for t in range(tiles):
                    if first:
                        pe.wait_ge(src_split, t + 1)
                    last = three_passes(nc, k.ps[:, b], (whi[:, b, t], wlo[:, b, t]), (shi[:, t], slo[:, t]),
                                        t == 0, t == tiles - 1)
                last.then_inc(made, 1)

            product(0, 0, True)
            product(1, 1)
            with pe.Fori(0, KT // 2 - 1) as i:
                for b in range(2):
                    product(2 * i + 2 + b, b)

        @block.scalar
        def _(act):
            def high(n, b, i):
                act.wait_ge(w_loaded[b], 16 * (i + 1))
                act.wait_ge(made, n + 1)
                nc.scalar.copy(whi[:, b], w[:, b]).then_inc(w_hi_ready, 1)

            high(0, 0, 0)
            for t in range(tiles):
                nc.scalar.copy(shi[:, t], src[:, t]).then_inc(src_hi_ready, 1)
            high(1, 1, 0)
            with act.Fori(0, KT // 2 - 1) as i:
                for b in range(2):
                    high(2 * i + 2 + b, b, i + 1)

        @block.vector
        def _(dve):
            dve.sem_inc(taken, 2)
            dve.sem_inc(w_split, 2)

            def low(n, b):
                dve.wait_ge(w_hi_ready, n + 1)
                nc.vector.tensor_tensor(wlo[:, b], w[:, b], whi[:, b].bitcast(F32), ALU.subtract).then_inc(w_split, 1)

            def add(n, b):
                dve.wait_ge(made, n + 3)
                for g, lo, hi, at in PIECES:
                    x = k.x[:, bass.ds(n, 1), lo:hi].rearrange("p o t -> p (o t)")
                    gate = k.mod[:, layer, 2, bass.ds(n, 1), g]
                    last = nc.vector.scalar_tensor_tensor(x, k.ps[:, b, at:at + hi - lo], gate, x, ALU.mult, ALU.add)
                last.then_inc(taken, 1)

            low(0, 0)
            for t in range(tiles):
                dve.wait_ge(src_hi_ready, t + 1)
                nc.vector.tensor_tensor(slo[:, t], src[:, t], shi[:, t].bitcast(F32), ALU.subtract
                                        ).then_inc(src_split, 1)
            low(1, 1)
            with dve.Fori(0, KT // 2 - 1) as i:
                for b in range(2):
                    low(2 * i + 2 + b, b)
                    add(2 * i + b, b)
            for n in range(KT - 2, KT):
                add(n, n % 2)


def mixer_input(k, ctx, layer):
    return [ctx.enter_context(k.nc.sbuf_tensor(f"mixer_in{layer}_{n}", [P, KT, T], F32R)) for n in ("hi", "lo")]



SDT, SDTA, SACS, SW, SDEC = range(5)


def ssd_steps_phase(k, stats):
    nc, d = k.nc, k.dram
    H2 = 2 * SH
    with ExitStack() as ctx:
        sb, sem = k.stage(ctx, "ssd_dt")
        w, bias, alog = sb("w", [P, KT, H2]), sb("bias", [P, H2]), sb("alog", [P, H2])
        e, u, l = (sb(n, [P, NC * H2]) for n in ("e", "u", "l"))
        loaded, made, raw, steps, neg_a = (sem(s) for s in ("loaded", "product_ready", "raw", "softplus", "minus_a"))
        dta_ready, sums, weighed = sem("dta_ready"), sem("sums_ready"), sem("exponents")
        dt = stats[:, SDT].rearrange("p c h -> p (c h)")
        block = ctx.enter_context(nc.Block())
        sum_ps = k.ps[:, 1, 0:NC * H2].rearrange("p (c h) -> p c h", h=H2)
        tot_ps = k.ps[:, 2, 0:NC * H2].rearrange("p (c h) -> p c h", h=H2)

        @block.sync
        def _(sp):
            sp.dma_start(w[:], d["ssd_w_dt"]).then_inc(loaded, 16)
            sp.dma_start(bias[:], d["ssd_dt_bias"]).then_inc(loaded, 16)
            sp.dma_start(alog[:], d["ssd_a_log"]).then_inc(loaded, 16)

        @block.tensor
        def _(pe):
            pe.wait_ge(loaded, 48)
            for c in range(NC):
                for t in range(KT):
                    last = nc.tensor.matmul(k.ps[:, 0, c * H2:(c + 1) * H2], k.h[:, t, c * P:(c + 1) * P], w[:, t],
                                            start=(t == 0), stop=(t == KT - 1))
            last.then_inc(made, 1)
            pe.wait_ge(dta_ready, 1)
            for i, tri in enumerate(("tri_f", "tri_b")):
                for c in range(NC):
                    nc.tensor.matmul(sum_ps[:, c, i * SH:(i + 1) * SH], k.c(tri),
                                     stats[:, SDTA, c, i * SH:(i + 1) * SH], start=True, stop=True)
            nc.tensor.matmul(k.ps[:, 2, 0:NC * H2], k.c("ones"), stats[:, SDTA].rearrange("p c h -> p (c h)"),
                             start=True, stop=True).then_inc(sums, 1)

        @block.scalar
        def _(act):
            act.wait_ge(loaded, 48)
            nc.scalar.activation(alog[:], alog[:], ACT.Exp).then_inc(neg_a, 1)
            act.wait_ge(raw, 1)
            softplus_steps(nc, act, "act", dt, e[:], u[:], l[:], steps)
            act.wait_ge(weighed, 1)
            nc.scalar.activation(stats[:, SW], stats[:, SW], ACT.Exp)
            nc.scalar.activation(stats[:, SDEC], tot_ps, ACT.Exp).then_inc(weighed, 1)

        @block.vector
        def _(dve):
            dve.wait_ge(loaded, 48)
            dve.wait_ge(made, 1)
            nc.vector.tensor_tensor(stats[:, SDT], k.ps[:, 0, 0:NC * H2].rearrange("p (c h) -> p c h", h=H2),
                                    bcast(bias[:], 1, [P, NC, H2]), ALU.add).then_inc(raw, 1)
            softplus_steps(nc, dve, "dve", dt, e[:], u[:], l[:], steps)
            dve.wait_ge(neg_a, 1)
            nc.vector.scalar_tensor_tensor(stats[:, SDTA], stats[:, SDT], -1.0, bcast(alog[:], 1, [P, NC, H2]),
                                           ALU.mult, ALU.mult).then_inc(dta_ready, 1)
            dve.wait_ge(sums, 1)
            nc.vector.tensor_copy(stats[:, SACS], sum_ps)
            dve.drain()
            nc.vector.tensor_tensor(stats[:, SW], tot_ps, stats[:, SACS], ALU.subtract).then_inc(weighed, 1)
            dve.wait_ge(weighed, 2)
            nc.vector.tensor_tensor(stats[:, SW], stats[:, SW], stats[:, SDT], ALU.mult)


def ssd_groups_phase(k, parts, stats, y):
    nc, d = k.nc, k.dram
    NW = 2
    assert STILES % NW == 0 and SXT > NW + 1
    FWD, BWD = 0, 1
    incs = [(FWD, 0), (BWD, 3), (FWD, 1), (BWD, 2), (FWD, 2), (BWD, 1), (FWD, CTXC), (BWD, CTXC)]
    order = [(("proj", t), t % 4) for t in range(SCONV)]
    order += [(("turn", c), (SCONV + c) % 4) for c in range(NC)]
    order += [("cb", 3)] + [(("inc", n), 2 + n % 2) for n in range(len(incs))]
    order += [((what, r), slot) for r in range(SR) for what, slot in (("sumf", 0), ("sumb", 1))]
    order += [((what, n + q), 2 + q % 2) for q in range(SXT) for what, n in (("proj", SCONV), ("y", 0))]
    with ExitStack() as ctx:
        sb, sem = k.stage(ctx, "ssd")
        slots = Slots(sem, order)
        w = sb("w", [P, KT, P])
        whi, wlo = sb("w_hi", [P, NW, KT, P], F32R), sb("w_lo", [P, NW, KT, P], F32R)
        convw_all, convw = sb("convw_all", [P, SG, SCONV, 4]), sb("convw", [P, SCONV, 4])
        skip_all, skip = sb("skip_all", [P, SG, SXT]), sb("skip", [P, SXT])
        st = sb("stats", [P, 5, NC, 2, SR])
        xbc = sb("xbc", [P, SCONV, T])
        tok = sb("tok", [P, NC, (SXT + 1) * P])
        cb = sb("cb", [P, T])
        state = sb("state", [P, 2, NC - 1, SXT * P])
        lm = sb("lm", [P, 2, 2, T])
        ea = sb("ea", [P, 2, 2, T])
        m = sb("m", [P, 2, T])
        tap = m
        xw = ea[:, 0].rearrange("p d t -> p (d t)")[:, 0:2 * SXT * P].rearrange("p (b n) -> p b n", b=2)
        decayed = ea[:, 1].rearrange("p d t -> p (d t)")[:, 0:SXT * P]
        ctx_state = lm[:, 1].rearrange("p d t -> p (d t)")[:, 0:2 * SXT * P].rearrange("p (b n) -> p b n", b=2)
        ysum = sb("ysum", [P, T])
        B, C = xbc[:, SXT], xbc[:, SXT + 1]

        small, w_loaded, w_split = sem("small_loaded"), sem("w_loaded"), sem("w_split")
        init_loaded, group_free, stat_ready = sem("init_loaded"), sem("group_free"), sem("stat_ready")
        centre, tapped, convolved, gated = sem("centre_ready"), sem("tapped"), sem("convolved"), sem("z_ready")
        turned, cb_ready = sem("turned"), sem("cb_ready")
        weighted, states_ready, ctx_ready, ctx_stored = (sem(s) for s in (
            "weighted", "states_ready", "ctx_ready", "ctx_stored"))
        diff, lm_ready, m_ready, m_used = sem("diff_ready"), sem("lm_ready"), sem("m_ready"), sem("m_used")
        ps = k.ps
        block = ctx.enter_context(nc.Block())

        @block.sync
        def _(sp):
            sp.dma_start(convw_all[:], d["ssd_conv"]).then_inc(small, 16)
            sp.dma_start(skip_all[:], d["ssd_skip"]).then_inc(small, 16)
            with sp.Fori(0, SG) as i:
                for t in range(STILES):
                    if t == SCONV:
                        sp.wait_ge(group_free, i + 1)
                        for dr, first in ((FWD, 0), (BWD, NC - 2)):
                            sp.dma_start(state[:, dr, first], d["ssd_state"][bass.ds(2 * i + dr, 1)]
                                         .rearrange("o n p -> n (o p)")).then_inc(init_loaded, 16)
                    if t == SCONV + NW + 1:
                        for dr in range(2):
                            sp.wait_ge(ctx_ready, 2 * i + dr + 1)
                            sp.dma_start(d["ssd_out"][bass.ds(2 * i + dr, 1)].rearrange("o n p -> n (o p)"),
                                         ctx_state[:, dr]).then_inc(ctx_stored, 16)
                    sp.wait_ge(w_split, STILES * i + t + 1)
                    sp.dma_start(w[:], d["ssd_w_in"][bass.ds(STILES * i + t, 1)]
                                 .rearrange("o p k n -> p (o k) n")).then_inc(w_loaded, 16)
            sp.wait_ge(ctx_stored, 32 * SG)

        @block.tensor
        def _(pe):
            with pe.Fori(0, SG) as i:
                def project(t):
                    pe.wait_ge(w_split, STILES * i + t + 2)
                    slots.claim(pe, ("proj", t), i)
                    s = slots.slot(("proj", t))
                    for kt in range(KT):
                        last = three_passes(nc, ps[:, s], (whi[:, t % NW, kt], wlo[:, t % NW, kt]),
                                            (parts[0][:, kt], parts[1][:, kt]), kt == 0, kt == KT - 1)
                    last.then_inc(slots.ready[s], 1)

                for t in range(SCONV):
                    project(t)
                pe.wait_ge(convolved, SCONV * (i + 1))
                for c in range(NC):
                    slots.claim(pe, ("turn", c), i)
                    s = slots.slot(("turn", c))
                    for t in range(SXT + 1):
                        last = nc.tensor.transpose(ps[:, s, t * P:(t + 1) * P], xbc[:, t, c * P:(c + 1) * P],
                                                   k.c("ident"))
                    last.then_inc(slots.ready[s], 1)
                slots.claim(pe, "cb", i)
                s = slots.slot("cb")
                for c in range(NC):
                    last = nc.tensor.matmul(ps[:, s, c * P:(c + 1) * P], B[:, c * P:(c + 1) * P],
                                            C[:, c * P:(c + 1) * P], start=True, stop=True)
                last.then_inc(slots.ready[s], 1)
                pe.wait_ge(turned, NC * (i + 1))
                for n, (dr, c) in enumerate(incs):
                    pe.wait_ge(weighted, len(incs) * i + n + 1)
                    slots.claim(pe, ("inc", n), i)
                    s = slots.slot(("inc", n))
                    nc.tensor.matmul(ps[:, s, 0:SXT * P], tok[:, c, SXT * P:], xw[:, n % 2],
                                     start=True, stop=True).then_inc(slots.ready[s], 1)

                def sums(r):
                    for dr, what, tri in ((FWD, "sumf", "tri_f"), (BWD, "sumb", "tri_b")):
                        slots.claim(pe, (what, r), i)
                        s = slots.slot((what, r))
                        for c in range(NC):
                            last = nc.tensor.matmul(ps[:, s, c * P:(c + 1) * P],
                                                    st[:, SDTA, c, dr, r:r + 1].to_broadcast([P, P]), k.c(tri),
                                                    start=True, stop=True)
                        last.then_inc(slots.ready[s], 1)

                pe.wait_ge(stat_ready, i + 1)
                sums(0)
                for r in range(SR):
                    if r + 1 < SR:
                        sums(r + 1)
                    q, half = r // 2, (r % 2) * SP_
                    s = slots.slot(("y", q))
                    if r % 2 == 0:
                        project(SCONV + q)
                        slots.claim(pe, ("y", q), i)
                    if r == 0:
                        pe.wait_ge(states_ready, i + 1)
                        pe.wait_ge(init_loaded, 32 * (i + 1))
                    pe.wait_ge(m_ready, SR * i + r + 1)
                    hp = slice(r * SP_, (r + 1) * SP_)
                    for c in range(NC):
                        cs = slice(c * P, (c + 1) * P)
                        o = ps[half:half + SP_, s, cs]
                        last = nc.tensor.matmul(o, tok[:, c, hp], m[:, r % 2, cs], start=True, stop=(c == CTXC))
                        if c != CTXC:
                            for dr in range(2):
                                last = nc.tensor.matmul(o, state[:, dr, c, hp], ea[:, r % 2, dr, cs],
                                                        start=False, stop=(dr == 1))
                    last.then_inc(m_used, 1)
                    if r % 2:
                        pe.wait_ge(m_used, SR * i + r + 1)
                        pe.sem_inc(slots.ready[s], 1)

        @block.scalar
        def _(act):
            act.wait_ge(small, 32)
            with act.Fori(0, SG) as i:
                act.wait_ge(group_free, i + 1)
                act.wait_ge(stat_ready, i + 1)
                for t in range(SCONV + 1):
                    if t < SCONV:
                        slots.wait(act, ("proj", t), i)
                        if t >= 2:
                            act.wait_ge(convolved, SCONV * i + t - 1)
                        nc.scalar.activation(halves(tap[:, t % 2]), banked(ps[:, slots.slot(("proj", t))]), ACT.Identity,
                                             scale=convw[:, t, 1:2], bias=convw[:, t, 3:4]).then_inc(centre, 1)
                    if t >= 1:
                        act.wait_ge(tapped, SCONV * i + t)
                        nc.scalar.activation(xbc[:, t - 1], tap[:, (t - 1) % 2], ACT.Silu).then_inc(convolved, 1)
                for c in range(NC):
                    slots.wait(act, ("turn", c), i)
                    s = slots.slot(("turn", c))
                    nc.scalar.copy(tok[:, c], ps[:, s, 0:(SXT + 1) * P]).then_inc(slots.free[s], 1)
                    act.drain()
                    act.sem_inc(turned, 1)
                for r in range(SR):
                    act.wait_ge(diff, SR * i + r + 1)
                    for dr, what in ((FWD, "sumf"), (BWD, "sumb")):
                        slots.wait(act, (what, r), i)
                        s = slots.slot((what, r))
                        nc.scalar.activation(ea[:, r % 2, dr], ps[:, s, 0:T], ACT.Exp).then_inc(slots.free[s], 1)
                    nc.scalar.activation(lm[:, r % 2], lm[:, r % 2], ACT.Exp)
                    act.drain()
                    act.sem_inc(lm_ready, 1)
                    if r % 2 == 0:
                        q = r // 2
                        slots.wait(act, ("proj", SCONV + q), i)
                        s = slots.slot(("proj", SCONV + q))
                        nc.scalar.activation(halves(y[:, bass.ds(SXT * i + q, 1)].rearrange("p o t -> p (o t)")),
                                             banked(ps[:, s]), ACT.Silu).then_inc(slots.free[s], 1)
                        act.drain()
                        act.sem_inc(gated, 1)

        @block.vector
        def _(dve):
            slots.credit(dve)
            dve.sem_inc(w_split, 1)

            def split_tile(i, t):
                dve.wait_ge(w_loaded, 16 * (STILES * i + t + 1))
                split_weights(nc, dve, whi[:, t % NW], wlo[:, t % NW], w[:]).then_inc(w_split, 1)

            dve.sem_inc(group_free, 1)
            dve.wait_ge(small, 32)
            with dve.Fori(0, SG) as i:
                dve.wait_ge(group_free, i + 1)
                nc.vector.tensor_copy(st[:].rearrange("p k c d r -> p (k c d) r"),
                                      stats[:].rearrange("p k c (d h) -> p (k c d) h", h=SH)[:, :, bass.ts(i, SR)])
                nc.vector.tensor_copy(skip[:], skip_all[:, bass.ds(i, 1)].rearrange("p o t -> p (o t)"))
                nc.vector.tensor_copy(convw[:], convw_all[:, bass.ds(i, 1)].rearrange("p o t n -> p (o t) n"))
                dve.drain()
                dve.sem_inc(stat_ready, 1)
                for t in range(NW):
                    split_tile(i, t)
                for t in range(SCONV):
                    dve.wait_ge(centre, SCONV * i + t + 1)
                    s = slots.slot(("proj", t))
                    conv_taps(nc, tap[:, t % 2], ps[:, s], convw[:, t, 0:1], convw[:, t, 2:3]
                              ).then_inc(slots.free[s], 1)
                    dve.drain()
                    dve.sem_inc(tapped, 1)
                    if t + NW < STILES:
                        split_tile(i, t + NW)
                slots.wait(dve, "cb", i)
                s = slots.slot("cb")
                nc.vector.tensor_copy(cb[:], ps[:, s, 0:T]).then_inc(slots.free[s], 1)
                dve.wait_ge(turned, NC * (i + 1))
                dve.wait_ge(init_loaded, 32 * (i + 1))

                def weigh(n):
                    dr, c = incs[n]
                    nc.vector.tensor_tensor(xw[:, n % 2].rearrange("p (r q) -> p r q", q=SP_),
                                            tok[:, c, 0:SXT * P].rearrange("p (r q) -> p r q", q=SP_),
                                            bcast(st[:, SW, c, dr], 2, [P, SR, SP_]), ALU.mult
                                            ).then_inc(weighted, 1)

                weigh(0)
                for n, (dr, c) in enumerate(incs):
                    if n + 1 < len(incs):
                        if n >= 1:
                            slots.wait(dve, ("inc", n - 1), i)
                        weigh(n + 1)
                    s = slots.slot(("inc", n))
                    if c == CTXC:
                        slots.wait(dve, ("inc", n), i)
                        nc.vector.tensor_copy(ctx_state[:, dr], ps[:, s, 0:SXT * P]).then_inc(slots.free[s], 1)
                        dve.drain()
                        dve.sem_inc(ctx_ready, 1)
                        continue
                    nc.vector.tensor_tensor(decayed.rearrange("p (r q) -> p r q", q=SP_),
                                            state[:, dr, c].rearrange("p (r q) -> p r q", q=SP_),
                                            bcast(st[:, SDEC, c, dr], 2, [P, SR, SP_]), ALU.mult)
                    dve.drain()
                    slots.wait(dve, ("inc", n), i)
                    nc.vector.tensor_tensor(state[:, dr, c + 1 if dr == FWD else c - 1], ps[:, s, 0:SXT * P],
                                            decayed, ALU.add).then_inc(slots.free[s], 1)
                    dve.drain()
                dve.sem_inc(states_ready, 1)

                def differences(r):
                    for dr, what, neg in ((FWD, "sumf", "neg_f"), (BWD, "sumb", "neg_b")):
                        slots.wait(dve, (what, r), i)
                        s = slots.slot((what, r))
                        for c in range(NC):
                            cs = slice(c * P, (c + 1) * P)
                            last = nc.vector.scalar_tensor_tensor(
                                lm[:, r % 2, dr, cs], ps[:, s, cs], st[:, SACS, c, dr, r:r + 1], k.c(neg),
                                ALU.subtract, ALU.add)
                    last.then_inc(diff, 1)

                def heads_out(q):
                    slots.wait(dve, ("y", q), i)
                    s = slots.slot(("y", q))
                    nc.vector.scalar_tensor_tensor(ysum[:], xbc[:, q], skip[:, q:q + 1], ps[:, s, 0:T],
                                                   ALU.mult, ALU.add).then_inc(slots.free[s], 1)
                    dve.drain()
                    out = y[:, bass.ds(SXT * i + q, 1)].rearrange("p o t -> p (o t)")
                    dve.wait_ge(gated, SXT * i + q + 1)
                    nc.vector.tensor_tensor(out, ysum[:], out, ALU.mult)
                    if q + NW < SXT:
                        split_tile(i, SCONV + q + NW)
                    dve.drain()

                differences(0)
                for r in range(SR):
                    if r + 1 < SR:
                        if r >= 1:
                            dve.wait_ge(m_used, SR * i + r)
                        else:
                            dve.wait_ge(ctx_stored, 32 * i + 32)
                        differences(r + 1)
                    if r >= 2 and r % 2 == 0:
                        heads_out(r // 2 - 1)
                    dve.wait_ge(lm_ready, SR * i + r + 1)
                    nc.vector.tensor_tensor(ea[:, r % 2], ea[:, r % 2], bcast(C, 1, [P, 2, T]), ALU.mult)
                    for c in range(NC):
                        cs = slice(c * P, (c + 1) * P)
                        nc.vector.tensor_scalar(lm[:, r % 2, BWD, cs], lm[:, r % 2, BWD, cs],
                                                st[:, SDT, c, BWD, r:r + 1], None, ALU.mult)
                    dve.drain()
                    for c in range(NC):
                        cs = slice(c * P, (c + 1) * P)
                        nc.vector.scalar_tensor_tensor(m[:, r % 2, cs], lm[:, r % 2, FWD, cs],
                                                       st[:, SDT, c, FWD, r:r + 1], lm[:, r % 2, BWD, cs],
                                                       ALU.mult, ALU.add)
                    dve.drain()
                    nc.vector.tensor_tensor(m[:, r % 2], m[:, r % 2], cb[:], ALU.mult)
                    dve.drain()
                    dve.sem_inc(m_ready, 1)
                heads_out(SXT - 1)
                dve.sem_inc(group_free, 1)


def ssd_mixer(k):
    nc = k.nc
    with ExitStack() as ctx:
        y = ctx.enter_context(nc.sbuf_tensor("ssd_y", [P, SINNER // P, T], F32))
        with ExitStack() as inner:
            stats = inner.enter_context(nc.sbuf_tensor("ssd_stats_all", [P, 5, NC, 2 * SH], F32))
            parts = mixer_input(k, inner, 0)
            with ExitStack() as whole:
                k.hidden(whole, "ssd_in")
                adaln_phase(k, 0, 0, parts)
                ssd_steps_phase(k, stats)
            ssd_groups_phase(k, parts, stats, y)
        gain = ctx.enter_context(nc.sbuf_tensor("ssd_gain", [P, SINNER // P], F32))
        with ExitStack() as inner:
            _, sem = k.stage(inner, "ssd_gain")
            got = sem("loaded")
            block = inner.enter_context(nc.Block())

            @block.sync
            def _(sp):
                sp.dma_start(gain[:], k.dram["ssd_norm"]).then_inc(got, 16)
                sp.wait_ge(got, 16)

        def finish(dve, rstd):
            for t in range(SINNER // P):
                nc.vector.scalar_tensor_tensor(y[:, t], y[:, t], gain[:, t:t + 1], rstd[:], ALU.mult, ALU.mult)

        norm_phase(k, "ssd_norm", y, SINNER // P, finish)
        out_projection_phase(k, "ssd_out", k.dram["ssd_w_out"], y, SINNER // P, 0)



GB, GG, GC, GNBE, GKW, GDEC = range(6)


def gdn_steps_phase(k, stats):
    nc, d = k.nc, k.dram
    H2 = 2 * GH
    with ExitStack() as ctx:
        sb, sem = k.stage(ctx, "gdn_g")
        w, bias, alog = sb("w", [P, KT, 2 * H2]), sb("bias", [P, H2]), sb("alog", [P, H2])
        e, u, l = (sb(n, [P, NC * H2]) for n in ("e", "u", "l"))
        loaded, made, raw, steps, neg_a = (sem(s) for s in ("loaded", "product_ready", "raw", "softplus", "minus_a"))
        g_ready, sums, weighed = sem("g_ready"), sem("sums_ready"), sem("exponents")
        g = stats[:, GG].rearrange("p c h -> p (c h)")
        block = ctx.enter_context(nc.Block())
        raw_ps = k.ps[:, 0, 0:NC * 2 * H2].rearrange("p (c w h) -> p c w h", w=2, h=H2)
        sum_ps = k.ps[:, 1, 0:NC * H2].rearrange("p (c h) -> p c h", h=H2)
        tot_ps = k.ps[:, 2, 0:NC * H2].rearrange("p (c h) -> p c h", h=H2)

        @block.sync
        def _(sp):
            sp.dma_start(w[:], d["gdn_w_ab"]).then_inc(loaded, 16)
            sp.dma_start(bias[:], d["gdn_dt_bias"]).then_inc(loaded, 16)
            sp.dma_start(alog[:], d["gdn_a_log"]).then_inc(loaded, 16)

        @block.tensor
        def _(pe):
            pe.wait_ge(loaded, 48)
            for c in range(NC):
                for t in range(KT):
                    last = nc.tensor.matmul(k.ps[:, 0, c * 2 * H2:(c + 1) * 2 * H2], k.h[:, t, c * P:(c + 1) * P],
                                            w[:, t], start=(t == 0), stop=(t == KT - 1))
            last.then_inc(made, 1)
            pe.wait_ge(g_ready, 1)
            for i, tri in enumerate(("tri_f", "tri_b")):
                for c in range(NC):
                    nc.tensor.matmul(sum_ps[:, c, i * GH:(i + 1) * GH], k.c(tri),
                                     stats[:, GG, c, i * GH:(i + 1) * GH], start=True, stop=True)
            nc.tensor.matmul(k.ps[:, 2, 0:NC * H2], k.c("ones"), g, start=True, stop=True).then_inc(sums, 1)

        @block.scalar
        def _(act):
            act.wait_ge(loaded, 48)
            nc.scalar.activation(alog[:], alog[:], ACT.Exp).then_inc(neg_a, 1)
            act.wait_ge(raw, 1)
            nc.scalar.activation(stats[:, GB], raw_ps[:, :, 0], ACT.Sigmoid)
            softplus_steps(nc, act, "act", g, e[:], u[:], l[:], steps)
            act.wait_ge(weighed, 1)
            nc.scalar.activation(stats[:, GKW], stats[:, GKW], ACT.Exp)
            nc.scalar.activation(stats[:, GNBE], stats[:, GC], ACT.Exp)
            nc.scalar.activation(stats[:, GDEC], tot_ps, ACT.Exp)
            act.drain()
            act.sem_inc(weighed, 1)

        @block.vector
        def _(dve):
            dve.wait_ge(loaded, 48)
            dve.wait_ge(made, 1)
            nc.vector.tensor_tensor(stats[:, GG], raw_ps[:, :, 1], bcast(bias[:], 1, [P, NC, H2]), ALU.add
                                    ).then_inc(raw, 1)
            softplus_steps(nc, dve, "dve", g, e[:], u[:], l[:], steps)
            dve.wait_ge(neg_a, 1)
            nc.vector.scalar_tensor_tensor(stats[:, GG], stats[:, GG], -1.0, bcast(alog[:], 1, [P, NC, H2]),
                                           ALU.mult, ALU.mult).then_inc(g_ready, 1)
            dve.wait_ge(sums, 1)
            nc.vector.tensor_copy(stats[:, GC], sum_ps)
            dve.drain()
            nc.vector.tensor_tensor(stats[:, GKW], tot_ps, stats[:, GC], ALU.subtract).then_inc(weighed, 1)
            dve.wait_ge(weighed, 2)
            nc.vector.scalar_tensor_tensor(stats[:, GNBE], stats[:, GNBE], -1.0, stats[:, GB], ALU.mult, ALU.mult)


def gdn_heads_phase(k, parts, stats, y, gain):
    nc, d = k.nc, k.dram
    NW = 2
    FWD, BWD = 0, 1
    NEGS = (("sneg_f", "neg_f", "tri_f"), ("sneg_b", "neg_b", "tri_b"))
    steps = [(FWD, 0), (BWD, 3), (FWD, CTXC), (BWD, CTXC), (FWD, 1), (BWD, 2), (FWD, 2), (BWD, 1), (FWD, 3), (BWD, 0)]
    last_of = {FWD: NC - 2, BWD: 0}
    order = [(("proj", t), t % 4) for t in range(GCONV)] + [("qsum", 0), ("ksum", 1)]
    order += [(("proj", GCONV + v), 2 + v) for v in range(GVT)]
    order += [(("turn", c), c % 2) for c in range(NC)] + [("kk", 2), ("qk", 3), (("g", 0), 0), (("g", 1), 1)]
    for n in range(LEVELS):
        for dr in range(2):
            if n:
                order += [(("lx", n, dr), 2 * dr)]
            order += [(("xt", n, dr), 2 * dr + 1)]
            if 0 < n < LEVELS - 1:
                order += [(("xi", n, dr), 2 * dr)]
    for dr, c in steps:
        if c != CTXC:
            order += [(("ks", dr, c), 2 * dr)]
        order += [(("vn", dr, c), 2 * dr + 1)]
        if c != last_of[dr]:
            order += [(("kv", dr, c), 2 * dr)]
    order += [(("o", v), v) for v in range(GVT)] + [("osum", 2)]
    with ExitStack() as ctx:
        sb, sem = k.stage(ctx, "gdn")
        slots = Slots(sem, order)
        w = sb("w", [P, KT, P])
        whi, wlo = sb("w_hi", [P, NW, KT, P], F32R), sb("w_lo", [P, NW, KT, P], F32R)
        masks = sb("level_masks", [P, 2, LEVELS, P])
        convw_all, convw = sb("convw_all", [P, GH, GCONV, 3]), sb("convw", [P, GCONV, 3])
        st = sb("stats", [P, 6, NC, 2])
        epsc = sb("eps", [P, 1])
        qkv = sb("qkv", [P, GCONV, T])
        tok = sb("tok", [P, NC, (1 + GVT) * P])
        products = sb("products", [P, 4, T])
        kk, qk = products[:, 0], products[:, 1]
        ba = products[:, 2:4]
        aqk = sb("aqk", [P, 2, T])
        qg = sb("qg", [P, 2, T])
        level = sb("level", [P, 2, T])
        xi, xt, lx = sb("xi", [P, 2, T]), sb("xt", [P, 2, T]), sb("lx", [P, 2, T])
        kg = sb("kg", [P, 2, P])
        rhs = sb("rhs", [P, 2, GDV])
        state = sb("state", [P, 2, NC - 1, GDV])
        ctx_state = sb("ctx_state", [P, 2, GDV])
        assert 2 * NC * GDV <= 4 * T and GVT == 2
        vn = products[:].rearrange("p m t -> p (m t)")[:, 0:2 * NC * GDV].rearrange("p (d c n) -> p d c n", d=2, c=NC)
        tap, sq, root = lx, level, xi

        def out_tile(i, v):
            return y[:, bass.ds(GVT * i + v, 1)].rearrange("p o t -> p (o t)")


        small, w_loaded, w_split = sem("small_loaded"), sem("w_loaded"), sem("w_split")
        init_loaded, head_free, stat_ready = sem("init_loaded"), sem("head_free"), sem("stat_ready")
        centre, tapped, convolved, gated = sem("centre_ready"), sem("tapped"), sem("convolved"), sem("z_ready")
        squared, rooted, unit = sem("squared"), sem("rooted"), sem("q_k_unit_length")
        turned, kk_ready, diff, decays = sem("turned"), sem("kk_ready"), sem("diff_ready"), sem("decays_ready")
        level_ready = [sem(f"level_ready{b}") for b in range(2)]
        lx_ready = [sem(f"lx_ready{b}") for b in range(2)]
        x_ready = [sem(f"x_ready{b}") for b in range(2)]
        rhs_ready = [sem(f"rhs_ready{b}") for b in range(2)]
        vn_ready = [sem(f"vn_ready{b}") for b in range(2)]
        state_ready = [sem(f"state_ready{b}") for b in range(2)]
        aqk_ready, ctx_stored = sem("aqk_ready"), sem("ctx_stored")
        osq, oroot, o_in_psum_read = sem("o_squared"), sem("o_rooted"), sem("o_read")
        ps = k.ps
        q, kf, v0 = qkv[:, 0], qkv[:, 1], 2
        NS = len(steps) // 2
        block = ctx.enter_context(nc.Block())

        def cs(c):
            return slice(c * P, (c + 1) * P)

        @block.sync
        def _(sp):
            sp.dma_start(convw_all[:], d["gdn_conv"]).then_inc(small, 16)
            sp.dma_start(masks[:], d["levels"]).then_inc(small, 16)
            sp.sem_inc(ctx_stored, 32)
            with sp.Fori(0, GH) as i:
                for t in range(GTILES):
                    if t == GCONV:
                        sp.wait_ge(head_free, i + 1)
                        for dr, first in ((FWD, 0), (BWD, NC - 2)):
                            sp.dma_start(state[:, dr, first], d["gdn_state"][bass.ds(2 * i + dr, 1)]
                                         .rearrange("o n p -> n (o p)")).then_inc(init_loaded, 16)
                    sp.wait_ge(w_split, GTILES * i + t + 1)
                    sp.dma_start(w[:], d["gdn_w_in"][bass.ds(GTILES * i + t, 1)]
                                 .rearrange("o p k n -> p (o k) n")).then_inc(w_loaded, 16)
                for dr in range(2):
                    sp.wait_ge(state_ready[dr], (NS - 1) * i + 2)
                    sp.dma_start(d["gdn_out"][bass.ds(2 * i + dr, 1)].rearrange("o n p -> n (o p)"),
                                 ctx_state[:, dr]).then_inc(ctx_stored, 16)
            sp.wait_ge(ctx_stored, 32 * (GH + 1))

        @block.tensor
        def _(pe):
            with pe.Fori(0, GH) as i:
                def use(key):
                    slots.claim(pe, key, i)
                    return slots.slot(key)

                def done(key, last):
                    last.then_inc(slots.ready[slots.slot(key)], 1)

                def project(t):
                    pe.wait_ge(w_split, GTILES * i + t + 2)
                    s = use(("proj", t))
                    for kt in range(KT):
                        last = three_passes(nc, ps[:, s], (whi[:, t % NW, kt], wlo[:, t % NW, kt]),
                                            (parts[0][:, kt], parts[1][:, kt]), kt == 0, kt == KT - 1)
                    done(("proj", t), last)

                for t in range(GCONV):
                    project(t)
                for n, key in enumerate(("qsum", "ksum")):
                    pe.wait_ge(squared, 2 * i + n + 1)
                    s = use(key)
                    done(key, both(nc, ps[:, s], k.c("ones"), sq[:, n], True, True))
                for v in range(GVT):
                    project(GCONV + v)
                pe.wait_ge(unit, i + 1)
                for c in range(NC):
                    s = use(("turn", c))
                    for t in range(1 + GVT):
                        last = nc.tensor.transpose(ps[:, s, t * P:(t + 1) * P], qkv[:, 1 + t, cs(c)], k.c("ident"))
                    done(("turn", c), last)
                for key, moving in (("kk", kf), ("qk", q)):
                    s = use(key)
                    for c in range(NC):
                        last = nc.tensor.matmul(ps[:, s, cs(c)], kf[:, cs(c)], moving[:, cs(c)],
                                                start=True, stop=True)
                    done(key, last)
                pe.wait_ge(stat_ready, i + 1)
                for dr in range(2):
                    s = use(("g", dr))
                    for c in range(NC):
                        last = nc.tensor.matmul(ps[:, s, cs(c)], st[:, GG, c, dr:dr + 1].to_broadcast([P, P]),
                                                k.c(NEGS[dr][2]), start=True, stop=True)
                    done(("g", dr), last)
                NX = LEVELS - 1
                for n in range(LEVELS):
                    for dr in range(2):
                        pe.wait_ge(level_ready[dr], LEVELS * i + n + 1)
                        if n:
                            pe.wait_ge(x_ready[dr], LEVELS * i + n)
                            s = use(("lx", n, dr))
                            for c in range(NC):
                                last = nc.tensor.matmul(ps[:, s, cs(c)], level[:, dr, cs(c)], xt[:, dr, cs(c)],
                                                        start=True, stop=True)
                            done(("lx", n, dr), last)
                    for dr in range(2):
                        s = use(("xt", n, dr))
                        if n:
                            pe.wait_ge(lx_ready[dr], NX * i + n)
                        for c in range(NC):
                            last = nc.tensor.matmul(ps[:, s, cs(c)], xi[:, dr, cs(c)] if n else level[:, dr, cs(c)],
                                                    lx[:, dr, cs(c)] if n else k.c("ident"), start=True, stop=True)
                        done(("xt", n, dr), last)
                        if 0 < n < LEVELS - 1:
                            s = use(("xi", n, dr))
                            for c in range(NC):
                                last = nc.tensor.matmul(ps[:, s, cs(c)], lx[:, dr, cs(c)], xi[:, dr, cs(c)],
                                                        start=True, stop=True)
                            done(("xi", n, dr), last)
                pe.wait_ge(init_loaded, 32 * (i + 1))
                for m in range(NS):
                    pair = steps[2 * m:2 * m + 2]
                    for dr, c in pair:
                        if c != CTXC:
                            if m:
                                pe.wait_ge(state_ready[dr], (NS - 1) * i + m)
                            s = use(("ks", dr, c))
                            done(("ks", dr, c), nc.tensor.matmul(ps[:, s, 0:GDV], kf[:, cs(c)], state[:, dr, c],
                                                                 start=True, stop=True))
                    for dr, c in pair:
                        if m == 0:
                            pe.wait_ge(x_ready[dr], LEVELS * (i + 1))
                        pe.wait_ge(rhs_ready[dr], NS * i + m + 1)
                        s = use(("vn", dr, c))
                        done(("vn", dr, c), nc.tensor.matmul(ps[:, s, 0:GDV], xt[:, dr, cs(c)], rhs[:, dr],
                                                             start=True, stop=True))
                    for dr, c in pair:
                        if c != last_of[dr]:
                            pe.wait_ge(vn_ready[dr], NS * i + m + 1)
                            s = use(("kv", dr, c))
                            done(("kv", dr, c), nc.tensor.matmul(ps[:, s, 0:GDV], kg[:, dr], vn[:, dr, c],
                                                                 start=True, stop=True))
                pe.wait_ge(aqk_ready, i + 1)
                for dr in range(2):
                    pe.wait_ge(vn_ready[dr], NS * (i + 1))
                for v in range(GVT):
                    s = use(("o", v))
                    for c in range(NC):
                        pairs = []
                        for dr in range(2):
                            if c != CTXC:
                                pairs.append((state[:, dr, c, v * P:(v + 1) * P], qg[:, dr, cs(c)]))
                            pairs.append((vn[:, dr, c, v * P:(v + 1) * P], aqk[:, dr, cs(c)]))
                        for n, (a, b) in enumerate(pairs):
                            last = nc.tensor.matmul(ps[:, s, cs(c)], a, b, start=(n == 0), stop=(n == len(pairs) - 1))
                    done(("o", v), last)
                s = use("osum")
                for v in range(GVT):
                    pe.wait_ge(osq, GVT * i + v + 1)
                    last = both(nc, ps[:, s], k.c("ones"), sq[:, v], v == 0, v == GVT - 1)
                done("osum", last)

        @block.scalar
        def _(act):
            act.wait_ge(small, 32)
            with act.Fori(0, GH) as i:
                act.wait_ge(head_free, i + 1)
                act.wait_ge(stat_ready, i + 1)
                for t in range(GCONV + 1):
                    if t < GCONV:
                        slots.wait(act, ("proj", t), i)
                        if t >= 2:
                            act.wait_ge(convolved, GCONV * i + t - 1)
                        nc.scalar.activation(halves(tap[:, t % 2]), banked(ps[:, slots.slot(("proj", t))]), ACT.Copy,
                                             scale=convw[:, t, 1:2]).then_inc(centre, 1)
                    if t >= 1:
                        act.wait_ge(tapped, GCONV * i + t)
                        nc.scalar.activation(qkv[:, t - 1], tap[:, (t - 1) % 2], ACT.Silu).then_inc(convolved, 1)
                    if t == 2:
                        act.drain()
                        for n in range(2):
                            nc.scalar.activation(sq[:, n], qkv[:, n], ACT.Square).then_inc(squared, 1)
                for n, key in enumerate(("qsum", "ksum")):
                    slots.wait(act, key, i)
                    s = slots.slot(key)
                    nc.scalar.activation(root[:, n], ps[:, s, 0:T], ACT.Sqrt, bias=epsc[:]
                                         ).then_inc(slots.free[s], 1)
                act.drain()
                act.sem_inc(rooted, 1)
                for t in range(GVT):
                    slots.wait(act, ("proj", GCONV + t), i)
                    s = slots.slot(("proj", GCONV + t))
                    nc.scalar.activation(halves(out_tile(i, t)), banked(ps[:, s]), ACT.Silu).then_inc(slots.free[s], 1)
                act.drain()
                act.sem_inc(gated, 1)
                for c in range(NC):
                    slots.wait(act, ("turn", c), i)
                    s = slots.slot(("turn", c))
                    nc.scalar.copy(tok[:, c], ps[:, s, 0:(1 + GVT) * P]).then_inc(slots.free[s], 1)
                act.drain()
                act.sem_inc(turned, 1)
                for dr in range(2):
                    act.wait_ge(diff, 2 * i + dr + 1)
                    s = slots.slot(("g", dr))
                    nc.scalar.activation(qg[:, dr], ps[:, s, 0:T], ACT.Exp).then_inc(slots.free[s], 1)
                    nc.scalar.activation(ba[:, dr], ba[:, dr], ACT.Exp, scale=-1.0)
                    nc.scalar.activation(aqk[:, dr], aqk[:, dr], ACT.Exp)
                    act.drain()
                    act.sem_inc(decays, 1)
                for n in range(1, LEVELS):
                    for dr in range(2):
                        slots.wait(act, ("lx", n, dr), i)
                        s = slots.slot(("lx", n, dr))
                        nc.scalar.copy(lx[:, dr], ps[:, s, 0:T]).then_inc(slots.free[s], 1)
                        act.drain()
                        act.sem_inc(lx_ready[dr], 1)
                for v in range(GVT):
                    slots.wait(act, ("o", v), i)
                    nc.scalar.activation(sq[:, v], ps[:, slots.slot(("o", v)), 0:T], ACT.Square).then_inc(osq, 1)
                slots.wait(act, "osum", i)
                s = slots.slot("osum")
                nc.scalar.activation(root[:, 0], ps[:, s, 0:T], ACT.Sqrt, scale=1.0 / GDV, bias=epsc[:]
                                     ).then_inc(slots.free[s], 1)
                act.drain()
                act.sem_inc(oroot, 1)

        @block.vector
        def _(dve):
            slots.credit(dve)
            dve.sem_inc(w_split, 1)

            def split_tile(i, t):
                dve.wait_ge(w_loaded, 16 * (GTILES * i + t + 1))
                split_weights(nc, dve, whi[:, t % NW], wlo[:, t % NW], w[:]).then_inc(w_split, 1)

            nc.vector.memset(epsc[:], EPS)
            dve.drain()
            dve.sem_inc(head_free, 1)
            dve.wait_ge(small, 32)
            with dve.Fori(0, GH) as i:
                def result(key):
                    slots.wait(dve, key, i)
                    return ps[:, slots.slot(key)], slots.free[slots.slot(key)]

                dve.wait_ge(head_free, i + 1)
                nc.vector.tensor_copy(st[:].rearrange("p k c (d o) -> p (k c d) o", o=1),
                                      stats[:].rearrange("p k c (d h) -> p (k c d) h", h=GH)[:, :, bass.ds(i, 1)])
                nc.vector.tensor_copy(convw[:], convw_all[:, bass.ds(i, 1)].rearrange("p o t n -> p (o t) n"))
                dve.drain()
                dve.sem_inc(stat_ready, 1)
                for t in range(NW):
                    split_tile(i, t)
                for t in range(GCONV):
                    dve.wait_ge(centre, GCONV * i + t + 1)
                    s = slots.slot(("proj", t))
                    conv_taps(nc, tap[:, t % 2], ps[:, s], convw[:, t, 0:1], convw[:, t, 2:3]
                              ).then_inc(slots.free[s], 1)
                    dve.drain()
                    dve.sem_inc(tapped, 1)
                    if t + NW < GTILES:
                        split_tile(i, t + NW)
                for t in range(GCONV, GTILES - NW):
                    slots.wait(dve, ("proj", t), i)
                    split_tile(i, t + NW)
                dve.wait_ge(rooted, i + 1)
                nc.vector.reciprocal(root[:, 0:2], root[:, 0:2])
                dve.drain()
                nc.vector.scalar_tensor_tensor(q, q, float(GDK) ** -0.5, root[:, 0], ALU.mult, ALU.mult)
                nc.vector.tensor_tensor(kf, kf, root[:, 1], ALU.mult)
                dve.drain()
                dve.sem_inc(unit, 1)
                src, free = result("kk")
                nc.vector.tensor_copy(kk, src[:, 0:T]).then_inc(free, 1)
                src, free = result("qk")
                nc.vector.tensor_copy(qk, src[:, 0:T]).then_inc(free, 1)
                for dr in range(2):
                    src, _ = result(("g", dr))
                    for c in range(NC):
                        gc = st[:, GC, c, dr:dr + 1]
                        nc.vector.scalar_tensor_tensor(ba[:, dr, cs(c)], src[:, cs(c)], gc, k.c(NEGS[dr][0]),
                                                       ALU.subtract, ALU.subtract)
                        nc.vector.scalar_tensor_tensor(aqk[:, dr, cs(c)], src[:, cs(c)], gc, k.c(NEGS[dr][1]),
                                                       ALU.subtract, ALU.add)
                    dve.drain()
                    dve.sem_inc(diff, 1)

                def next_level(n, dr):
                    nc.vector.tensor_tensor(level[:, dr].rearrange("p (c j) -> p c j", j=P),
                                            ba[:, dr].rearrange("p (c j) -> p c j", j=P),
                                            bcast(masks[:, dr, n], 1, [P, NC, P]), ALU.mult)
                    dve.drain()
                    dve.sem_inc(level_ready[dr], 1)

                for dr in range(2):
                    dve.wait_ge(decays, 2 * i + dr + 1)
                    for c in range(NC):
                        nc.vector.scalar_tensor_tensor(ba[:, dr, cs(c)], kk[:, cs(c)], st[:, GB, c, dr:dr + 1],
                                                       ba[:, dr, cs(c)], ALU.mult, ALU.mult)
                    dve.drain()
                    next_level(0, dr)
                nc.vector.tensor_tensor(aqk[:], aqk[:], bcast(qk, 1, [P, 2, T]), ALU.mult)
                nc.vector.tensor_tensor(qg[:], qg[:], bcast(q, 1, [P, 2, T]), ALU.mult)
                dve.drain()
                dve.sem_inc(aqk_ready, 1)
                eye = bcast(k.c("ident"), 1, [P, NC, P])
                for n in range(LEVELS):
                    for dr in range(2):
                        src, free = result(("xt", n, dr))
                        if n == 0:
                            nc.vector.tensor_tensor(xt[:, dr].rearrange("p (c j) -> p c j", j=P), eye,
                                                    src[:, 0:T].rearrange("p (c j) -> p c j", j=P), ALU.subtract
                                                    ).then_inc(free, 1)
                            nc.vector.tensor_tensor(xi[:, dr].rearrange("p (c j) -> p c j", j=P), eye,
                                                    level[:, dr].rearrange("p (c j) -> p c j", j=P), ALU.subtract)
                        else:
                            nc.vector.tensor_tensor(xt[:, dr], xt[:, dr], src[:, 0:T], ALU.subtract
                                                    ).then_inc(free, 1)
                            if n < LEVELS - 1:
                                src, free = result(("xi", n, dr))
                                nc.vector.tensor_tensor(xi[:, dr], xi[:, dr], src[:, 0:T], ALU.subtract
                                                        ).then_inc(free, 1)
                        dve.drain()
                        dve.sem_inc(x_ready[dr], 1)
                        if n + 1 < LEVELS:
                            next_level(n + 1, dr)
                dve.wait_ge(turned, i + 1)
                dve.wait_ge(init_loaded, 32 * (i + 1))
                dve.wait_ge(ctx_stored, 32 * i + 32)
                for m in range(NS):
                    pair = steps[2 * m:2 * m + 2]
                    for dr, c in pair:
                        nc.vector.tensor_scalar(kg[:, dr], tok[:, c, 0:P], st[:, GKW, c, dr:dr + 1], None, ALU.mult)
                        nc.vector.tensor_scalar(rhs[:, dr], tok[:, c, P:], st[:, GB, c, dr:dr + 1], None, ALU.mult)
                    dve.drain()
                    for dr, c in pair:
                        if c != CTXC:
                            src, free = result(("ks", dr, c))
                            nc.vector.scalar_tensor_tensor(rhs[:, dr], src[:, 0:GDV], st[:, GNBE, c, dr:dr + 1],
                                                           rhs[:, dr], ALU.mult, ALU.add).then_inc(free, 1)
                            dve.drain()
                        dve.sem_inc(rhs_ready[dr], 1)
                    for dr, c in pair:
                        src, free = result(("vn", dr, c))
                        nc.vector.tensor_copy(vn[:, dr, c], src[:, 0:GDV]).then_inc(free, 1)
                        dve.drain()
                        dve.sem_inc(vn_ready[dr], 1)
                    for dr, c in pair:
                        if c == last_of[dr]:
                            continue
                        src, free = result(("kv", dr, c))
                        if c == CTXC:
                            nc.vector.tensor_copy(ctx_state[:, dr], src[:, 0:GDV]).then_inc(free, 1)
                        else:
                            nc.vector.scalar_tensor_tensor(state[:, dr, c + 1 if dr == FWD else c - 1],
                                                           state[:, dr, c], st[:, GDEC, c, dr:dr + 1],
                                                           src[:, 0:GDV], ALU.mult, ALU.add).then_inc(free, 1)
                        dve.drain()
                        dve.sem_inc(state_ready[dr], 1)
                dve.wait_ge(oroot, i + 1)
                dve.wait_ge(gated, i + 1)
                nc.vector.reciprocal(root[:, 0], root[:, 0])
                dve.drain()
                for v in range(GVT):
                    src, free = result(("o", v))
                    nc.vector.scalar_tensor_tensor(root[:, 1], root[:, 0], gain[:, v:v + 1], src[:, 0:T],
                                                   ALU.mult, ALU.mult).then_inc(free, 1)
                    dve.drain()
                    nc.vector.tensor_tensor(out_tile(i, v), root[:, 1], out_tile(i, v), ALU.mult)
                    dve.drain()
                dve.sem_inc(head_free, 1)


def gdn_mixer(k):
    nc = k.nc
    with ExitStack() as ctx:
        y = ctx.enter_context(nc.sbuf_tensor("gdn_y", [P, GH * GVT, T], F32))
        stats = ctx.enter_context(nc.sbuf_tensor("gdn_stats_all", [P, 6, NC, 2 * GH], F32))
        gain = ctx.enter_context(nc.sbuf_tensor("gdn_gain", [P, GVT], F32))
        with ExitStack() as inner:
            _, sem = k.stage(inner, "gdn_gain")
            got = sem("loaded")
            block = inner.enter_context(nc.Block())

            @block.sync
            def _(sp):
                sp.dma_start(gain[:], k.dram["gdn_norm"]).then_inc(got, 16)
                sp.wait_ge(got, 16)

        with ExitStack() as inner:
            parts = mixer_input(k, inner, 1)
            with ExitStack() as whole:
                k.hidden(whole, "gdn_in")
                adaln_phase(k, 1, 0, parts)
                gdn_steps_phase(k, stats)
            gdn_heads_phase(k, parts, stats, y, gain)
        out_projection_phase(k, "gdn_out", k.dram["gdn_w_out"], y, GH * GVT, 1)



HALF = P // 2
NHALF = T // HALF
TG = 8


def top16(nc, dve, values, spare, best, index):
    for c in range(NC):
        nc.vector.max(best[:, c, 0:8], values[:, c])
    dve.drain()
    for c in range(NC):
        nc.vector.match_replace(spare[:, c], best[:, c, 0:8], values[:, c], 4 * NEG)
        nc.vector.max_index(index[:, c, 0:8], best[:, c, 0:8], values[:, c])
    dve.drain()
    for c in range(NC):
        nc.vector.max(best[:, c, 8:16], spare[:, c])
    dve.drain()
    for c in range(NC):
        nc.vector.max_index(index[:, c, 8:16], best[:, c, 8:16], spare[:, c])
    dve.drain()


def peer_retrieval_phase(k, layer, parts, picks):
    nc, d = k.nc, k.dram
    order = [(("proj", s), s) for s in range(2)] + [(("score", s), 2 + s) for s in range(2)]
    K2 = TOPK * TOPK
    with ExitStack() as ctx:
        sb, sem = k.stage(ctx, f"top{layer}")
        slots = Slots(sem, order)
        w, keys = sb("w", [P, 2, KT, P]), sb("keys", [P, 2, NK])
        whi, wlo = sb("w_hi", [P, 2, KT, P], F32R), sb("w_lo", [P, 2, KT, P], F32R)
        hi_ready, w_split = [sem(f"w{s}_hi_ready") for s in range(2)], [sem(f"w{s}_split") for s in range(2)]
        q = sb("q", [P, 2, T])
        score, spare = sb("score", [P, 2, NC, NK]), sb("spare", [P, NC, K2])
        best, index = sb("best", [P, 2, NC, TOPK]), sb("index", [P, 2, NC, TOPK], U32)
        comb = sb("comb", [P, NC, K2])
        cv, ci = sb("cv", [P, NC, TOPK]), sb("ci", [P, NC, TOPK], U32)
        place = sb("place", [P, 2, NC, TOPK], U32)
        placef, indexf = sb("placef", [P, 2, NC, TOPK]), sb("indexf", [P, 2, NC, TOPK])
        hit = sb("hit", [P, NC * TOPK, TOPK])
        out = sb("out", [P, 3, NC, TOPK])
        total = sb("total", [P, NC])
        w_loaded, k_loaded = [sem(f"w{s}_loaded") for s in range(2)], [sem(f"keys{s}_loaded") for s in range(2)]
        w_free, q_ready, score_ready, score_free = sem("w_free"), sem("q_ready"), sem("score_ready"), sem("score_free")
        score_seen, seen, centred, powered = sem("scores_copied"), sem("scores_seen"), sem("centred"), sem("exp_ready")
        ps = k.ps
        block = ctx.enter_context(nc.Block())

        @block.sync
        def _(sp):
            with sp.Fori(0, PH) as i:
                for s in range(2):
                    sp.wait_ge(w_free, 2 * i + s + 1)
                    sp.dma_start(w[:, s], d[f"peer_w_q{layer}"][bass.ds(2 * i + s, 1)]
                                 .rearrange("o p k n -> p (o k) n")).then_inc(w_loaded[s], 16)
                    sp.dma_start(keys[:, s], d[f"peer_keys{layer}"][bass.ds(2 * i + s, 1)]
                                 .rearrange("o p n -> p (o n)")).then_inc(k_loaded[s], 16)

        @block.tensor
        def _(pe):
            pe.sem_inc(w_free, 2)
            with pe.Fori(0, PH) as i:
                for s in range(2):
                    pe.wait_ge(w_split[s], i + 1)
                    slots.claim(pe, ("proj", s), i)
                    for kt in range(KT):
                        last = three_passes(nc, ps[:, s], (whi[:, s, kt], wlo[:, s, kt]),
                                            (parts[0][:, kt], parts[1][:, kt]), kt == 0, kt == KT - 1)
                    last.then_inc(slots.ready[s], 1)
                for s in range(2):
                    pe.wait_ge(k_loaded[s], 16 * (i + 1))
                    pe.wait_ge(q_ready, 2 * i + s + 1)
                    slots.claim(pe, ("score", s), i)
                    for c in range(NC):
                        last = nc.tensor.matmul(ps[:, 2 + s, c * NK:(c + 1) * NK], q[:, s, c * P:(c + 1) * P],
                                                keys[:, s], start=True, stop=True)
                    last.then_inc(slots.ready[2 + s], 1)
                    slots.wait(pe, ("score", s), i)
                    pe.sem_inc(w_free, 1)

        @block.scalar
        def _(act):
            act.sem_inc(slots.free[0], 1)
            act.sem_inc(slots.free[1], 1)
            act.sem_inc(slots.free[2], 1)
            act.sem_inc(slots.free[3], 1)
            act.sem_inc(score_seen, 2)

            def scores(i):
                for s in range(2):
                    act.wait_ge(w_loaded[s], 16 * (i + 1))
                    act.wait_ge(score_seen, 2 * i + s + 1)
                    nc.scalar.copy(whi[:, s], w[:, s])
                    act.drain()
                    act.sem_inc(hi_ready[s], 1)
                for s in range(2):
                    slots.wait(act, ("proj", s), i)
                    nc.scalar.copy(halves(q[:, s]), banked(ps[:, s])).then_inc(slots.free[s], 1)
                    act.drain()
                    act.sem_inc(q_ready, 1)
                for s in range(2):
                    slots.wait(act, ("score", s), i)
                    act.wait_ge(score_free, 2 * i + s + 1)
                    nc.scalar.copy(score[:, s].rearrange("p c n -> p (c n)"), ps[:, 2 + s, 0:T]
                                   ).then_inc(slots.free[2 + s], 1)
                    act.drain()
                    act.sem_inc(score_ready, 1)
                    act.sem_inc(score_seen, 1)

            def power(i):
                act.wait_ge(centred, i + 1)
                nc.scalar.activation(out[:, 2], out[:, 2], ACT.Exp).then_inc(powered, 1)

            scores(0)
            with act.Fori(0, PH - 1) as i:
                scores(i + 1)
                power(i)
            power(PH - 1)

        @block.gpsimd
        def _(pool):
            with pool.Fori(0, PH) as i:
                for s in range(2):
                    pool.wait_ge(hi_ready[s], i + 1)
                    nc.gpsimd.tensor_tensor(wlo[:, s].rearrange("p k n -> p (k n)"),
                                            w[:, s].rearrange("p k n -> p (k n)"),
                                            whi[:, s].rearrange("p k n -> p (k n)").bitcast(F32), ALU.subtract
                                            ).then_inc(w_split[s], 1)

        @block.vector
        def _(dve):
            dve.sem_inc(score_free, 2)
            with dve.Fori(0, PH) as i:
                for s in range(2):
                    dve.wait_ge(score_ready, 2 * i + s + 1)
                    dve.sem_inc(seen, 1)
                    top16(nc, dve, score[:, s], spare[:, :, 0:NK], best[:, s], index[:, s])
                    dve.sem_inc(score_free, 1)
                c4 = comb[:].rearrange("p c (a b) -> p c a b", b=TOPK)
                nc.vector.tensor_tensor(c4, bcast(best[:, 0], 3, [P, NC, TOPK, TOPK]),
                                        bcast(best[:, 1], 2, [P, NC, TOPK, TOPK]), ALU.add)
                nc.vector.tensor_copy(indexf[:], index[:])
                dve.drain()
                top16(nc, dve, comb[:], spare[:], cv[:], ci[:])
                nc.vector.tensor_scalar(place[:, 0], ci[:], 4, None, ALU.logical_shift_right)
                nc.vector.tensor_scalar(place[:, 1], ci[:], TOPK - 1, None, ALU.bitwise_and)
                nc.vector.tensor_tensor(out[:, 2], cv[:], cv[:, :, 0:1].to_broadcast([P, NC, TOPK]), ALU.subtract
                                        ).then_inc(centred, 1)
                dve.drain()
                nc.vector.tensor_copy(placef[:], place[:])
                dve.drain()
                for s in range(2):
                    nc.vector.tensor_tensor(hit[:], bcast(placef[:, s].rearrange("p c r -> p (c r)"), 2,
                                                          [P, NC * TOPK, TOPK]),
                                            bcast(k.c("iota")[:, 0:TOPK], 1, [P, NC * TOPK, TOPK]), ALU.is_equal)
                    dve.drain()
                    h4 = hit[:].rearrange("p (c r) a -> p c r a", c=NC)
                    nc.vector.tensor_tensor(h4, h4, bcast(indexf[:, s], 2, [P, NC, TOPK, TOPK]), ALU.mult)
                    dve.drain()
                    nc.vector.tensor_reduce(out[:, s].rearrange("p c r -> p (c r)"), hit[:], AX.X, ALU.add)
                    dve.drain()
                dve.wait_ge(powered, i + 1)
                nc.vector.tensor_reduce(total[:], out[:, 2], AX.X, ALU.add)
                dve.drain()
                nc.vector.reciprocal(total[:], total[:])
                dve.drain()
                nc.vector.tensor_tensor(out[:, 2], out[:, 2], bcast(total[:], 2, [P, NC, TOPK]), ALU.mult)
                dve.drain()
                for n in range(3):
                    nc.vector.tensor_copy(picks[:, :, n, bass.ts(i, TOPK)], out[:, n])
                dve.drain()


def peer_gates_phase(k, layer, picks, gates):
    nc = k.nc
    SCALE = float(2 ** 15)
    G = 2 * TG
    with ExitStack() as ctx:
        sb, sem = k.stage(ctx, f"gate{layer}")
        turned = sb("turned", [P, 3, T])
        scaled = sb("scaled", [P, T])
        pick = sb("pick", [P, 4, T], F16)
        iota = sb("iota", [P, NK, G], F16)
        hot = sb("hot", [P, NK, G], F16)
        second, high, low = (sb(n, [P, 2, NK, G], F16) for n in ("second", "high", "low"))
        stage = sb("stage", [P, 2, NK, HALF])
        turn_made, turn_taken = sem("turn_ready"), sem("turn_taken")
        hot_ready = [sem(f"one_hot{j}_ready") for j in range(2)]
        used, ps_free = [sem(f"product{j}_ready") for j in range(2)], [sem(f"product{j}_taken") for j in range(2)]
        staged, stored = [sem(f"staged{b}") for b in range(2)], [sem(f"stored{b}") for b in range(2)]
        ps = k.ps
        PER = HALF // (2 * G)
        block = ctx.enter_context(nc.Block())

        @block.sync
        def _(sp):
            for b in range(2):
                sp.sem_inc(stored[b], 16)
            with sp.Fori(0, NC) as c:
                for b in range(2):
                    sp.wait_ge(staged[b], 4 * PER * (c + 1))
                    sp.dma_start(gates[bass.ds(2 * c + b, 1)].rearrange("o p k t -> p (o k) t"), stage[:, b]
                                 ).then_inc(stored[b], 16)
            for b in range(2):
                sp.wait_ge(stored[b], 16 * (NC + 1))

        @block.tensor
        def _(pe):
            for c in range(NC):
                if c >= 2:
                    pe.wait_ge(turn_taken, c - 1)
                for n in range(3):
                    last = nc.tensor.transpose(ps[:, 2 + c % 2, n * P:(n + 1) * P], picks[:, c, n], k.c("ident"))
                last.then_inc(turn_made, 1)
            pe.wait_ge(turn_taken, NC)
            with pe.Fori(0, NC) as c:
                for b in range(2):
                    with pe.Fori(0, PER) as g:
                        n = (2 * c + b) * PER + g
                        for j in range(2):
                            pe.wait_ge(hot_ready[j], n + 1)
                            for q in range(2):
                                pe.wait_ge(ps_free[j], 2 * n + q + 1)
                                for u in range(q * TG, (q + 1) * TG):
                                    o = ps[:, 2 * j + q, (u % TG) * NK:(u % TG + 1) * NK]
                                    nc.tensor.matmul(o, second[:, j, :, u], high[:, j, :, u], start=True, stop=False)
                                    last = nc.tensor.matmul(o, second[:, j, :, u], low[:, j, :, u],
                                                            start=False, stop=True)
                                last.then_inc(used[j], 1)

        @block.scalar
        def _(act):
            for j in range(2):
                act.sem_inc(ps_free[j], 2)
            with act.Fori(0, NC) as c:
                for b in range(2):
                    act.wait_ge(stored[b], 16 * (c + 1))
                    with act.Fori(0, PER) as g:
                        n = (2 * c + b) * PER + g
                        for j in range(2):
                            for q in range(2):
                                act.wait_ge(used[j], 2 * n + q + 3)
                                to = stage[:, b].rearrange("p k t -> p t k")
                                nc.scalar.activation(to[:, bass.ds(2 * G * g + G * j + TG * q, TG)],
                                                     ps[:, 2 * j + q].rearrange("p (t k) -> p t k", k=NK),
                                                     ACT.Copy, scale=1.0 / SCALE).then_inc(ps_free[j], 1)
                                act.drain()
                                act.sem_inc(staged[b], 1)

        @block.vector
        def _(dve):
            nc.vector.tensor_copy(iota[:], bcast(k.c("iota"), 2, [P, NK, G]))
            for c in range(NC):
                dve.wait_ge(turn_made, c + 1)
                nc.vector.tensor_copy(turned[:, :, c * P:(c + 1) * P],
                                      ps[:, 2 + c % 2, 0:3 * P].rearrange("p (n t) -> p n t", n=3)
                                      ).then_inc(turn_taken, 1)
            dve.drain()
            nc.vector.tensor_copy(pick[:, 0:2], turned[:, 0:2])
            nc.vector.tensor_scalar(scaled[:], turned[:, 2], SCALE, None, ALU.mult)
            dve.drain()
            nc.vector.tensor_copy(pick[:, 2], scaled[:])
            dve.drain()
            nc.vector.tensor_tensor(pick[:, 3], scaled[:], pick[:, 2], ALU.subtract)
            dve.drain()
            for j in range(2):
                dve.sem_inc(used[j], 2)
            with dve.Fori(0, NC) as c:
                for b in range(2):
                    with dve.Fori(0, PER) as g:
                        n = (2 * c + b) * PER + g
                        for j in range(2):
                            now = pick[:, :, bass.ds(2 * G * n + G * j, G)]
                            kind = [bcast(now[:, m], 1, [P, NK, G]) for m in range(4)]
                            nc.vector.tensor_tensor(hot[:], iota[:], kind[0], ALU.is_equal)
                            dve.wait_ge(used[j], 2 * n + 2)
                            nc.vector.tensor_tensor(second[:, j], iota[:], kind[1], ALU.is_equal)
                            dve.drain()
                            nc.vector.tensor_tensor(high[:, j], hot[:], kind[2], ALU.mult)
                            nc.vector.tensor_tensor(low[:, j], hot[:], kind[3], ALU.mult)
                            dve.drain()
                            dve.sem_inc(hot_ready[j], 1)


def peer_experts_phase(k, layer, parts, gates):
    nc, d = k.nc, k.dram
    u_dram, v_dram = d[f"peer_u{layer}"], d[f"peer_v{layer}"]
    g_dram = gates.rearrange("n p (b e) t -> b p n e t", e=EB)
    assert EB == 2
    with ExitStack() as ctx:
        sb, sem = k.stage(ctx, f"dense{layer}")
        u, v = sb("u", [P, 2, EB * D]), sb("v", [P, 2, EB * D])
        uhi, ulo, vhi, vlo = (sb(n, [P, 2, EB * D], F32R) for n in ("u_hi", "u_lo", "v_hi", "v_lo"))
        g = sb("g", [P, 2, NHALF, EB, HALF])
        act_out = sb("gelu", [P, EB, T])
        ahi, alo = sb("a_hi", [P, 2, EB, T], F32R), sb("a_lo", [P, 2, EB, T], F32R)
        u_loaded, v_loaded, g_loaded = ([sem(f"{n}{b}_loaded") for b in range(2)] for n in "uvg")
        s_ready, s_free = [sem(f"s{e}_ready") for e in range(2)], [sem(f"s{e}_free") for e in range(2)]
        o_ready, o_free = [sem(f"o{j}_ready") for j in range(2)], [sem(f"o{j}_free") for j in range(2)]
        uhi_ready, vhi_ready, ahi_ready = sem("u_hi_ready"), sem("v_hi_ready"), sem("a_hi_ready")
        u_split, v_split, a_split = sem("u_split"), sem("v_split"), sem("a_split")
        activated, gated = sem("activated"), sem("gated")
        ps = k.ps
        OP = KT // 2
        block = ctx.enter_context(nc.Block())

        @block.sync
        def _(sp):
            with sp.Fori(0, NB // 2) as i:
                for b in range(2):
                    n = 2 * i + b
                    sp.wait_ge(u_split, n + 1)
                    sp.dma_start(u[:, b], u_dram[bass.ds(n, 1)].rearrange("o p e k n -> p (o e k n)")
                                 ).then_inc(u_loaded[b], 16)
                    sp.wait_ge(gated, EB * (n + 1))
                    sp.dma_start(g[:, b].rearrange("p n e t -> p n (e t)"),
                                 g_dram[bass.ds(n, 1)].rearrange("o p n e t -> p (o n) (e t)")
                                 ).then_inc(g_loaded[b], 16)
                    sp.wait_ge(v_split, n + 1)
                    sp.dma_start(v[:, b], v_dram[bass.ds(n, 1)].rearrange("o p e n -> p (o e n)")
                                 ).then_inc(v_loaded[b], 16)

        @block.tensor
        def _(pe):
            for j in range(2):
                pe.sem_inc(s_ready[j], 2)
                pe.sem_inc(o_ready[j], 2 * OP)

            def score(n, b):
                pe.wait_ge(u_split, n + 3)
                for e in range(EB):
                    pe.wait_ge(s_free[e], n + 1)
                    for kt in range(KT):
                        cut = slice((e * KT + kt) * P, (e * KT + kt + 1) * P)
                        last = three_passes(nc, ps[:, e], (uhi[:, b, cut], ulo[:, b, cut]),
                                            (parts[0][:, kt], parts[1][:, kt]), kt == 0, kt == KT - 1)
                    last.then_inc(s_ready[e], 1)

            def output(n, b):
                pe.wait_ge(v_split, n + 3)
                pe.wait_ge(a_split, EB * (n + 2))
                for t in range(KT):
                    pe.wait_ge(o_free[t % 2], OP * n + t // 2 + 1)
                    for e in range(EB):
                        cut = slice(e * D + t * P, e * D + (t + 1) * P)
                        last = three_passes(nc, ps[:, 2 + t % 2], (vhi[:, b, cut], vlo[:, b, cut]),
                                            (ahi[:, b, e], alo[:, b, e]), e == 0, e == EB - 1)
                    last.then_inc(o_ready[t % 2], 1)

            score(0, 0)
            with pe.Fori(0, NB // 2 - 1) as i:
                score(2 * i + 1, 1)
                output(2 * i, 0)
                score(2 * i + 2, 0)
                output(2 * i + 1, 1)
            score(NB - 1, 1)
            output(NB - 2, 0)
            output(NB - 1, 1)

        @block.scalar
        def _(act):
            for e in range(2):
                act.sem_inc(s_free[e], 1)

            def high_u(n, b, i):
                act.wait_ge(u_loaded[b], 16 * (i + 1))
                act.wait_ge(s_ready[1], n + 1)
                nc.scalar.copy(uhi[:, b], u[:, b]).then_inc(uhi_ready, 1)

            def high_v(n, b, i):
                act.wait_ge(v_loaded[b], 16 * (i + 1))
                act.wait_ge(o_ready[1], OP * (n + 1))
                nc.scalar.copy(vhi[:, b], v[:, b]).then_inc(vhi_ready, 1)

            def activate(n, b):
                for e in range(EB):
                    act.wait_ge(s_ready[e], n + 3)
                    act.wait_ge(a_split, EB * n + e + 1)
                    nc.scalar.activation(halves(act_out[:, e]), banked(ps[:, e]), ACT.Gelu).then_inc(s_free[e], 1)
                    act.drain()
                    act.sem_inc(activated, 1)
                    act.wait_ge(gated, EB * (n + 2) + e + 1)
                    nc.scalar.copy(ahi[:, b, e], act_out[:, e]).then_inc(ahi_ready, 1)

            high_u(0, 0, 0)
            high_u(1, 1, 0)
            high_v(0, 0, 0)
            activate(0, 0)
            with act.Fori(0, NB // 2 - 1) as i:
                high_u(2 * i + 2, 0, i + 1)
                high_v(2 * i + 1, 1, i)
                activate(2 * i + 1, 1)
                high_u(2 * i + 3, 1, i + 1)
                high_v(2 * i + 2, 0, i + 1)
                activate(2 * i + 2, 0)
            high_v(NB - 1, 1, NB // 2 - 1)
            activate(NB - 1, 1)

        @block.vector
        def _(dve):
            dve.sem_inc(gated, 2 * EB)
            dve.sem_inc(a_split, EB)
            dve.sem_inc(u_split, 2)
            dve.sem_inc(v_split, 2)
            for j in range(2):
                dve.sem_inc(o_free[j], 1)

            def low_u(n, b):
                dve.wait_ge(uhi_ready, n + 1)
                nc.vector.tensor_tensor(ulo[:, b], u[:, b], uhi[:, b].bitcast(F32), ALU.subtract).then_inc(u_split, 1)

            def low_v(n, b):
                dve.wait_ge(vhi_ready, n + 1)
                nc.vector.tensor_tensor(vlo[:, b], v[:, b], vhi[:, b].bitcast(F32), ALU.subtract).then_inc(v_split, 1)

            def gate(n, b, i, e):
                if e == 0:
                    dve.wait_ge(g_loaded[b], 16 * (i + 1))
                dve.wait_ge(activated, EB * n + e + 1)
                ae = act_out[:, e].rearrange("p (n t) -> p n t", t=HALF)
                nc.vector.tensor_tensor(ae, ae, g[:, b, :, e], ALU.mult).then_inc(gated, 1)

            def low_a(n, b, e):
                dve.wait_ge(ahi_ready, EB * n + e + 1)
                nc.vector.tensor_tensor(alo[:, b, e], act_out[:, e], ahi[:, b, e].bitcast(F32), ALU.subtract
                                        ).then_inc(a_split, 1)

            def add(n, t):
                dve.wait_ge(o_ready[t % 2], OP * (n + 2) + t // 2 + 1)
                for s, lo, hi, at in PIECES:
                    x = k.x[:, t, lo:hi]
                    last = nc.vector.scalar_tensor_tensor(x, ps[:, 2 + t % 2, at:at + hi - lo],
                                                          k.mod[:, layer, 5, t, s:s + 1], x, ALU.mult, ALU.add)
                last.then_inc(o_free[t % 2], 1)

            def stage(n, b, i, ni, more):
                if more:
                    low_u(n + 2, b)
                low_v(n + 1, 1 - b)
                gate(n + 1, 1 - b, ni, 0)
                low_a(n + 1, 1 - b, 0)
                for t in range(KT):
                    if t == 2:
                        gate(n + 1, 1 - b, ni, 1)
                    if t == 4:
                        low_a(n + 1, 1 - b, 1)
                    add(n, t)

            low_u(0, 0)
            low_u(1, 1)
            low_v(0, 0)
            for e in range(EB):
                gate(0, 0, 0, e)
                low_a(0, 0, e)
            with dve.Fori(0, NB // 2 - 1) as i:
                stage(2 * i, 0, i, i, True)
                stage(2 * i + 1, 1, i, i + 1, True)
            stage(NB - 2, 0, 0, NB // 2 - 1, False)
            for t in range(KT):
                add(NB - 1, t)


def peer_mixer(k, layer):
    nc = k.nc
    gates = nc.dram_tensor(f"gate_matrix{layer}", (NHALF, P, NK, HALF), F32, kind="Internal").ap()
    with ExitStack() as ctx:
        parts = [ctx.enter_context(nc.sbuf_tensor(f"peer_in{layer}_{n}", [P, KT, T], F32R)) for n in ("hi", "lo")]
        with ExitStack() as inner:
            k.hidden(inner, f"peer_in{layer}")
            adaln_phase(k, layer, 1, parts)
        with ExitStack() as inner:
            picks = inner.enter_context(nc.sbuf_tensor(f"picks{layer}", [P, NC, 3, P], F32))
            peer_retrieval_phase(k, layer, parts, picks)
            peer_gates_phase(k, layer, picks, gates)
        peer_experts_phase(k, layer, parts, gates)



def build(nc, dram):
    with ExitStack() as ctx:
        k = Core(nc, ctx, dram)
        load_phase(k)
        modulation_phase(k)
        for layer, mixer in enumerate((ssd_mixer, gdn_mixer)):
            mixer(k)
            peer_mixer(k, layer)
        k.hidden(ctx, "normed_out")
        final_phase(k)


def grid_positions():
    width, quarter = 64, D // 4
    omega = (1.0 / (np.float32(10000.0) ** (np.arange(quarter, dtype=np.float32) / quarter))).astype(np.float32)

    def enc(p):
        ang = p.astype(np.float32)[:, None] * omega[None, :]
        return np.concatenate([np.sin(ang), np.cos(ang)], -1)

    t = np.arange(LAT)
    return np.concatenate([enc(t // width), enc(t % width)], -1).astype(np.float32)


def features_first(a):
    n, f = a.shape
    return np.ascontiguousarray(a.reshape(n, f // P, P).transpose(2, 1, 0))


def weight_tiles(w, columns=None):
    if columns is not None:
        w = w[:, columns]
    kk, n = w.shape
    return np.ascontiguousarray(w.reshape(kk // P, P, n // P, P).transpose(2, 1, 0, 3))


def lay_out(a):
    a = {n: np.asarray(v) for n, v in a.items()}
    out = {"consts": constants(), "levels": level_masks(), "pos": features_first(grid_positions())}
    out["x"] = features_first(np.concatenate([a["x_sample"][0], a["x_prompt"][0]], 0))
    out["cond"] = features_first(np.stack([a["c"][0], a["c_ctx"]], 0))
    out["b_mod"] = np.repeat(a["b_mod"].reshape(DEPTH * 6 * KT, P).T[:, :, None], 2, 2)
    w = a["w_mod"].reshape(DEPTH, KT, P, 6 * KT // 4, 4 * P)
    out["w_mod"] = w.transpose(0, 3, 2, 1, 4).reshape(DEPTH * 6 * KT // 4, P, KT, 4 * P)
    gains = np.concatenate([a["norm_mix_g"], a["norm_ffn_g"], a["final_norm_g"][None]], 0)
    out["gains"] = np.repeat(gains.reshape(2 * DEPTH + 1, KT, P).transpose(2, 0, 1)[..., None], 2, 3)

    z0, x0, b0 = 0, SINNER, 2 * SINNER
    c0, dt0 = b0 + SG * SN, b0 + 2 * SG * SN
    xw = SXT * P
    cols, conv_cols = [], []
    for g in range(SG):
        conv = np.concatenate([np.arange(x0 + g * xw, x0 + (g + 1) * xw), np.arange(b0 + g * SN, b0 + (g + 1) * SN),
                               np.arange(c0 + g * SN, c0 + (g + 1) * SN)])
        conv_cols.append(conv - x0)
        cols += [conv, np.arange(z0 + g * xw, z0 + (g + 1) * xw)]
    w_in = a["ssd_w_in"][0]
    out["ssd_w_in"] = weight_tiles(w_in, np.concatenate(cols))
    out["ssd_w_dt"] = w_in[:, dt0:].reshape(KT, P, 2 * SH).transpose(1, 0, 2)
    conv = np.concatenate([a["ssd_conv_w"][0], a["ssd_conv_b"]], 0)[:, np.concatenate(conv_cols)]
    out["ssd_conv"] = conv.reshape(4, SG, SCONV, P).transpose(3, 1, 2, 0)
    out["ssd_skip"] = np.repeat(a["ssd_d"][0], SP_).reshape(SG, SXT, P).transpose(2, 0, 1)
    out["ssd_dt_bias"] = np.broadcast_to(a["ssd_dt_bias"].reshape(1, 2 * SH), (P, 2 * SH))
    out["ssd_a_log"] = np.broadcast_to(a["ssd_a_log"].reshape(1, 2 * SH), (P, 2 * SH))
    st = np.stack([a["state_ssd_fwd"][0, 0], a["state_ssd_bwd"][0, 0]], 0).reshape(2, SG, xw, SN)
    out["ssd_state"] = st.transpose(1, 0, 3, 2).reshape(SG * 2, SN, xw)
    out["ssd_norm"] = a["ssd_norm_g"].reshape(SINNER // P, P).T
    out["ssd_w_out"] = weight_tiles(a["ssd_w_out"][0])

    cols, conv_cols = [], []
    q0, k0, v0, z0 = 0, GH * GDK, 2 * GH * GDK, 2 * GH * GDK + GH * GDV
    ab0 = z0 + GH * GDV
    for h in range(GH):
        conv = np.concatenate([np.arange(q0 + h * GDK, q0 + (h + 1) * GDK), np.arange(k0 + h * GDK, k0 + (h + 1) * GDK),
                               np.arange(v0 + h * GDV, v0 + (h + 1) * GDV)])
        conv_cols.append(conv)
        cols += [conv, np.arange(z0 + h * GDV, z0 + (h + 1) * GDV)]
    w_in = a["gdn_w_in"][0]
    out["gdn_w_in"] = weight_tiles(w_in, np.concatenate(cols))
    out["gdn_w_ab"] = w_in[:, ab0:].reshape(KT, P, 4 * GH).transpose(1, 0, 2)
    conv = a["gdn_conv_w"][0][:, np.concatenate(conv_cols)]
    out["gdn_conv"] = conv.reshape(3, GH, GCONV, P).transpose(3, 1, 2, 0)
    out["gdn_dt_bias"] = np.broadcast_to(a["gdn_dt_bias"].reshape(1, 2 * GH), (P, 2 * GH))
    out["gdn_a_log"] = np.broadcast_to(a["gdn_a_log"].reshape(1, 2 * GH), (P, 2 * GH))
    st = np.stack([a["state_gdn_fwd"][0, 0], a["state_gdn_bwd"][0, 0]], 1)
    out["gdn_state"] = st.reshape(GH * 2, GDK, GDV)
    out["gdn_norm"] = a["gdn_norm_g"].reshape(GVT, P).T
    out["gdn_w_out"] = weight_tiles(a["gdn_w_out"][0])

    for l in range(DEPTH):
        out[f"peer_w_q{l}"] = weight_tiles(a["peer_w_q"][l])
        out[f"peer_keys{l}"] = a["peer_keys"][l].transpose(1, 0, 3, 2).reshape(2 * PH, PHALF, NK)
        out[f"peer_u{l}"] = a["peer_u"][l].reshape(NB, EB, P, KT, P).transpose(0, 4, 1, 3, 2)
        out[f"peer_v{l}"] = a["peer_v"][l].reshape(NB, EB, P, D).transpose(0, 2, 1, 3)
    return {n: np.ascontiguousarray(v) for n, v in out.items()}


def kernel(**inputs):
    import concourse.bacc as bacc
    from concourse.bass_utils import run_bass_kernel_spmd

    nc = bacc.Bacc("TRN2", target_bir_lowering=False, num_devices=1)
    arrays = lay_out(inputs)
    dram = {n: nc.dram_tensor(f"in_{n}", v.shape, mybir.dt.from_np(v.dtype), kind="ExternalInput").ap()
            for n, v in arrays.items()}
    outputs = {"y": (P, KT, T), "ssd_out": (2 * SG, SN, SXT * P), "gdn_out": (2 * GH, GDK, GDV)}
    for n, shape in outputs.items():
        dram[n] = nc.dram_tensor(f"out_{n}", shape, F32, kind="ExternalOutput").ap()
    build(nc, dram)
    got = run_bass_kernel_spmd(nc, [{f"in_{n}": v for n, v in arrays.items()}], core_ids=[0]).results[0]
    y = got["out_y"].transpose(2, 1, 0).reshape(T, D)
    ssd = got["out_ssd_out"].reshape(SG, 2, SN, SR, SP_).transpose(1, 0, 3, 4, 2).reshape(2, 1, 1, SH, SP_, SN)
    gdn = got["out_gdn_out"].reshape(GH, 2, GDK, GDV).transpose(1, 0, 2, 3).reshape(2, 1, 1, GH, GDK, GDV)
    return (np.ascontiguousarray(y[None, LAT:]), np.ascontiguousarray(y[None, :LAT]),
            np.ascontiguousarray(ssd[0]), np.ascontiguousarray(ssd[1]),
            np.ascontiguousarray(gdn[0]), np.ascontiguousarray(gdn[1]))
```
